# Optimizing a Trainium2 kernel written in Bass

```python
import math
import jax, jax.numpy as jnp
from jax import lax
import numpy as np

D_MODEL = 1024
BATCH = 1
SEQ = 256
DEPTH = 1
DEC_BATCH = 8
DEC_SEQ = 4
PAST_LEN = 1024
PAGE_SIZE = 128

F32 = jnp.float32
HEAD_DIM = 64
N_HEADS_A = D_MODEL // 128
N_HEADS_B = D_MODEL // 256
WIDTH_A = N_HEADS_A * HEAD_DIM
WIDTH_B = N_HEADS_B * 2 * HEAD_DIM
N_IN = 3 * WIDTH_A + 3 * WIDTH_B
MOBA_BLOCK = 256
MOBA_TOPK = 3
MOBA_QBLOCK = 16
DIFF_QBLOCK = 128
NUM_BUCKETS = 32
MAX_DISTANCE = 128
D_FF = ((8 * D_MODEL // 3 + 127) // 128) * 128
CONV_W = 3
EPS = 1e-6

kernel_name = "moba_diffattn_gated_hybrid_step"

def rmsnorm(x, g):
    xf = x.astype(F32)
    y = xf * lax.rsqrt(jnp.mean(xf * xf, axis=-1, keepdims=True) + EPS)
    return (y * g.astype(F32)).astype(x.dtype)

def t5_bucket(dist):
    n = jnp.maximum(dist, 0)
    max_exact = NUM_BUCKETS // 2
    nf = jnp.maximum(n, 1).astype(F32)
    large = max_exact + (jnp.log(nf / max_exact) / math.log(MAX_DISTANCE / max_exact)
                         * (NUM_BUCKETS - max_exact)).astype(jnp.int32)
    large = jnp.minimum(large, NUM_BUCKETS - 1)
    return jnp.where(n < max_exact, n, large)

def project(h, w):
    B, L, _ = h.shape
    u = h @ w
    cuts = [WIDTH_A, 2 * WIDTH_A, 3 * WIDTH_A, 3 * WIDTH_A + WIDTH_B, 3 * WIDTH_A + 2 * WIDTH_B]
    qa, ka, va, qd, kd, vd = jnp.split(u, cuts, axis=-1)
    sa = (B, L, N_HEADS_A, HEAD_DIM)
    sd = (B, L, N_HEADS_B, 2, HEAD_DIM)
    return (qa.reshape(sa), ka.reshape(sa), va.reshape(sa),
            qd.reshape(sd), kd.reshape(sd), vd.reshape(B, L, N_HEADS_B, 2 * HEAD_DIM))

def moba_select(qh, kmean, n_full):
    gate = jnp.einsum('bhqd,bhnd->bhqn', qh.astype(F32), kmean)
    gate = jnp.where(jnp.arange(kmean.shape[2]) < n_full, gate, -jnp.inf)
    top, idx = lax.top_k(gate, MOBA_TOPK)
    return idx, jnp.isfinite(top)

def moba_attend(qh, q_pos, k_sel, v_sel, k_pos_sel, sel_valid, k_own, v_own, k_pos_own, bias_t):
    scale = HEAD_DIM ** -0.5
    hi = jnp.arange(bias_t.shape[0])[None, :, None, None, None]
    d_sel = q_pos[None, None, :, None, None] - k_pos_sel
    s_sel = jnp.einsum('bhqd,bhqnkd->bhqnk', qh, k_sel).astype(F32) * scale + bias_t[hi, t5_bucket(d_sel)]
    s_sel = jnp.where(sel_valid[..., None], s_sel, -jnp.inf)
    d_own = q_pos[:, None] - k_pos_own[None, :]
    s_own = jnp.einsum('bhqd,bhkd->bhqk', qh, k_own).astype(F32) * scale + bias_t[:, t5_bucket(d_own)][None]
    s_own = jnp.where(d_own >= 0, s_own, -jnp.inf)
    B, H, Q, N, BLK = s_sel.shape
    p = jax.nn.softmax(jnp.concatenate([s_sel.reshape(B, H, Q, N * BLK), s_own], axis=-1), axis=-1)
    p = p.astype(v_own.dtype)
    p_sel = p[..., :N * BLK].reshape(B, H, Q, N, BLK)
    p_own = p[..., N * BLK:]
    return (jnp.einsum('bhqnk,bhqnkd->bhqd', p_sel, v_sel)
            + jnp.einsum('bhqk,bhkd->bhqd', p_own, v_own))

def moba_prompt(q, k, v, bias_t):
    B, S, H, Dh = q.shape
    nb = -(-S // MOBA_BLOCK)
    pad = nb * MOBA_BLOCK - S
    kb = jnp.pad(k, ((0, 0), (0, pad), (0, 0), (0, 0))).reshape(B, nb, MOBA_BLOCK, H, Dh).transpose(0, 3, 1, 2, 4)
    vb = jnp.pad(v, ((0, 0), (0, pad), (0, 0), (0, 0))).reshape(B, nb, MOBA_BLOCK, H, Dh).transpose(0, 3, 1, 2, 4)
    n_cand = max(nb, MOBA_TOPK)
    kmean = jnp.pad(kb.astype(F32).mean(3), ((0, 0), (0, 0), (0, n_cand - nb), (0, 0)))
    n_qb = S // MOBA_QBLOCK
    qblocks = q.transpose(0, 2, 1, 3).reshape(B, H, n_qb, MOBA_QBLOCK, Dh).transpose(2, 0, 1, 3, 4)
    bi = jnp.arange(B)[:, None, None, None]
    hi = jnp.arange(H)[None, :, None, None]

    def one_block(args):
        qb_idx, qblk = args
        q_pos = qb_idx * MOBA_QBLOCK + jnp.arange(MOBA_QBLOCK)
        own = (qb_idx * MOBA_QBLOCK) // MOBA_BLOCK
        idx, valid = moba_select(qblk, kmean, own)
        idx = jnp.minimum(idx, nb - 1)
        k_sel = kb[bi, hi, idx]
        v_sel = vb[bi, hi, idx]
        k_pos_sel = idx[..., None] * MOBA_BLOCK + jnp.arange(MOBA_BLOCK)
        k_own = lax.dynamic_index_in_dim(kb, own, axis=2, keepdims=False)
        v_own = lax.dynamic_index_in_dim(vb, own, axis=2, keepdims=False)
        k_pos_own = own * MOBA_BLOCK + jnp.arange(MOBA_BLOCK)
        return moba_attend(qblk, q_pos, k_sel, v_sel, k_pos_sel, valid, k_own, v_own, k_pos_own, bias_t)

    o = lax.map(one_block, (jnp.arange(n_qb), qblocks))
    return o.transpose(1, 0, 3, 2, 4).reshape(B, S, H * Dh)

def moba_sample(q, k_new, v_new, pool_k, pool_v, page_table, bias_t):
    DB, T, H, Dh = q.shape
    n_pages = page_table.shape[1]
    P = n_pages * PAGE_SIZE
    ppb = MOBA_BLOCK // PAGE_SIZE
    nbp = P // MOBA_BLOCK
    r = P - nbp * MOBA_BLOCK
    kfull = pool_k[page_table[:, :nbp * ppb]].reshape(DB, nbp, MOBA_BLOCK, H, Dh)
    n_cand = max(nbp, MOBA_TOPK)
    kmean = jnp.pad(kfull.astype(F32).mean(2).transpose(0, 2, 1, 3),
                    ((0, 0), (0, 0), (0, n_cand - nbp), (0, 0)))
    qh = q.transpose(0, 2, 1, 3)
    idx, valid = moba_select(qh, kmean, nbp)
    idx = jnp.minimum(idx, max(nbp - 1, 0))
    lp = jnp.minimum(idx[..., None] * ppb + jnp.arange(ppb), n_pages - 1)
    phys = page_table[jnp.arange(DB)[:, None, None, None, None], lp]
    hi = jnp.arange(H)[None, :, None, None, None, None]
    row = jnp.arange(PAGE_SIZE)
    k_sel = pool_k[phys[..., None], row, hi].reshape(DB, H, T, MOBA_TOPK, MOBA_BLOCK, Dh)
    v_sel = pool_v[phys[..., None], row, hi].reshape(DB, H, T, MOBA_TOPK, MOBA_BLOCK, Dh)
    k_pos_sel = idx[..., None] * MOBA_BLOCK + jnp.arange(MOBA_BLOCK)
    pt_own = page_table[:, nbp * ppb: nbp * ppb + r // PAGE_SIZE]
    k_own = jnp.concatenate([pool_k[pt_own].reshape(DB, r, H, Dh), k_new], axis=1).transpose(0, 2, 1, 3)
    v_own = jnp.concatenate([pool_v[pt_own].reshape(DB, r, H, Dh), v_new], axis=1).transpose(0, 2, 1, 3)
    k_pos_own = jnp.concatenate([nbp * MOBA_BLOCK + jnp.arange(r), P + jnp.arange(T)])
    q_pos = P + jnp.arange(T)
    o = moba_attend(qh, q_pos, k_sel, v_sel, k_pos_sel, valid, k_own, v_own, k_pos_own, bias_t)
    return o.transpose(0, 2, 1, 3).reshape(DB, T, H * Dh)

def diff_attend(q, k, v, q_pos, k_pos, bias_t, lam):
    scale = HEAD_DIM ** -0.5
    d = q_pos[:, None] - k_pos[None, :]
    s = jnp.einsum('bqhcd,bkhcd->bhcqk', q, k).astype(F32) * scale + bias_t[:, t5_bucket(d)][None, :, None]
    s = jnp.where(d >= 0, s, -jnp.inf)
    p = jax.nn.softmax(s, axis=-1)
    a = (p[:, :, 0] - lam * p[:, :, 1]).astype(v.dtype)
    return jnp.einsum('bhqk,bkhe->bqhe', a, v)

def diff_prompt(q, k, v, bias_t, lam):
    B, S = q.shape[:2]
    n = S // DIFF_QBLOCK
    qblocks = q.reshape(B, n, DIFF_QBLOCK, N_HEADS_B, 2, HEAD_DIM).swapaxes(0, 1)
    k_pos = jnp.arange(S)
    o = lax.map(lambda a: diff_attend(a[1], k, v, a[0] * DIFF_QBLOCK + jnp.arange(DIFF_QBLOCK),
                                      k_pos, bias_t, lam), (jnp.arange(n), qblocks))
    return o.swapaxes(0, 1).reshape(B, S, N_HEADS_B, 2 * HEAD_DIM)

def diff_sample(q, k_new, v_new, pool_k, pool_v, page_table, bias_t, lam):
    DB, T = q.shape[:2]
    P = page_table.shape[1] * PAGE_SIZE
    kp = pool_k[page_table].reshape(DB, P, N_HEADS_B, 2, HEAD_DIM)
    vp = pool_v[page_table].reshape(DB, P, N_HEADS_B, 2 * HEAD_DIM)
    k_all = jnp.concatenate([kp, k_new], axis=1)
    v_all = jnp.concatenate([vp, v_new], axis=1)
    return diff_attend(q, k_all, v_all, P + jnp.arange(T), jnp.arange(P + T), bias_t, lam)

def diff_post(o, gain, lam_init):
    B, L = o.shape[:2]
    return (rmsnorm(o, gain) * (1.0 - lam_init)).reshape(B, L, WIDTH_B)

def merge(h, oa, ob, w_gate, w_out_a, w_out_b, w_out):
    g = jax.nn.sigmoid((h @ w_gate).astype(F32)).astype(h.dtype)
    ga, gb = jnp.split(g, 2, axis=-1)
    return (ga * (oa @ w_out_a) + gb * (ob @ w_out_b)) @ w_out

def conv_ffn(h, prev, w_up, conv_w, conv_b, w_down):
    L = h.shape[1]
    u = h @ w_up
    ext = jnp.concatenate([prev.astype(u.dtype), u], axis=1)
    c = conv_b
    for i in range(CONV_W):
        c = c + conv_w[i] * ext[:, i:i + L]
    gate, val = jnp.split(c, 2, axis=-1)
    return (jax.nn.silu(gate) * val) @ w_down, ext[:, L:]

def layer_forward(x, conv_prev, attend, nrm_a, w_in_l, w_gate_l, w_oa, w_ob, w_o, nrm_f, w_up_l, cw, cb, w_dn):
    B, L, _ = x.shape
    h = rmsnorm(x, nrm_a)
    qa, ka, va, qd, kd, vd = project(h, w_in_l)
    oa, ob = attend(qa, ka, va, qd, kd, vd)
    x = x + merge(h, oa, ob, w_gate_l, w_oa, w_ob, w_o)
    f, conv_new = conv_ffn(rmsnorm(x, nrm_f), conv_prev, w_up_l, cw, cb, w_dn)
    return x + f, (ka, va, kd.reshape(B, L, N_HEADS_B, 2 * HEAD_DIM), vd, conv_new)

def setup_inputs(seed: int = 0) -> dict:
    key = jax.random.key(seed)
    ks = jax.random.split(key, 32)
    n_pages = PAST_LEN // PAGE_SIZE
    n_used = DEC_BATCH * n_pages
    n_phys = n_used + n_used // 4

    def nrm(k, shape, s):
        return jax.random.normal(k, shape, F32) * s

    return {
        "x_prompt": nrm(ks[0], (BATCH, SEQ, D_MODEL), 1.0),
        "x_sample": nrm(ks[1], (DEC_BATCH, DEC_SEQ, D_MODEL), 1.0),
        "cache_moba_k": nrm(ks[2], (DEPTH, n_phys, PAGE_SIZE, N_HEADS_A, HEAD_DIM), 1.0),
        "cache_moba_v": nrm(ks[3], (DEPTH, n_phys, PAGE_SIZE, N_HEADS_A, HEAD_DIM), 1.0),
        "cache_diff_k": nrm(ks[4], (DEPTH, n_phys, PAGE_SIZE, N_HEADS_B, 2 * HEAD_DIM), 1.0),
        "cache_diff_v": nrm(ks[5], (DEPTH, n_phys, PAGE_SIZE, N_HEADS_B, 2 * HEAD_DIM), 1.0),
        "state_conv": nrm(ks[6], (DEPTH, DEC_BATCH, CONV_W - 1, 2 * D_FF), 1.0),
        "page_table": jax.random.permutation(ks[7], n_phys)[:n_used].reshape(DEC_BATCH, n_pages).astype(jnp.int32),
        "rel_bias": nrm(ks[8], (NUM_BUCKETS, N_HEADS_A + N_HEADS_B), 0.5),
        "norm_attn": 1.0 + nrm(ks[9], (DEPTH, D_MODEL), 0.01),
        "w_in": nrm(ks[10], (DEPTH, D_MODEL, N_IN), D_MODEL ** -0.5),
        "w_gate": nrm(ks[11], (DEPTH, D_MODEL, 2 * D_MODEL), D_MODEL ** -0.5),
        "w_out_a": nrm(ks[12], (DEPTH, WIDTH_A, D_MODEL), WIDTH_A ** -0.5),
        "w_out_b": nrm(ks[13], (DEPTH, WIDTH_B, D_MODEL), WIDTH_B ** -0.5),
        "w_out": nrm(ks[14], (DEPTH, D_MODEL, D_MODEL), D_MODEL ** -0.5),
        "lambda_q1": nrm(ks[15], (DEPTH, HEAD_DIM), 0.1),
        "lambda_k1": nrm(ks[16], (DEPTH, HEAD_DIM), 0.1),
        "lambda_q2": nrm(ks[17], (DEPTH, HEAD_DIM), 0.1),
        "lambda_k2": nrm(ks[18], (DEPTH, HEAD_DIM), 0.1),
        "diff_norm": 1.0 + nrm(ks[19], (DEPTH, 2 * HEAD_DIM), 0.01),
        "norm_ffn": 1.0 + nrm(ks[20], (DEPTH, D_MODEL), 0.01),
        "w_up": nrm(ks[21], (DEPTH, D_MODEL, 2 * D_FF), D_MODEL ** -0.5),
        "conv_w": nrm(ks[22], (DEPTH, CONV_W, 2 * D_FF), CONV_W ** -0.5),
        "conv_b": nrm(ks[23], (DEPTH, 2 * D_FF), 0.01),
        "w_down": nrm(ks[24], (DEPTH, D_FF, D_MODEL), D_FF ** -0.5),
        "norm_final": 1.0 + nrm(ks[25], (D_MODEL,), 0.01),
    }

def reference(x_prompt, x_sample, cache_moba_k, cache_moba_v, cache_diff_k, cache_diff_v, state_conv,
              page_table, rel_bias, norm_attn, w_in, w_gate, w_out_a, w_out_b, w_out,
              lambda_q1, lambda_k1, lambda_q2, lambda_k2, diff_norm, norm_ffn, w_up, conv_w, conv_b,
              w_down, norm_final):
    bias_a = rel_bias[:, :N_HEADS_A].T
    bias_d = rel_bias[:, N_HEADS_A:].T
    xp, xs = x_prompt, x_sample
    mk_p, mv_p, dk_p, dv_p, cv_p = [], [], [], [], []
    mk_s, mv_s, dk_s, dv_s, cv_s = [], [], [], [], []
    for l in range(DEPTH):
        lam_init = 0.8 - 0.6 * math.exp(-0.3 * l)
        lam = (jnp.exp(jnp.sum(lambda_q1[l].astype(F32) * lambda_k1[l].astype(F32)))
               - jnp.exp(jnp.sum(lambda_q2[l].astype(F32) * lambda_k2[l].astype(F32))) + lam_init)
        lw = (norm_attn[l], w_in[l], w_gate[l], w_out_a[l], w_out_b[l], w_out[l],
              norm_ffn[l], w_up[l], conv_w[l], conv_b[l], w_down[l])

        def attend_prompt(qa, ka, va, qd, kd, vd, l=l, lam=lam, lam_init=lam_init):
            oa = moba_prompt(qa, ka, va, bias_a)
            ob = diff_post(diff_prompt(qd, kd, vd, bias_d, lam), diff_norm[l], lam_init)
            return oa, ob

        def attend_sample(qa, ka, va, qd, kd, vd, l=l, lam=lam, lam_init=lam_init):
            oa = moba_sample(qa, ka, va, cache_moba_k[l], cache_moba_v[l], page_table, bias_a)
            ob = diff_post(diff_sample(qd, kd, vd, cache_diff_k[l], cache_diff_v[l], page_table, bias_d, lam),
                           diff_norm[l], lam_init)
            return oa, ob

        conv0 = jnp.zeros((xp.shape[0], CONV_W - 1, 2 * D_FF), xp.dtype)
        xp, (a, b, c, d, e) = layer_forward(xp, conv0, attend_prompt, *lw)
        mk_p.append(a); mv_p.append(b); dk_p.append(c); dv_p.append(d); cv_p.append(e)
        xs, (a, b, c, d, e) = layer_forward(xs, state_conv[l], attend_sample, *lw)
        mk_s.append(a); mv_s.append(b); dk_s.append(c); dv_s.append(d); cv_s.append(e)
    y_prompt = rmsnorm(xp, norm_final)
    y_sample = rmsnorm(xs, norm_final)
    return (y_prompt, y_sample,
            jnp.stack(mk_p), jnp.stack(mv_p), jnp.stack(dk_p), jnp.stack(dv_p), jnp.stack(cv_p),
            jnp.stack(mk_s), jnp.stack(mv_s), jnp.stack(dk_s), jnp.stack(dv_s), jnp.stack(cv_s))


_drawn_inputs = setup_inputs


def setup_inputs(seed=0):
    import zlib

    import numpy as np

    out = dict(_drawn_inputs(seed))
    spreads = {}
    factors = {'norm_attn': 5.675,
     'lambda_k1': 2.909,
     'lambda_k2': 4.57,
     'diff_norm': 8.0,
     'norm_ffn': 5.93,
     'conv_b': 8.0,
     'norm_final': 5.548}
    for name, (base, spread) in spreads.items():
        noise = np.random.default_rng([zlib.crc32(name.encode()), seed]).standard_normal(out[name].shape)
        drawn = base * np.exp(spread * noise) if base else spread * noise
        out[name] = __import__('jax').numpy.asarray(drawn.astype(out[name].dtype))
    for name, factor in factors.items():
        out[name] = (out[name] * factor).astype(out[name].dtype)
    return out
```

```python
import math
from contextlib import ExitStack

import numpy as np
import concourse.bass as bass
from concourse import mybir

F32 = mybir.dt.float32
I32 = mybir.dt.int32
ALU = mybir.AluOpType
ACT = mybir.ActivationFunctionType
AX = mybir.AxisListType

P = 128
D = 1024
DT = D // P
SEQ = 256
DB, T = 8, 4
NEW = DB * T
TOK = SEQ + NEW
PAST, PAGE = 1024, 128
NPG = PAST // PAGE
NPHYS = DB * NPG + DB * NPG // 4
BLOCK = 256
NBLK = PAST // BLOCK
HD = 64
WID = 512
N_IN = 6 * WID
FF = 2816
FT = FF // P
BUCKETS, HEADS = 32, 12
EPS = 1e-6
LAM0 = 0.8 - 0.6 * math.exp(0.0)
SCALE = HD ** -0.5
MASKED = -1.0e30
LOWEST = -3.0e38

TOKENS = [(0, P), (P, P), (SEQ, NEW)]
PAIRS = DB // 2
STEPS = 2 * NPG
KSLOTS = 8
OWN = PAST
KEYS = PAST + NEW
RESULT = [0, 1, 2, 3, 4, 5, 6, 7, 9, 11, 13, 15]
SET_UP = 10
EXT = 310
CONV = 304
GW = 384

C_ID, C_TM, C_HOT, C_MASK, C_G, C_VEC = 0, 128, 256, 417, 545, 929
C_ALL = 936


def bucket(n):
    n = max(int(n), 0)
    if n < BUCKETS // 2:
        return n
    large = 16 + int(np.float32(np.log(np.float32(n) / np.float32(16))) / np.float32(math.log(8.0)) * np.float32(16))
    return min(large, BUCKETS - 1)


def constants():
    c = np.zeros((P, C_ALL), np.float32)
    c[:, C_ID:C_ID + P] = np.eye(P)
    rows = np.arange(P)
    for part in range(P):
        t, b = divmod(part, BUCKETS)
        c[part, C_TM:C_TM + P] = rows % T == t
        hot = [bucket(PAST)] + [bucket(PAST + t - k) for k in range(PAST - PAGE, PAST)]
        hot += [bucket(t - k % T) for k in range(NEW)]
        c[part, C_HOT:C_HOT + 161] = np.array(hot) == b
    for r in range(P):
        for i in range(PAIRS):
            for k in range(NEW):
                seen = k // T == 2 * i + r // 64 and k % T <= r % T
                c[r, C_MASK + NEW * i + k] = 0.0 if seen else MASKED
    for m in range(GW):
        n = 2 * P - 1 - m
        c[bucket(n) if n >= 0 else BUCKETS, C_G + m] = 1.0
    diff = rows // 32 % 2 == 1
    second = diff & (rows // T % 2 == 1)
    c[:, C_VEC] = ~second
    c[:, C_VEC + 1] = second
    c[:, C_VEC + 2] = np.where(diff, 0.0, MASKED)
    c[:, C_VEC + 3:C_VEC + 7] = np.arange(1, NBLK + 1)
    return c


def so_far(c, par, per):
    return (c + par) * (per // 2) + (0 if par else per)


def first(i):
    return isinstance(i, int) and i == 0


def early(c):
    return isinstance(c, int) and c < 2


def page_used(i, s):
    return i * (STEPS + 1) + (s - 1 if s >= 2 else s - 2)


class Tally:

    def __init__(self, sem):
        self.sem, self.n, self.base = sem, 0, 0

    def add(self, ins):
        ins.then_inc(self.sem, 1)
        self.n += 1

    def wait(self, eng):
        eng.wait_ge(self.sem, self.base + self.n)

    def enter(self, i, first, per):
        self.start, self.per = self.n, per
        self.base, self.n = (i - first) * per + self.n, 0

    def leave(self, times):
        assert self.n == self.per, (self.n, self.per)
        self.base, self.n = 0, self.start + times * self.per


def build(nc, a, out):
    with ExitStack() as ctx:
        def sb(name, shape, dt=F32):
            return ctx.enter_context(nc.sbuf_tensor(name, shape, dt))

        def sem(name):
            return ctx.enter_context(nc.semaphore(name))

        ps = ctx.enter_context(nc.psum_tensor("ps", [P, 8, 512], F32))
        con = sb("con", [P, C_ALL])
        ones = sb("ones", [P, P])
        xT = sb("xT", [P, DT, TOK])
        hT = sb("hT", [P, DT, TOK])
        oT = sb("oT", [P, 8, TOK])
        wbuf = sb("wbuf", [P, 2, 4096])
        arena_q = sb("arena_q", [P, 24 * TOK])
        vnat = sb("vnat", [P, 3, 2, WID])
        arena_v = sb("arena_v", [P, 8192])
        arena_k = sb("arena_k", [P, 8192])
        arena_s = sb("arena_s", [P, 6400])
        bias_s = sb("bias_s", [P, KEYS])
        gcol = sb("gcol", [P, DT, 3])
        vecs = sb("vecs", [4, D])
        relb = sb("relb", [P, HEADS])
        relm = sb("relm", [BUCKETS + 1, HEADS])
        pages = sb("pages", [1, DB * NPG], I32)
        small = sb("small", [P, 64])
        rr = sb("rr", [P, TOK])
        qbd = sb("qbd", [P, 8 * (DB + 2) * 8])
        qrow = sb("qrow", [P, 128])
        endbuf = sb("endbuf", [P, 2 * 4 * 18])

        ident = con[:, C_ID:C_ID + P]
        hot = con[:, C_HOT:C_HOT + 161]
        qkvT = arena_q[:, :].rearrange("p (m t) -> p m t", t=TOK)
        ffT = arena_q[:, 0:FT * TOK].rearrange("p (m t) -> p m t", t=TOK)
        vring = arena_v[:, :].rearrange("p (s g n) -> p s g n", s=2, n=WID)
        pbias = arena_v[:, 0:HEADS * GW].rearrange("p (h n) -> p h n", n=GW)
        pS = arena_v[:, 4608:4608 + 4 * GW].rearrange("p (u n) -> p u n", n=GW)
        pPT = arena_v[:, 6144:6144 + 2 * GW].rearrange("p (u n) -> p u n", n=GW)
        pstat = arena_v[:, 6912:6912 + 16 * 8].rearrange("p (u n) -> p u n", n=8)
        gT = arena_v[:, 0:2 * DT * TOK].rearrange("p (m t) -> p m t", t=TOK)
        kring = arena_k[:, :].rearrange("p (s k n) -> p s k n", s=KSLOTS, n=WID)
        mT = arena_k[:, 0:DT * TOK].rearrange("p (m t) -> p m t", t=TOK)
        ext = arena_k[:, 2304:2304 + 8 * EXT].rearrange("p (m t) -> p m t", t=EXT)
        cv = arena_k[:, 4784:4784 + 4 * 306].rearrange("p (m t) -> p m t", t=306)
        frow = arena_k[:, 6016:6016 + 2 * 512].rearrange("p (s n) -> p s n", s=2)
        fcol = arena_k[:, 7040:7040 + 80].rearrange("p (m n) -> p m n", n=20)
        ends = endbuf[:, :].rearrange("p (s q r) -> p s q r", s=2, q=4)
        cst = arena_k[:, 7120:7120 + 1024].rearrange("p (s n) -> p s n", s=2)
        kTs = arena_s[:, 0:2048].rearrange("p (s k n) -> p s k n", s=2, k=2)
        STs = arena_s[:, 2048:3072].rearrange("p (g r) -> p g r", g=NPG)
        STo = arena_s[:, 3072:3200]
        Sb = arena_s[:, 3200:3200 + KEYS]
        PTs = arena_s[:, 4256:5280].rearrange("p (g r) -> p g r", g=NPG)
        PTo = arena_s[:, 5280:5408]
        Qbd = qbd[:, :].rearrange("p (k b c) -> p k b c", k=8, c=8)
        Qcur = qrow[:, :].rearrange("p (k b c) -> p k b c", k=8, c=8)
        sst = arena_s[:, 6048:6112]
        ownb = arena_s[:, 6112:6144]
        xnat = arena_s[:, 0:3072].rearrange("p (t n) -> p t n", n=D)
        knat = arena_s[:, 2048:5120].rearrange("p (t k n) -> p t k n", t=3, n=WID)
        Wrel = arena_s[:, 5120:5248]
        Gsb = arena_s[0:HEADS, 5248:5248 + GW]
        lamv = arena_s[:, 5632:5888].rearrange("p (v n) -> p v n", v=4)
        ynat = arena_s[:, 0:3072].rearrange("p (t n) -> p t n", n=D)
        dsq = arena_s[:, 0:4 * TOK].rearrange("p (m t) -> p m t", t=TOK)
        drr = arena_s[:, 1152:1152 + 4 * TOK].rearrange("p (m t) -> p m t", t=TOK)
        ztmp = arena_s[:, 2304:2304 + 2 * TOK].rearrange("p (s t) -> p s t", s=2)
        neglam, dgain, far = small[:, 0:1], small[:, 1:2], small[:, 2:3]
        rweight = small[:, 3:4]

        gdram = nc.dram_tensor("bias_lines", [HEADS, P, GW], F32, kind="Internal")

        x_in, con_in, small_in, pt_in, bias_in = (sem(n) for n in ("x_in", "con_in", "small_in", "pt_in", "bias_in"))
        w_in = [sem(f"w_in{s}") for s in range(2)]
        k_in = [sem(f"k_in{s}") for s in range(KSLOTS)]
        v_in = [sem(f"v_in{s}") for s in range(2)]
        f_in = [sem(f"f_in{s}") for s in range(2)]
        g_out, k_out, stored = sem("g_out"), sem("k_out"), sem("stored")
        cst_out = [sem(f"cst_out{s}") for s in range(2)]
        consts_set, set_up, set_pe, lam_summed, lam_exped = (
            sem(n) for n in ("consts_set", "set_up", "set_pe", "lam_summed", "lam_exped"))
        vec_own, act_own = Tally(sem("vec_own")), Tally(sem("act_own"))
        x_turned, x_copied = sem("x_turned"), sem("x_copied")
        squared, summed, meaned, rooted, normed = (sem(n) for n in ("squared", "summed", "meaned", "rooted", "normed"))
        tile_ready = sem("tile_ready")
        in_taken, mix_taken, down_taken = sem("in_taken"), sem("mix_taken"), sem("down_taken")
        nat_ready, nat_taken = sem("nat_ready"), sem("nat_taken")
        q_scaled = sem("q_scaled")
        p_scores, p_biased, p_exped, p_probs = (sem(n) for n in ("p_scores", "p_biased", "p_exped", "p_probs"))
        p_turned, p_pt, p_mixed, p_taken = (sem(n) for n in ("p_turned", "p_pt", "p_mixed", "p_taken"))
        vec_p, own_biased, edges_set = sem("p_maxima"), sem("own_biased"), sem("edges_set")
        q_ready = sem("q_ready")
        k_turned, scored = sem("k_turned"), sem("scored")
        k_copied = [sem("k_copied_moba"), sem("k_copied_diff")]
        st_copied_v, st_copied_a = sem("st_copied_v"), sem("st_copied_a")
        rows_ready, m_ready, s_exped, s_probs = (sem(n) for n in ("rows_ready", "m_ready", "s_exped", "s_probs"))
        pt_ready, pt_copied_v, pt_copied_a = sem("pt_ready"), sem("pt_copied_v"), sem("pt_copied_a")
        v_used, o_taken = sem("v_used"), sem("o_taken")
        d_squared, d_summed, d_meaned, d_rooted, d_done = (
            sem(n) for n in ("d_squared", "d_summed", "d_meaned", "d_rooted", "d_done"))
        f_turned, f_copied, ext_ready = sem("f_turned"), sem("f_copied"), sem("ext_ready")
        conv_done, silu_done, ff_done = sem("conv_done"), sem("silu_done"), sem("ff_done")
        ends_packed, mask_set = sem("ends_packed"), sem("mask_set")
        c_turned, c_staged, half_used = sem("c_turned"), sem("c_staged"), sem("half_used")
        y_turned, y_copied_a, y_copied_v = sem("y_turned"), sem("y_copied_a"), sem("y_copied_v")

        NCH = 33
        IN0, GATE0, OA, OB, OUT0, UP0, DOWN0 = 0, 6, 10, 11, 12, 14, 25
        T_GATE, T_OA, T_OB, T_OUT, T_UP, T_DOWN = 24, 40, 48, 56, 64, 108

        w_in_v = a["w_in"][0].rearrange("(k p) n -> p k n", p=P)
        w_gate_v = a["w_gate"][0].rearrange("(k p) n -> p k n", p=P)
        w_oa_v = a["w_out_a"][0].rearrange("(k p) n -> p k n", p=P)
        w_ob_v = a["w_out_b"][0].rearrange("(k p) n -> p k n", p=P)
        w_out_v = a["w_out"][0].rearrange("(k p) n -> p k n", p=P)
        w_up_v = a["w_up"][0].rearrange("(k p) (h n) -> p k h n", p=P, h=2)
        w_down_v = a["w_down"][0].rearrange("(k p) n -> p k n", p=P)

        def slot8(s):
            return wbuf[:, s, :].rearrange("p (k n) -> p k n", k=8)

        def slot4(s):
            return wbuf[:, s, :].rearrange("p (k n) -> p k n", k=4)

        def slot_up(s, h):
            return wbuf[:, s, 2048 * h:2048 * h + 2048].rearrange("p (k n) -> p k n", k=8)

        def slot11(s):
            return wbuf[:, s, 0:11 * 256].rearrange("p (k n) -> p k n", k=11)

        block = ctx.enter_context(nc.Block())

        @block.sync
        def _(sp):
            for n, (t0, cnt) in enumerate(TOKENS):
                src = a["x_prompt"][0][t0:t0 + cnt] if n < 2 else a["x_sample"].rearrange("b t n -> (b t) n")
                sp.dma_start(xnat[0:cnt, n, :], src).then_inc(x_in, 16)
            sp.dma_start(con[:, :], a["constants"]).then_inc(con_in, 16)
            sp.dma_start(vecs[0:1, :], a["norm_attn"]).then_inc(small_in, 16)
            sp.dma_start(vecs[1:2, :], a["norm_ffn"]).then_inc(small_in, 16)
            sp.dma_start(vecs[2:3, :], a["norm_final"].rearrange("(o n) -> o n", o=1)).then_inc(small_in, 16)
            for t in range(T):
                sp.dma_start(relb[32 * t:32 * t + 32, :], a["rel_bias"]).then_inc(small_in, 16)
            sp.dma_start(relm[0:BUCKETS, :], a["rel_bias"]).then_inc(small_in, 16)
            sp.dma_start(small[:, 4:5], a["diff_norm"].rearrange("o n -> n o")).then_inc(small_in, 16)
            for n, name in enumerate(("lambda_q1", "lambda_k1", "lambda_q2", "lambda_k2")):
                sp.dma_start(lamv[:, n, :], a[name].broadcast_to([P, HD])).then_inc(small_in, 16)
            sp.dma_start(pages[:, :], a["page_table"].rearrange("(o b) g -> o (b g)", o=1)).then_inc(pt_in, 16)
            sp.wait_ge(set_up, 2)
            sp.dma_start(gdram[:, :, :], Gsb.unsqueeze(1).broadcast_to([HEADS, P, GW])).then_inc(g_out, 16)
            sp.wait_ge(g_out, 16)
            g = gdram[:, :, :]
            sp.dma_start(pbias[:, :, 0:256], bass.AP(g.tensor, P - 1, [[GW - 1, P], [P * GW, HEADS], [1, 256]])
                         ).then_inc(bias_in, 16)
            sp.dma_start(pbias[:, :, 256:384], bass.AP(g.tensor, 2 * P - 1, [[GW - 1, P], [P * GW, HEADS], [1, P]])
                         ).then_inc(bias_in, 16)
            sp.wait_ge(pt_in, 16)

            def page_id(entry):
                return sp.value_load(pages[0:1, bass.ds(entry, 1)], min_val=0, max_val=NPHYS - 1)

            def page(name, pg):
                return a[name][0].rearrange("g p h n -> g p (h n)")[bass.ds(pg, 1)].rearrange("o p n -> (o p) n")

            def load_k(i):
                for s in range(STEPS):
                    pg = page_id(i * STEPS + s)
                    if not (first(i) and s < KSLOTS):
                        sp.wait_ge(k_turned, i * 2 * STEPS + 2 * (s - KSLOTS + 1))
                    for kind, name in enumerate(("cache_moba_k", "cache_diff_k")):
                        sp.dma_start(kring[:, s % KSLOTS, kind, :], page(name, pg)
                                     ).then_inc(k_in[s % KSLOTS], 16)

            def load_v(i):
                for n in range(4):
                    b2, kind = divmod(n, 2)
                    for g in range(NPG):
                        pg = page_id(i * STEPS + b2 * NPG + g)
                        if g == 0 and not (first(i) and n < 2):
                            sp.wait_ge(v_used, i * 4 + n - 1)
                        sp.dma_start(vring[:, kind, g, :], page("cache_diff_v" if kind else "cache_moba_v", pg)
                                     ).then_inc(v_in[kind], 16)

            load_k(0)
            sp.wait_ge(p_taken, 8)
            load_k(1)
            load_v(0)
            with sp.Fori(2, PAIRS) as i:
                load_k(i)
                load_v(i - 1)
            load_v(PAIRS - 1)

            def conv_rows(c, par):
                for r0, src in ((0, a["state_conv"][0].rearrange("b r n -> (b r) n")),
                                (16, a["conv_w"][0]), (19, a["conv_b"])):
                    rows = src.shape[0]
                    for h in range(2):
                        sp.dma_start(frow[r0:r0 + rows, par, h * 256:h * 256 + 256],
                                     src[:, bass.ds(c * 256 + h * FF, 256)]).then_inc(f_in[par], 16)

            sp.wait_ge(k_turned, PAIRS * 2 * STEPS)
            conv_rows(0, 0)
            conv_rows(1, 1)
            sp.wait_ge(f_turned, 1)
            conv_rows(2, 0)
            with sp.Fori(1, 5) as i:
                for c, par in ((2 * i + 1, 1), (2 * i + 2, 0)):
                    sp.wait_ge(f_turned, c - 1)
                    conv_rows(c, par)

        @block.gpsimd
        def _(pool):
            nc.gpsimd.memset(ones[:, :], 1.0).then_inc(consts_set, 1)
            nc.gpsimd.memset(qbd[:, :], 0.0).then_inc(consts_set, 1)
            nc.gpsimd.memset(sst[:, :], 0.0).then_inc(consts_set, 1)
            for g in range(12):
                kind, tt = divmod(g, 3)
                pool.wait_ge(nat_taken, g + 1)
                src = (knat if kind < 2 else vnat)[0:TOKENS[tt][1], tt, kind % 2, :]
                name = ("moba_k", "diff_k", "moba_v", "diff_v")[kind]
                if tt < 2:
                    dst = out[name + "_prompt"][0, 0, tt * P:tt * P + P].rearrange("t h n -> t (h n)")
                else:
                    dst = out[name + "_sample"][0].rearrange("b t h n -> (b t) (h n)")
                pool.dma_start(dst, src).then_inc(k_out if kind < 2 else stored, 16)

            def conv_store(c, par):
                pool.wait_ge(c_staged, c + 1)
                for h in range(2):
                    cols = slice(h * 256, h * 256 + 256)
                    for part, dst in ((cst[0:2, par, cols], out["conv_prompt"][0, 0]),
                                      (cst[2:18, par, cols], out["conv_sample"][0].rearrange("b r n -> (b r) n"))):
                        pool.dma_start(dst[:, bass.ds(c * 256 + h * FF, 256)], part).then_inc(cst_out[par], 16)

            for c in range(3):
                conv_store(c, c % 2)
            with pool.Fori(1, 5) as i:
                conv_store(2 * i + 1, 1)
                conv_store(2 * i + 2, 0)
            for n, (t0, cnt) in enumerate(TOKENS):
                pool.wait_ge(y_copied_a, n + 1)
                pool.wait_ge(y_copied_v, n + 1)
                dst = out["y_prompt"][0][t0:t0 + cnt] if n < 2 else out["y_sample"].rearrange("b t n -> (b t) n")
                pool.dma_start(dst, ynat[0:cnt, n, :]).then_inc(stored, 16)
            pool.wait_ge(stored, 16 * 9)
            pool.wait_ge(k_out, 16 * 6)
            pool.wait_ge(cst_out[0], 64 * 6)
            pool.wait_ge(cst_out[1], 64 * 5)

        @block.tensor
        def _(pe):
            mm, turn = nc.tensor.matmul, nc.tensor.transpose

            def sum_of_squares(use):
                for j in range(DT):
                    pe.wait_ge(squared, DT * use + j + 1)
                    last = mm(ps[:, 7, 0:TOK], ones[:, :], hT[:, j, :], start=(j == 0), stop=(j == DT - 1))
                last.then_inc(summed, 1)

            def tile(bank, weights, moving, opens=True, stop=True):
                for k, (w, x) in enumerate(zip(weights, moving)):
                    last = mm(ps[:, bank, 0:TOK], w, x, start=(opens and k == 0),
                              stop=(stop and k == len(moving) - 1))
                return last

            pe.wait_ge(con_in, 16)
            pe.wait_ge(small_in, 16 * 13)
            pe.wait_ge(consts_set, 3)
            pe.wait_ge(mask_set, 1)
            for j in range(DT):
                last = turn(ps[:, 4, 4 * j:4 * j + 3], vecs[0:3, j * P:j * P + P], ident[0:3, 0:3])
            last.then_inc(set_pe, 1)
            mm(ps[0:HEADS, 5, 0:GW], relm[:, :], con[0:BUCKETS + 1, C_G:C_G + GW], start=True, stop=True
               ).then_inc(set_pe, 1)
            pe.wait_ge(x_in, 48)
            for j in range(DT):
                if j >= 4:
                    pe.wait_ge(x_copied, j - 3)
                for n, (t0, cnt) in enumerate(TOKENS):
                    last = turn(ps[:, j % 4, t0:t0 + cnt], xnat[0:cnt, n, j * P:j * P + P], ident[0:cnt, 0:cnt])
                last.then_inc(x_turned, 1)
            pe.wait_ge(set_up, 6)
            mm(ps[:, 6, 0:161], Wrel, hot, start=True, stop=True).then_inc(set_pe, 1)
            sum_of_squares(0)

            h = [hT[:, k, :] for k in range(DT)]
            pe.wait_ge(normed, DT)
            with pe.Fori(0, 3) as i:
                for s in range(2):
                    pe.wait_ge(w_in[s], (i + 1) * 16)
                    for q in range(4):
                        pe.wait_ge(in_taken, i * 8 + (4 * s + q + 1))
                        tile(q, [slot8(s)[:, k, q * P:q * P + P] for k in range(DT)], h).then_inc(tile_ready, 1)

            pe.wait_ge(set_up, SET_UP)
            for g in range(12):
                kind, tt = divmod(g, 3)
                m0 = (4, 16, 8, 20)[kind]
                t0, cnt = TOKENS[tt]
                pe.wait_ge(in_taken, 4 + m0 + 4)
                if g >= 2:
                    pe.wait_ge(nat_taken, g - 1)
                for q in range(4):
                    last = turn(ps[0:cnt, 4 + g % 2, q * P:q * P + P], qkvT[:, m0 + q, t0:t0 + cnt], ident)
                last.then_inc(nat_ready, 1)

            def p_score(u):
                kind, p, hh = u // 8, u % 8 // 2, u % 2
                q0, k0, rows = 12 * kind + p, 12 * kind + 4 + p, slice(64 * hh, 64 * hh + 64)
                if u >= 3:
                    pe.wait_ge(p_biased, 2 * (u - 2))
                mm(ps[:, u % 3, 0:256], qkvT[rows, q0, P:2 * P], qkvT[rows, k0, 0:256], start=True, stop=True)
                mm(ps[:, u % 3, 256:384], qkvT[rows, q0, 0:P], qkvT[rows, k0, 0:P], start=True, stop=True
                   ).then_inc(p_scores, 1)

            def p_turn(v):
                u = RESULT[v]
                pe.wait_ge(p_probs, 2 * (v + 1))
                if v >= 2:
                    pe.wait_ge(p_pt, v - 1)
                b = 3 + v % 2
                turn(ps[:, b, 0:P], pS[:, u % 4, 256:384], ident)
                turn(ps[:, b, P:2 * P], pS[:, u % 4, 0:P], ident)
                turn(ps[:, b, 2 * P:3 * P], pS[:, u % 4, P:2 * P], ident).then_inc(p_turned, 1)

            def p_mix(v):
                kind, o = v // 8, (v // 2 if v < 8 else v - 4)
                if kind == 0:
                    rows, cols = slice(64 * (v % 2), 64 * (v % 2) + 64), slice(HD * v, HD * v + HD)
                else:
                    rows, cols = slice(0, P), slice(P * (v - 8), P * (v - 8) + P)
                if o >= 2 and (kind == 1 or v % 2 == 0):
                    pe.wait_ge(p_taken, o - 1)
                pe.wait_ge(p_pt, v + 1)
                b = 5 + o % 2
                mm(ps[rows, b, 0:256], vnat[:, 0, kind, cols], pPT[:, v % 2, 0:256], start=True, stop=False)
                mm(ps[rows, b, P:256], vnat[:, 1, kind, cols], pPT[:, v % 2, 256:384], start=False, stop=True
                   ).then_inc(p_mixed, 1)

            pe.wait_ge(in_taken, 4 + 24)
            pe.wait_ge(q_scaled, 2)
            pe.wait_ge(nat_taken, 12)
            for u in range(16 + 3):
                if u < 16:
                    p_score(u)
                if u - 2 in RESULT:
                    p_turn(RESULT.index(u - 2))
                if u - 3 in RESULT:
                    p_mix(RESULT.index(u - 3))

            def s_turn(i, s):
                slot = s % KSLOTS
                pe.wait_ge(k_in[slot], i * 64 + 32 * (s // KSLOTS + 1))
                for kind in range(2):
                    if not (first(i) and s == 0):
                        pe.wait_ge(k_copied[kind], i * STEPS + s)
                    for p in range(4):
                        last = turn(ps[:, kind, p * P:p * P + P], kring[:, slot, kind, p * P:p * P + P], ident)
                    last.then_inc(k_turned, 1)

            def s_score(i, s):
                b2, g = divmod(s, NPG)
                for kind in range(2):
                    pe.wait_ge(k_copied[kind], i * STEPS + s + 1)
                    for p in range(4):
                        col = P * (g % 4) + 64 * b2 + 32 * kind + 8 * p
                        last = mm(ps[:, 2 + g // 4, col:col + 8], kTs[:, s % 2, kind, p * P:p * P + P],
                                  Qcur[:, 4 * kind + p, b2, :], start=True, stop=True)
                last.then_inc(scored, 1)

            def s_keys(i):
                pe.wait_ge(q_ready, i + 1)
                if not first(i):
                    pe.wait_ge(st_copied_v, i * 2)
                    pe.wait_ge(st_copied_a, i)
                for s in range(STEPS + 1):
                    if s < STEPS:
                        s_turn(i, s)
                    if s >= 1:
                        s_score(i, s - 1)
                if not first(i):
                    pe.wait_ge(m_ready, i)
                own = ps[0:NEW, 7, 0:P].rearrange("r (b k c) -> r b k c", b=2, c=8)
                for k in range(8):
                    last = mm(own[:, :, k, :], qkvT[:, 12 * (k // 4) + 4 + k % 4, SEQ:TOK], Qcur[:, k, :, :],
                              start=True, stop=True)
                last.then_inc(scored, 1)

            def s_rows(i):
                pe.wait_ge(st_copied_v, i * 2 + 2)
                pe.wait_ge(st_copied_a, i + 1)
                for g in range(NPG):
                    turn(ps[:, 4 + g // 4, P * (g % 4):P * (g % 4) + P], STs[:, g, :], ident)
                turn(ps[:, 7, P:P + NEW], STo[0:NEW, :], ident[0:NEW, 0:NEW]).then_inc(rows_ready, 1)

            def s_probs_turn(i, later=4):
                pe.wait_ge(s_probs, i + 1)
                for g in range(NPG):
                    turn(ps[:, 4 + g // 4, P * (g % 4):P * (g % 4) + P], Sb[:, g * P:g * P + P], ident)
                pe.wait_ge(st_copied_v, i * 2 + later)
                turn(ps[0:NEW, 7, 160:288], Sb[:, OWN:KEYS], ident).then_inc(pt_ready, 1)

            def s_values(i):
                pe.wait_ge(pt_copied_v, i * 2 + 2)
                pe.wait_ge(pt_copied_a, i + 1)
                for n in range(4):
                    b2, kind = divmod(n, 2)
                    pe.wait_ge(v_in[kind], i * 256 + P * (b2 + 1))
                    for p in range(4):
                        row = 64 * b2 + 32 * kind + 8 * p
                        for g in range(NPG):
                            mm(ps[:, 6, row:row + 8], vring[:, kind, g, p * P:p * P + P], PTs[:, g, row:row + 8],
                               start=(g == 0), stop=False)
                        last = mm(ps[:, 6, row:row + 8], vnat[0:NEW, 2, kind, p * P:p * P + P],
                                  PTo[0:NEW, row:row + 8], start=False, stop=True)
                    last.then_inc(v_used, 1)

            pe.wait_ge(p_taken, 8)
            s_keys(0)
            s_rows(0)
            with pe.Fori(1, PAIRS) as i:
                s_keys(i)
                s_probs_turn(i - 1)
                s_values(i - 1)
                s_rows(i)
            s_probs_turn(PAIRS - 1, 2)
            s_values(PAIRS - 1)

            with pe.Fori(0, 2) as i:
                for s in range(2):
                    pe.wait_ge(w_in[s], i * 16 + 16 * 4)
                    for q in range(4):
                        pe.wait_ge(in_taken, i * 8 + (T_GATE + 4 * s + q + 1))
                        tile(q, [slot8(s)[:, k, q * P:q * P + P] for k in range(DT)], h).then_inc(tile_ready, 1)
            pe.wait_ge(d_squared, 1)
            for n in range(4):
                last = mm(ps[:, 4 + n, 0:TOK], ones[:, :], dsq[:, n, :], start=True, stop=True)
            last.then_inc(d_summed, 1)

            pe.wait_ge(in_taken, 4 + T_OA)
            for kind, n in ((0, OA), (1, OB)):
                if kind == 1:
                    pe.wait_ge(d_done, 1)
                pe.wait_ge(w_in[n % 2], 16 * (n // 2 + 1))
                for m in range(DT):
                    if 8 * kind + m >= 4:
                        pe.wait_ge(mix_taken, 8 * kind + m - 3)
                    tile(m % 4, [slot4(n % 2)[:, k, m * P:m * P + P] for k in range(4)],
                         [oT[:, 4 * kind + k, :] for k in range(4)]).then_inc(tile_ready, 1)
            pe.wait_ge(mix_taken, 16)
            for m in range(DT):
                n = OUT0 + m // 4
                if m % 4 == 0:
                    pe.wait_ge(w_in[n % 2], 16 * (n // 2 + 1))
                pe.wait_ge(mix_taken, 16 + max(m - 3, 0))
                tile(m % 4, [slot8(n % 2)[:, k, (m % 4) * P:(m % 4) * P + P] for k in range(DT)],
                     [mT[:, k, :] for k in range(DT)]).then_inc(tile_ready, 1)
            sum_of_squares(1)

            def state_turn(c, par):
                pe.wait_ge(ends_packed, c + 1)
                if not first(c):
                    pe.wait_ge(c_staged, c)
                for q in range(4):
                    last = turn(ps[0:18, 5, q * P:q * P + P], ends[:, par, q, :], ident)
                last.then_inc(c_turned, 1)

            def up(c, par):
                pe.wait_ge(f_in[par], so_far(c, par, 96))
                if not first(c):
                    pe.wait_ge(f_copied, c)
                for q in range(4):
                    last = mm(ps[:, 4, 20 * q:20 * q + 20], frow[0:20, par, q * P:q * P + P], ident[0:20, 0:20],
                              start=True, stop=True)
                last.then_inc(f_turned, 1)
                pe.wait_ge(w_in[par], 16 * (UP0 // 2) + so_far(c, par, 32))
                for q in range(4):
                    if not first(c):
                        pe.wait_ge(ext_ready, c * 8 + 2 * (q - 3))
                    tile(q, [slot_up(par, q // 2)[:, k, (q % 2) * P:(q % 2) * P + P] for k in range(DT)], h
                         ).then_inc(tile_ready, 1)

            pe.wait_ge(mix_taken, 24)
            pe.wait_ge(normed, 2 * DT)
            up(0, 0)
            up(1, 1)
            state_turn(0, 0)
            up(2, 0)
            state_turn(1, 1)
            with pe.Fori(1, 5) as i:
                up(2 * i + 1, 1)
                state_turn(2 * i, 0)
                up(2 * i + 2, 0)
                state_turn(2 * i + 1, 1)
            state_turn(10, 0)

            pe.wait_ge(ff_done, 22)
            with pe.Fori(0, 2) as i:
                for e in range(2):
                    for half in range(2):
                        s = (DOWN0 + half) % 2
                        pe.wait_ge(w_in[s], i * 32 + (16 * (UP0 // 2) + 32 * (5 + half) + 16 * (e + 1)))
                        for q in range(2):
                            if half == 0:
                                pe.wait_ge(down_taken, i * 4 + (2 * e + q + 1))
                            last = tile(2 * e + q, [slot11(s)[:, k, q * P:q * P + P] for k in range(11)],
                                        [ffT[:, 11 * half + k, :] for k in range(11)], half == 0, half == 1)
                            if half == 1:
                                last.then_inc(tile_ready, 1)
                        if half == 0:
                            last.then_inc(half_used, 1)
            sum_of_squares(2)

            pe.wait_ge(normed, 3 * DT)
            for g in range(6):
                n, half = divmod(g, 2)
                t0, cnt = TOKENS[n]
                if g >= 4:
                    pe.wait_ge((y_copied_a, y_copied_v)[half], n - 1)
                for q in range(4):
                    last = turn(ps[0:cnt, g % 4, q * P:q * P + P], hT[:, 4 * half + q, t0:t0 + cnt], ident)
                last.then_inc(y_turned, 1)

        @block.scalar
        def _(act):
            fn, copy = nc.scalar.activation, nc.scalar.copy

            def load(s, dst, src):
                act.dma_start(dst, src).then_inc(w_in[s], 16)

            def load_up(c, par):
                for hlf in range(2):
                    src = w_up_v[:, :, hlf, :][:, :, bass.ds(c * 256, 256)]
                    act.dma_start(slot_up(par, hlf), src).then_inc(w_in[par], 16)

            def root(use):
                act.wait_ge(meaned, use + 1)
                fn(rr[:, :], rr[:, :], ACT.Sqrt).then_inc(rooted, 1)

            load(0, slot8(0), w_in_v[:, :, 0:512])
            load(1, slot8(1), w_in_v[:, :, 512:1024])
            for j in range(DT):
                act.wait_ge(x_turned, j + 1)
                fn(hT[:, j, :], ps[:, j % 4, 0:TOK], ACT.Square).then_inc(squared, 1)
                copy(xT[:, j, :], ps[:, j % 4, 0:TOK]).then_inc(x_copied, 1)
            act.wait_ge(lam_summed, 2)
            fn(small[:, 10:12], small[:, 8:10], ACT.Exp).then_inc(lam_exped, 1)
            root(0)
            act.sem_inc(in_taken, 4)

            def take_in(n, dst0):
                for q in range(4):
                    act.wait_ge(tile_ready, n * 4 + q + 1)
                    copy(qkvT[:, bass.ds(n * 4 + q, 1), :].rearrange("p o t -> p (o t)"), ps[:, q, 0:TOK]
                         ).then_inc(in_taken, 1)

            with act.Fori(0, 2) as i:
                for s in range(2):
                    take_in(2 * i + s, 0)
                    load(s, slot8(s), w_in_v[:, :, bass.ds((2 * i + s + 2) * 512, 512)])
            for n in (4, 5):
                take_in(n, 0)
                load(n % 2, slot8(n % 2), w_gate_v[:, :, (n - 4) * 512:(n - 3) * 512])

            def p_exp(u):
                act.wait_ge(p_biased, 2 * u + 2)
                act.wait_ge(vec_p, u + 1)
                fn(pS[:, u % 4, 0:256], pS[:, u % 4, 0:256], ACT.Exp, bias=pstat[:, u, 2:3],
                   accum_out=pstat[:, u, 4:5]).then_inc(p_exped, 1)
                fn(pS[:, u % 4, 256:384], pS[:, u % 4, 256:384], ACT.Exp, bias=pstat[:, u, 3:4],
                   accum_out=pstat[:, u, 5:6]).then_inc(p_exped, 1)

            def p_copy(v):
                act.wait_ge(p_turned, v + 1)
                if v >= 2:
                    act.wait_ge(p_mixed, v - 1)
                copy(pPT[:, v % 2, :], ps[:, 3 + v % 2, 0:GW]).then_inc(p_pt, 1)

            for u in range(16 + 2):
                if u < 16:
                    p_exp(u)
                if u - 2 in RESULT:
                    p_copy(RESULT.index(u - 2))

            def s_copy_k(i):
                for s in range(STEPS):
                    act.wait_ge(k_turned, i * 2 * STEPS + 2 * s + 1)
                    if not (first(i) and s < 2):
                        act.wait_ge(scored, page_used(i, s))
                    copy(kTs[:, s % 2, 0, :], ps[:, 0, :]).then_inc(k_copied[0], 1)

            def s_exp(i):
                act.wait_ge(m_ready, i + 1)
                for n in range(NBLK + 1):
                    cols = slice(n * BLOCK, min(n * BLOCK + BLOCK, KEYS))
                    fn(Sb[:, cols], Sb[:, cols], ACT.Exp, bias=sst[:, 32 + n:33 + n],
                       accum_out=sst[:, 40 + n:41 + n]).then_inc(s_exped, 1)

            def s_copy_st(i):
                act.wait_ge(scored, i * 17 + 17)
                copy(STs[:, 4:8, :].rearrange("p g r -> p (g r)"), ps[:, 3, :]).then_inc(st_copied_a, 1)

            def s_copy_pt(i):
                act.wait_ge(pt_ready, i + 1)
                copy(PTs[:, 4:8, :].rearrange("p g r -> p (g r)"), ps[:, 5, :]).then_inc(pt_copied_a, 1)

            act.wait_ge(k_out, 16 * 6)
            s_copy_k(0)
            s_copy_st(0)
            with act.Fori(1, PAIRS) as i:
                s_exp(i - 1)
                s_copy_k(i)
                s_copy_st(i)
                s_copy_pt(i - 1)
            s_exp(PAIRS - 1)
            s_copy_pt(PAIRS - 1)

            act.wait_ge(o_taken, 4 * PAIRS)
            fn(dsq[:, :, :], oT[:, 4:8, :], ACT.Square).then_inc(d_squared, 1)
            for n in range(GATE0, GATE0 + 4):
                for q in range(4):
                    m = 4 * (n - GATE0) + q
                    act.wait_ge(tile_ready, T_GATE + m + 1)
                    fn(gT[:, m, :], ps[:, q, 0:TOK], ACT.Sigmoid).then_inc(in_taken, 1)
                s = n % 2
                if n == GATE0:
                    load(s, slot8(s), w_gate_v[:, :, 1024:1536])
                elif n == GATE0 + 1:
                    load(s, slot8(s), w_gate_v[:, :, 1536:2048])
                elif n == GATE0 + 2:
                    load(s, slot4(s), w_oa_v)
                else:
                    load(s, slot4(s), w_ob_v)
            act.wait_ge(d_meaned, 1)
            fn(drr[:, :, :], drr[:, :, :], ACT.Sqrt).then_inc(d_rooted, 1)
            act.wait_ge(tile_ready, T_OB)
            load(0, slot8(0), w_out_v[:, :, 0:512])
            act.wait_ge(tile_ready, T_OUT)
            load(1, slot8(1), w_out_v[:, :, 512:1024])
            act.wait_ge(tile_ready, T_OUT + 4)
            load_up(0, 0)
            for j in range(DT):
                act.wait_ge(mix_taken, 16 + j + 1)
                fn(hT[:, j, :], xT[:, j, :], ACT.Square).then_inc(squared, 1)
            load_up(1, 1)
            root(1)

            def take_up(c, par):
                for q in range(4):
                    act.wait_ge(tile_ready, c * 4 + T_UP + q + 1)
                    if q == 0 and not early(c):
                        act.wait_ge(conv_done, (c - 1) * 4)
                    e = ext[:, 4 * par + q, :]
                    copy(e[:, 2:258], ps[:, q, 0:SEQ]).then_inc(ext_ready, 1)
                    copy(e[:, 258:306].rearrange("p (b r) -> p b r", r=6)[:, :, 2:6],
                         ps[:, q, SEQ:TOK].rearrange("p (b t) -> p b t", t=T)).then_inc(ext_ready, 1)

            def silu(c):
                act.wait_ge(conv_done, c * 4 + 4)
                fn(cv[:, 0:2, 0:CONV], cv[:, 0:2, 0:CONV], ACT.Silu).then_inc(silu_done, 1)

            act.wait_ge(edges_set, 1)
            for c in range(3):
                take_up(c, c % 2)
                load_up(c + 2, c % 2)
                silu(c)
            with act.Fori(1, 4) as i:
                for c, par in ((2 * i + 1, 1), (2 * i + 2, 0)):
                    take_up(c, par)
                    load_up(c + 2, par)
                    silu(c)
            for c, par in ((9, 1), (10, 0)):
                take_up(c, par)
                load(par, slot11(par), w_down_v[:, 11 * (c - 9):11 * (c - 9) + 11, 0:256])
                silu(c)
            with act.Fori(0, 3) as d:
                for half, s in ((0, 1), (1, 0)):
                    if half == 0:
                        act.wait_ge(half_used, d + 1)
                    else:
                        act.wait_ge(tile_ready, d * 2 + T_DOWN + 2)
                    load(s, slot11(s), w_down_v[:, 11 * half:11 * half + 11, bass.ds((d + 1) * 256, 256)])
            for j in range(DT):
                act.wait_ge(down_taken, 4 + j + 1)
                fn(hT[:, j, :], xT[:, j, :], ACT.Square).then_inc(squared, 1)
            root(2)
            for n, (t0, cnt) in enumerate(TOKENS):
                act.wait_ge(y_turned, 2 * n + 1)
                copy(ynat[0:cnt, n, 0:512], ps[0:cnt, 2 * n % 4, :]).then_inc(y_copied_a, 1)

        @block.vector
        def _(dve):
            v = nc.vector

            def own(ins):
                vec_own.add(ins)
                vec_own.wait(dve)

            v.memset(relm[BUCKETS:BUCKETS + 1, :], MASKED).then_inc(mask_set, 1)
            dve.wait_ge(set_pe, 1)
            v.tensor_copy(gcol[:, :, :], ps[:, 4, 0:32].rearrange("p (j c) -> p j c", c=4)[:, :, 0:3]).then_inc(set_up, 1)
            dve.wait_ge(set_pe, 2)
            v.tensor_copy(Gsb, ps[0:HEADS, 5, 0:GW]).then_inc(set_up, 1)
            W6 = Wrel.rearrange("p (b k q r) -> p b k q r", b=2, k=2, q=4)
            M6 = con[:, C_TM:C_TM + P].rearrange("p (b k q r) -> p b k q r", b=2, k=2, q=4)
            for b in range(2):
                v.tensor_tensor(W6[:, b, 0].rearrange("p q (h t) -> p (q h) t", t=T),
                                relb[:, 0:8].unsqueeze(2).broadcast_to([P, 8, T]),
                                M6[:, b, 0].rearrange("p q (h t) -> p (q h) t", t=T), ALU.mult).then_inc(set_up, 1)
                v.tensor_tensor(W6[:, b, 1], relb[:, 8:12].unsqueeze(2).broadcast_to([P, 4, 8]),
                                M6[:, b, 1], ALU.mult).then_inc(set_up, 1)
            for n in range(2):
                v.tensor_tensor_reduce(lamv[:, 2 * n, :], lamv[:, 2 * n, :], lamv[:, 2 * n + 1, :], 1.0, 0.0,
                                       ALU.mult, ALU.add, small[:, 8 + n:9 + n]).then_inc(lam_summed, 1)
            v.tensor_scalar(dgain, small[:, 4:5], 1.0 - LAM0, None, ALU.mult).then_inc(set_up, 1)
            dve.wait_ge(set_pe, 3)
            v.tensor_copy(ownb, ps[:, 6, 129:161]).then_inc(set_up, 1)
            v.tensor_copy(bias_s[:, PAST - PAGE:PAST], ps[:, 6, 1:129]).then_inc(set_up, 1)
            own(v.tensor_copy(far, ps[:, 6, 0:1]))
            v.tensor_copy(bias_s[:, 0:PAST - PAGE], far.broadcast_to([P, PAST - PAGE])).then_inc(set_up, 1)
            dve.wait_ge(lam_exped, 1)
            own(v.tensor_tensor(small[:, 12:13], small[:, 11:12], small[:, 10:11], ALU.subtract))
            own(v.tensor_scalar(neglam, small[:, 12:13], -LAM0, None, ALU.add))
            own(v.scalar_tensor_tensor(out=rweight, in0=con[:, C_VEC + 1:C_VEC + 2], scalar=neglam,
                                       in1=con[:, C_VEC:C_VEC + 1], op0=ALU.mult, op1=ALU.add))

            def normalise(use):
                dve.wait_ge(summed, use + 1)
                v.tensor_scalar(rr[:, :], ps[:, 7, 0:TOK], 1.0 / D, EPS, ALU.mult, ALU.add).then_inc(meaned, 1)
                dve.wait_ge(rooted, use + 1)
                own(v.reciprocal(rr[:, :], rr[:, :]))
                for j in range(DT):
                    v.scalar_tensor_tensor(out=hT[:, j, :], in0=xT[:, j, :], scalar=gcol[:, j, use:use + 1],
                                           in1=rr[:, :], op0=ALU.mult, op1=ALU.mult).then_inc(normed, 1)

            dve.wait_ge(x_copied, DT)
            normalise(0)
            for g in range(12):
                kind, tt = divmod(g, 3)
                cnt = TOKENS[tt][1]
                dve.wait_ge(nat_ready, g + 1)
                v.tensor_copy((knat if kind < 2 else vnat)[0:cnt, tt, kind % 2, :], ps[0:cnt, 4 + g % 2, :]
                              ).then_inc(nat_taken, 1)
            for m0 in (0, 12):
                v.tensor_scalar(qkvT[:, m0:m0 + 4, :], qkvT[:, m0:m0 + 4, :], SCALE, None, ALU.mult
                                ).then_inc(q_scaled, 1)
            dve.wait_ge(q_scaled, 2)
            dve.wait_ge(consts_set, 3)
            for kind in range(2):
                for hh in range(2):
                    rows = slice(64 * hh, 64 * hh + 64)
                    own(v.tensor_copy(Qbd[rows, 4 * kind:4 * kind + 4, 0:DB, 4 * hh:4 * hh + 4],
                                      qkvT[rows, 12 * kind:12 * kind + 4, SEQ:TOK].rearrange(
                                          "p q (b t) -> p q b t", t=T)))
            v.tensor_copy(Qcur[:, :, :, :], Qbd[:, :, 0:2, :]).then_inc(q_ready, 1)

            def p_bias(u):
                head = u if u < 8 else 8 + (u - 8) // 2
                dve.wait_ge(p_scores, u + 1)
                if u >= 4:
                    done = sum(c <= u - 4 for c in RESULT)
                    if done:
                        dve.wait_ge(p_turned, done)
                for n, cols in enumerate((slice(0, 256), slice(256, 384))):
                    v.tensor_tensor_reduce(pS[:, u % 4, cols], ps[:, u % 3, cols], pbias[:, head, cols], 1.0, LOWEST,
                                           ALU.add, ALU.max, pstat[:, u, n:n + 1]).then_inc(p_biased, 1)
                dve.wait_ge(p_biased, 2 * u + 2)
                v.tensor_scalar(pstat[:, u, 2:4], pstat[:, u, 0:2], -1.0, None, ALU.mult).then_inc(vec_p, 1)

            def p_norm(u):
                dve.wait_ge(p_exped, 2 * u + 2)
                own(v.reciprocal(pstat[:, u, 6:8], pstat[:, u, 4:6]))
                second = u >= 8 and u % 2 == 1
                if second:
                    own(v.tensor_scalar(pstat[:, u, 6:8], pstat[:, u, 6:8], neglam, None, ALU.mult))
                for n, cols in enumerate((slice(0, 256), slice(256, 384))):
                    x, r = pS[:, u % 4, cols], pstat[:, u, 6 + n:7 + n]
                    if second:
                        v.scalar_tensor_tensor(out=x, in0=x, scalar=r, in1=pS[:, (u - 1) % 4, cols],
                                               op0=ALU.mult, op1=ALU.add).then_inc(p_probs, 1)
                    elif u >= 8:
                        own(v.tensor_scalar(x, x, r, None, ALU.mult))
                    else:
                        v.tensor_scalar(x, x, r, None, ALU.mult).then_inc(p_probs, 1)

            def p_take(o):
                dve.wait_ge(p_mixed, 2 * o + 2 if o < 4 else o + 5)
                v.tensor_copy(oT[:, o, 0:SEQ], ps[:, 5 + o % 2, 0:SEQ]).then_inc(p_taken, 1)

            dve.wait_ge(bias_in, 32)
            taken = 0
            for u in range(16 + 4):
                if u < 16:
                    p_bias(u)
                if 1 <= u < 17:
                    p_norm(u - 1)
                if u - 4 in RESULT:
                    r = RESULT.index(u - 4)
                    if r >= 8 or r % 2 == 1:
                        p_take(taken)
                        taken += 1

            def s_copy_k(i):
                for s in range(STEPS):
                    dve.wait_ge(k_turned, i * 2 * STEPS + 2 * s + 2)
                    if not (first(i) and s < 2):
                        dve.wait_ge(scored, page_used(i, s))
                    v.tensor_copy(kTs[:, s % 2, 1, :], ps[:, 1, :]).then_inc(k_copied[1], 1)

            def s_copy_st(i):
                dve.wait_ge(scored, i * 17 + 17)
                v.tensor_copy(STs[:, 0:4, :].rearrange("p g r -> p (g r)"), ps[:, 2, :]).then_inc(st_copied_v, 1)
                v.tensor_copy(STo[0:NEW, :], ps[0:NEW, 7, 0:P]).then_inc(st_copied_v, 1)
                v.tensor_tensor(bias_s[:, OWN:KEYS], ownb, con[:, bass.ds(i * NEW + C_MASK, NEW)], ALU.add
                                ).then_inc(own_biased, 1)

            def next_queries(i):
                v.tensor_copy(Qcur[:, :, :, :], Qbd[:, :, bass.ds(i * 2 + 2, 2), :]).then_inc(q_ready, 1)

            def s_copy_pt(i):
                dve.wait_ge(pt_ready, i + 1)
                v.tensor_copy(PTs[:, 0:4, :].rearrange("p g r -> p (g r)"), ps[:, 4, :]).then_inc(pt_copied_v, 1)
                v.tensor_copy(PTo[0:NEW, :], ps[0:NEW, 7, 160:288]).then_inc(pt_copied_v, 1)

            def s_take(i):
                dve.wait_ge(v_used, i * 4 + 4)
                O = ps[:, 6, 0:P].rearrange("p (b k q h t) -> p k h q b t", b=2, k=2, q=4, h=2)
                dst = oT[:, :, bass.ds(i * 8 + SEQ, 8)].rearrange("p q (b t) -> p q b t", t=T)
                for hh in range(2):
                    rows = slice(64 * hh, 64 * hh + 64)
                    v.tensor_copy(dst[rows, 0:4], O[rows, 0, hh]).then_inc(o_taken, 1)
                v.tensor_copy(dst[:, 4:8], O[:, 1, 0]).then_inc(o_taken, 1)
                dve.wait_ge(o_taken, i * 4 + 3)
                v.tensor_tensor(dst[:, 4:8], dst[:, 4:8], O[:, 1, 1], ALU.add).then_inc(o_taken, 1)

            def s_softmax(i):
                dve.wait_ge(rows_ready, i + 1)
                dve.wait_ge(own_biased, i + 1)
                vec_own.add(v.tensor_reduce(sst[:, 0:NBLK], ps[:, 4:6, :].rearrange("p a (n k) -> p (a n) k", k=BLOCK),
                                            AX.X, ALU.add))
                for n in range(NBLK):
                    cols = slice(n * BLOCK, n * BLOCK + BLOCK)
                    vec_own.add(v.tensor_tensor_reduce(Sb[:, cols], ps[:, 4 + n // 2, (n % 2) * BLOCK:(n % 2) * BLOCK + BLOCK],
                                                       bias_s[:, cols], 1.0, LOWEST, ALU.add, ALU.max, sst[:, 4 + n:5 + n]))
                vec_own.add(v.tensor_tensor_reduce(Sb[:, OWN:KEYS], ps[:, 7, P:P + NEW], bias_s[:, OWN:KEYS], 1.0, LOWEST,
                                                   ALU.add, ALU.max, sst[:, 28:29]))
                vec_own.wait(dve)
                own(v.tensor_reduce(sst[:, 9:10], sst[:, 0:NBLK], AX.X, ALU.min))
                own(v.scalar_tensor_tensor(out=sst[:, 10:14], in0=sst[:, 0:NBLK], scalar=sst[:, 9:10],
                                           in1=con[:, C_VEC + 3:C_VEC + 7], op0=ALU.is_equal, op1=ALU.mult))
                own(v.tensor_reduce(sst[:, 14:15], sst[:, 10:14], AX.X, ALU.max))
                own(v.tensor_scalar(sst[:, 16:20], sst[:, 10:14], sst[:, 14:15], con[:, C_VEC + 2:C_VEC + 3],
                                    ALU.is_equal, ALU.mult))
                own(v.tensor_tensor(sst[:, 24:28], sst[:, 4:8], sst[:, 16:20], ALU.add))
                own(v.tensor_reduce(sst[:, 29:30], sst[:, 24:29], AX.X, ALU.max))
                v.tensor_scalar(sst[:, 32:37], sst[:, 16:21], sst[:, 29:30], None, ALU.subtract).then_inc(m_ready, 1)
                dve.wait_ge(s_exped, i * 5 + 5)
                own(v.tensor_reduce(sst[:, 46:47], sst[:, 40:45], AX.X, ALU.add))
                own(v.reciprocal(sst[:, 47:48], sst[:, 46:47]))
                own(v.tensor_tensor(sst[:, 48:49], sst[:, 47:48], rweight, ALU.mult))
                v.tensor_scalar(Sb[:, :], Sb[:, :], sst[:, 48:49], None, ALU.mult).then_inc(s_probs, 1)

            dve.wait_ge(k_out, 16 * 6)
            s_copy_k(0)
            s_copy_st(0)
            next_queries(0)
            s_softmax(0)
            with dve.Fori(1, PAIRS) as i:
                vec_own.enter(i, 1, 15)
                s_copy_k(i)
                s_copy_st(i)
                next_queries(i)
                s_copy_pt(i - 1)
                s_take(i - 1)
                s_softmax(i)
            vec_own.leave(PAIRS - 1)
            s_copy_pt(PAIRS - 1)
            s_take(PAIRS - 1)

            dve.wait_ge(d_summed, 1)
            v.tensor_scalar(drr[:, :, :], ps[:, 4:8, 0:TOK], 1.0 / P, EPS, ALU.mult, ALU.add).then_inc(d_meaned, 1)
            dve.wait_ge(d_rooted, 1)
            own(v.reciprocal(drr[:, :, :], drr[:, :, :]))
            v.scalar_tensor_tensor(out=oT[:, 4:8, :], in0=oT[:, 4:8, :], scalar=dgain, in1=drr[:, :, :],
                                   op0=ALU.mult, op1=ALU.mult).then_inc(d_done, 1)
            dve.wait_ge(in_taken, 4 + T_OA)
            for m in range(DT):
                dve.wait_ge(tile_ready, T_OA + m + 1)
                v.tensor_tensor(mT[:, m, :], ps[:, m % 4, 0:TOK], gT[:, m, :], ALU.mult).then_inc(mix_taken, 1)
            for m in range(DT):
                dve.wait_ge(tile_ready, T_OB + m + 1)
                own(v.tensor_tensor(ztmp[:, m % 2, :], ps[:, m % 4, 0:TOK], gT[:, DT + m, :], ALU.mult))
                v.tensor_tensor(mT[:, m, :], mT[:, m, :], ztmp[:, m % 2, :], ALU.add).then_inc(mix_taken, 1)
            for m in range(DT):
                dve.wait_ge(tile_ready, T_OUT + m + 1)
                v.tensor_tensor(xT[:, m, :], xT[:, m, :], ps[:, m % 4, 0:TOK], ALU.add).then_inc(mix_taken, 1)
            v.memset(ext[:, :, 0:2], 0.0).then_inc(edges_set, 1)
            dve.wait_ge(mix_taken, 24)
            normalise(1)

            def convolve(c, par):
                dve.wait_ge(f_turned, c + 1)
                v.tensor_copy(fcol[:, :, :], ps[:, 4, 0:80].rearrange("p (m n) -> p m n", n=20)).then_inc(f_copied, 1)
                dve.wait_ge(f_copied, c + 1)
                own(v.tensor_copy(
                    ext[:, 4 * par:4 * par + 4, 258:306].rearrange("p m (b r) -> p m b r", r=6)[:, :, :, 0:2],
                    fcol[:, :, 0:16].rearrange("p m (b r) -> p m b r", r=2)))
                for q in range(4):
                    dve.wait_ge(ext_ready, c * 8 + 2 * q + 2)
                    vec_own.add(v.tensor_scalar(cv[:, q, 0:CONV], ext[:, 4 * par + q, 0:CONV], fcol[:, q, 16:17],
                                                fcol[:, q, 19:20], ALU.mult, ALU.add))
                vec_own.wait(dve)
                for q in range(4):
                    vec_own.add(v.scalar_tensor_tensor(out=cv[:, q, 0:CONV], in0=ext[:, 4 * par + q, 1:1 + CONV],
                                                       scalar=fcol[:, q, 17:18], in1=cv[:, q, 0:CONV],
                                                       op0=ALU.mult, op1=ALU.add))
                if not early(c):
                    dve.wait_ge(c_turned, c - 1)
                v.tensor_copy(ends[:, par].rearrange("p q (s r) -> p q s r", r=2),
                              ext[:, 4 * par:4 * par + 4, 256:310].rearrange("p q (s r) -> p q s r", r=6)[:, :, :, 0:2]
                              ).then_inc(ends_packed, 1)
                vec_own.wait(dve)
                for q in range(4):
                    v.scalar_tensor_tensor(out=cv[:, q, 0:CONV], in0=ext[:, 4 * par + q, 2:2 + CONV],
                                           scalar=fcol[:, q, 18:19], in1=cv[:, q, 0:CONV],
                                           op0=ALU.mult, op1=ALU.add).then_inc(conv_done, 1)
                dve.wait_ge(conv_done, c * 4 + 4)
                dve.wait_ge(silu_done, c + 1)
                v.tensor_tensor(ffT[:, bass.ds(c * 2, 2), 0:SEQ], cv[:, 0:2, 0:SEQ], cv[:, 2:4, 0:SEQ], ALU.mult
                                ).then_inc(ff_done, 1)
                new = cv[:, :, 258:306].rearrange("p m (b r) -> p m b r", r=6)[:, :, :, 0:T]
                v.tensor_tensor(ffT[:, bass.ds(c * 2, 2), SEQ:TOK].rearrange("p m (b t) -> p m b t", t=T),
                                new[:, 0:2], new[:, 2:4], ALU.mult).then_inc(ff_done, 1)

            def stage_state(c, par):
                dve.wait_ge(c_turned, c + 1)
                if not early(c):
                    dve.wait_ge(cst_out[par], so_far(c, par, 64) - 64)
                v.tensor_copy(cst[0:18, par, :], ps[0:18, 5, :]).then_inc(c_staged, 1)

            convolve(0, 0)
            convolve(1, 1)
            stage_state(0, 0)
            convolve(2, 0)
            stage_state(1, 1)
            with dve.Fori(1, 5) as i:
                vec_own.enter(i, 1, 18)
                convolve(2 * i + 1, 1)
                stage_state(2 * i, 0)
                convolve(2 * i + 2, 0)
                stage_state(2 * i + 1, 1)
            vec_own.leave(4)
            stage_state(10, 0)
            dve.sem_inc(down_taken, 4)
            for m in range(DT):
                dve.wait_ge(tile_ready, T_DOWN + m + 1)
                v.tensor_tensor(xT[:, m, :], xT[:, m, :], ps[:, m % 4, 0:TOK], ALU.add).then_inc(down_taken, 1)
            dve.wait_ge(down_taken, 4 + DT)
            normalise(2)
            for n, (t0, cnt) in enumerate(TOKENS):
                dve.wait_ge(y_turned, 2 * n + 2)
                v.tensor_copy(ynat[0:cnt, n, 512:1024], ps[0:cnt, (2 * n + 1) % 4, :]).then_inc(y_copied_v, 1)


_INS = ["x_prompt", "x_sample", "cache_moba_k", "cache_moba_v", "cache_diff_k", "cache_diff_v", "state_conv",
        "page_table", "rel_bias", "norm_attn", "w_in", "w_gate", "w_out_a", "w_out_b", "w_out",
        "lambda_q1", "lambda_k1", "lambda_q2", "lambda_k2", "diff_norm", "norm_ffn", "w_up", "conv_w", "conv_b",
        "w_down", "norm_final"]
_OUTS = [("y_prompt", (1, SEQ, D)), ("y_sample", (DB, T, D)),
         ("moba_k_prompt", (1, 1, SEQ, 8, HD)), ("moba_v_prompt", (1, 1, SEQ, 8, HD)),
         ("diff_k_prompt", (1, 1, SEQ, 4, 2 * HD)), ("diff_v_prompt", (1, 1, SEQ, 4, 2 * HD)),
         ("conv_prompt", (1, 1, 2, 2 * FF)),
         ("moba_k_sample", (1, DB, T, 8, HD)), ("moba_v_sample", (1, DB, T, 8, HD)),
         ("diff_k_sample", (1, DB, T, 4, 2 * HD)), ("diff_v_sample", (1, DB, T, 4, 2 * HD)),
         ("conv_sample", (1, DB, 2, 2 * FF))]


def kernel(**inputs):
    import concourse.bacc as _bacc
    from concourse.bass_utils import run_bass_kernel_spmd as _run

    nc = _bacc.Bacc("TRN2", target_bir_lowering=False, num_devices=1)
    arrays, ins, outs = {}, {}, {}
    given = {name: np.ascontiguousarray(inputs[name]) for name in _INS}
    given["constants"] = constants()
    for name, x in given.items():
        arrays[f"in_{name}"] = x
        ins[name] = nc.dram_tensor(f"in_{name}", x.shape, mybir.dt.from_np(x.dtype), kind="ExternalInput").ap()
    for name, shape in _OUTS:
        outs[name] = nc.dram_tensor(f"out_{name}", shape, F32, kind="ExternalOutput").ap()
    build(nc, ins, outs)
    r = _run(nc, [arrays], core_ids=[0])
    return tuple(r.results[0][f"out_{name}"] for name, _ in _OUTS)
```

```python
import math
from contextlib import ExitStack

import numpy as np
import concourse.bass as bass
from concourse import mybir

F32 = mybir.dt.float32
I32 = mybir.dt.int32
ALU = mybir.AluOpType
ACT = mybir.ActivationFunctionType
AX = mybir.AxisListType

P = 128
D = 1024
DT = D // P
SEQ = 256
DB, T = 8, 4
NEW = DB * T
TOK = SEQ + NEW
PAST, PAGE = 1024, 128
NPG = PAST // PAGE
NPHYS = DB * NPG + DB * NPG // 4
BLOCK = 256
NBLK = PAST // BLOCK
HD = 64
WID = 512
N_IN = 6 * WID
FF = 2816
FT = FF // P
BUCKETS, HEADS = 32, 12
EPS = 1e-6
LAM0 = 0.8 - 0.6 * math.exp(0.0)
SCALE = HD ** -0.5
MASKED = -1.0e30
LOWEST = -3.0e38

TOKENS = [(0, P), (P, P), (SEQ, NEW)]
LAST = DB - 1
QUADS = 4
ROWS = 8 * T
HALF = NPG * 32
LINE = HALF + NEW
RESULT = [0, 1, 2, 3, 4, 5, 6, 7, 9, 11, 13, 15]
SET_UP = 11
EXT = 310
CONV = 304
GW = 384

C_ID, C_TM, C_HOT, C_MASK, C_G, C_SUM, C_VEC = 0, 128, 256, 417, 673, 1057, 1185
C_ALL = 1192


def bucket(n):
    n = max(int(n), 0)
    if n < BUCKETS // 2:
        return n
    large = 16 + int(np.float32(np.log(np.float32(n) / np.float32(16))) / np.float32(math.log(8.0)) * np.float32(16))
    return min(large, BUCKETS - 1)


def constants():
    c = np.zeros((P, C_ALL), np.float32)
    c[:, C_ID:C_ID + P] = np.eye(P)
    rows = np.arange(P)
    for part in range(P):
        t, b = divmod(part, BUCKETS)
        c[part, C_TM:C_TM + P] = rows % T == t
        hot = [bucket(PAST)] + [bucket(PAST + t - k) for k in range(PAST - PAGE, PAST)]
        hot += [bucket(t - k % T) for k in range(NEW)]
        c[part, C_HOT:C_HOT + 161] = np.array(hot) == b
    for r in range(ROWS):
        for b in range(DB):
            for k in range(NEW):
                c[r, C_MASK + NEW * b + k] = 0.0 if k // T == b and k % T <= r % T else MASKED
    for m in range(GW):
        n = 2 * P - 1 - m
        c[bucket(n) if n >= 0 else BUCKETS, C_G + m] = 1.0
    c[:, C_SUM:C_SUM + P] = rows[:, None] % ROWS == rows[None, :] % ROWS
    second = (rows // ROWS == 1) & (rows // T % 2 == 1)
    c[:, C_VEC] = ~second
    c[:, C_VEC + 1] = second
    c[:, C_VEC + 3:C_VEC + 7] = np.arange(1, NBLK + 1)
    return c


def so_far(c, par, per):
    return (c + par) * (per // 2) + (0 if par else per)


def first(i):
    return isinstance(i, int) and i == 0


def early(c):
    return isinstance(c, int) and c < 2


class Tally:

    def __init__(self, sem):
        self.sem, self.n, self.base = sem, 0, 0

    def add(self, ins):
        ins.then_inc(self.sem, 1)
        self.n += 1

    def wait(self, eng):
        eng.wait_ge(self.sem, self.base + self.n)

    def enter(self, i, first, per):
        self.start, self.per = self.n, per
        self.base, self.n = (i - first) * per + self.n, 0

    def leave(self, times):
        assert self.n == self.per, (self.n, self.per)
        self.base, self.n = 0, self.start + times * self.per


def build(nc, a, out):
    with ExitStack() as ctx:
        def sb(name, shape, dt=F32):
            return ctx.enter_context(nc.sbuf_tensor(name, shape, dt))

        def sem(name):
            return ctx.enter_context(nc.semaphore(name))

        ps = ctx.enter_context(nc.psum_tensor("ps", [P, 8, 512], F32))
        con = sb("con", [P, C_ALL])
        ones = sb("ones", [P, P])
        xT = sb("xT", [P, DT, TOK])
        hT = sb("hT", [P, DT, TOK])
        oT = sb("oT", [P, 8, TOK])
        wbuf = sb("wbuf", [P, 2, 4096])
        arena_q = sb("arena_q", [P, 24 * TOK])
        vnat = sb("vnat", [P, 3, 2, WID])
        arena_v = sb("arena_v", [P, 8192])
        arena_k = sb("arena_k", [P, 8192])
        arena_s = sb("arena_s", [P, 6400])
        bias_s = sb("bias_s", [P, 2, NPG, 32])
        ownS = sb("ownS", [P, DB, 2, NEW])
        qrep = sb("qrep", [P, 2, DB, 16, T])
        stats = sb("stats", [P, 256])
        gcol = sb("gcol", [P, DT, 3])
        vecs = sb("vecs", [4, D])
        relb = sb("relb", [P, HEADS])
        relm = sb("relm", [BUCKETS + 1, HEADS])
        pages = sb("pages", [1, DB * NPG], I32)
        small = sb("small", [P, 64])
        rr = sb("rr", [P, TOK])
        endbuf = sb("endbuf", [P, 2 * 4 * 18])

        ident = con[:, C_ID:C_ID + P]
        hot = con[:, C_HOT:C_HOT + 161]
        qkvT = arena_q[:, :].rearrange("p (m t) -> p m t", t=TOK)
        ffT = arena_q[:, 0:FT * TOK].rearrange("p (m t) -> p m t", t=TOK)
        gT = qkvT
        vals = arena_v[:, :].rearrange("p (k g n) -> p k g n", k=2, n=WID)
        pbias = arena_v[:, 0:HEADS * GW].rearrange("p (h n) -> p h n", n=GW)
        pS = arena_v[:, 4608:4608 + 4 * GW].rearrange("p (u n) -> p u n", n=GW)
        pPT = arena_v[:, 6144:6144 + 2 * GW].rearrange("p (u n) -> p u n", n=GW)
        pstat = arena_v[:, 6912:6912 + 16 * 8].rearrange("p (u n) -> p u n", n=8)
        sel = arena_v[:, 7040:7552].rearrange("p (v n) -> p v n", v=4)
        Qbd = arena_v[:, 7552:8064].rearrange("p (k b c) -> p k b c", k=8, c=8)
        keys = arena_k[:, :].rearrange("p (g n) -> p g n", g=NPG)
        kblocks = arena_k[:, :].rearrange("p (g k c i) -> p g k c i", g=NPG, k=2, i=32)
        mT = arena_k[:, 0:DT * TOK].rearrange("p (m t) -> p m t", t=TOK)
        ext = arena_k[:, 2304:2304 + 8 * EXT].rearrange("p (m t) -> p m t", t=EXT)
        cv = arena_k[:, 4784:4784 + 4 * 306].rearrange("p (m t) -> p m t", t=306)
        frow = arena_k[:, 6016:6016 + 2 * 512].rearrange("p (s n) -> p s n", s=2)
        fcol = arena_k[:, 7040:7040 + 80].rearrange("p (m n) -> p m n", n=20)
        ends = endbuf[:, :].rearrange("p (s q r) -> p s q r", s=2, q=4)
        cst = arena_k[:, 7120:7120 + 1024].rearrange("p (s n) -> p s n", s=2)
        Z = arena_s[:, 0:4160].rearrange("p (k n) -> p k n", k=2)
        S = arena_s[:, 4160:4736].rearrange("p (k n) -> p k n", k=2)
        PT = arena_s[:, 4736:5888].rearrange("p (e k g r) -> p e k g r", e=2, k=2, r=ROWS)
        On = arena_s[0:2 * ROWS, 5888:6400]
        smax = stats[:, 0:10].rearrange("p (k n) -> p k n", k=2)
        blocksum = stats[:, 10:14]
        allsum, pen = stats[:, 14:18], stats[:, 18:22]
        low, order, worst = stats[:, 22:23], stats[:, 23:27], stats[:, 27:28]
        fmax = stats[:, 28:38].rearrange("p (k n) -> p k n", k=2)
        rowmax, negmax = stats[:, 38:40], stats[:, 40:42]
        rowsum = stats[:, 224:228].rearrange("p (e k) -> p e k", e=2)
        owt = stats[0:2 * ROWS, 44:46]
        ownmax = stats[:, 46:62].rearrange("p (b k) -> p b k", k=2)
        mx = stats[0:10, 64:96]
        mxb = stats[0:10, 96:224].rearrange("p (j r) -> p j r", j=QUADS)
        xnat = arena_s[:, 0:3072].rearrange("p (t n) -> p t n", n=D)
        knat = arena_s[:, 2048:5120].rearrange("p (t k n) -> p t k n", t=3, n=WID)
        Wrel = arena_s[:, 5120:5376].rearrange("p (k n) -> p k n", k=2)
        Gsb = arena_s[0:HEADS, 5376:5376 + GW]
        lamv = arena_s[:, 5760:6016].rearrange("p (v n) -> p v n", v=4)
        ownb = arena_s[0:ROWS, 6016:6080].rearrange("p (k n) -> p k n", k=2)
        ynat = arena_s[:, 0:3072].rearrange("p (t n) -> p t n", n=D)
        dsq = arena_s[:, 0:4 * TOK].rearrange("p (m t) -> p m t", t=TOK)
        drr = arena_s[:, 1152:1152 + 4 * TOK].rearrange("p (m t) -> p m t", t=TOK)
        ztmp = arena_s[:, 2304:2304 + 2 * TOK].rearrange("p (s t) -> p s t", s=2)
        neglam, dgain = small[:, 0:1], small[:, 1:2]
        far = small[:, 14:16]
        rweight = small[:, 3:4]

        gdram = nc.dram_tensor("bias_lines", [HEADS, P, GW], F32, kind="Internal")

        x_in, con_in, small_in, pt_in, bias_in = (sem(n) for n in ("x_in", "con_in", "small_in", "pt_in", "bias_in"))
        w_in = [sem(f"w_in{s}") for s in range(2)]
        k_in = [sem(f"k_in{s}") for s in range(NPG)]
        v_in = [sem(f"v_in{s}") for s in range(2)]
        f_in = [sem(f"f_in{s}") for s in range(2)]
        g_out, k_out, stored = sem("g_out"), sem("k_out"), sem("stored")
        cst_out = [sem(f"cst_out{s}") for s in range(2)]
        consts_set, set_up, set_pe, lam_summed, lam_exped = (
            sem(n) for n in ("consts_set", "set_up", "set_pe", "lam_summed", "lam_exped"))
        vec_own, act_own = Tally(sem("vec_own")), Tally(sem("act_own"))
        gated = sem("gated")
        x_turned, x_copied = sem("x_turned"), sem("x_copied")
        squared, summed, meaned, rooted, normed = (sem(n) for n in ("squared", "summed", "meaned", "rooted", "normed"))
        tile_ready = sem("tile_ready")
        in_taken, mix_taken, down_taken = sem("in_taken"), sem("mix_taken"), sem("down_taken")
        nat_ready, nat_taken = sem("nat_ready"), sem("nat_taken")
        q_scaled = sem("q_scaled")
        p_scores, p_biased, p_exped, p_probs = (sem(n) for n in ("p_scores", "p_biased", "p_exped", "p_probs"))
        p_turned, p_pt, p_mixed, p_taken = (sem(n) for n in ("p_turned", "p_pt", "p_mixed", "p_taken"))
        vec_p, edges_set = sem("p_maxima"), sem("edges_set")
        sel_set, q_laid, q_spread, z_cleared = sem("sel_set"), sem("q_laid"), sem("q_spread"), sem("z_cleared")
        q_copied, own_scored, own_done = sem("q_copied"), sem("own_scored"), sem("own_done")
        k_turned = sem("k_turned")
        z_ready = sem("z_ready")
        scored = sem("scored")
        stats_ready, stats_turned = sem("stats_ready"), sem("stats_turned")
        max_ready, max_turned, m_ready = sem("max_ready"), sem("max_turned"), sem("m_ready")
        s_exped, pt_ready, s_summed = sem("s_exped"), sem("pt_ready"), sem("s_summed")
        v_half_used, v_used = sem("v_half_used"), sem("v_used")
        on_ready, o_turned, o_taken = sem("on_ready"), sem("o_turned"), sem("o_taken")
        d_squared, d_summed, d_meaned, d_rooted, d_done = (
            sem(n) for n in ("d_squared", "d_summed", "d_meaned", "d_rooted", "d_done"))
        f_turned, f_copied, ext_ready = sem("f_turned"), sem("f_copied"), sem("ext_ready")
        conv_done, silu_done, ff_done = sem("conv_done"), sem("silu_done"), sem("ff_done")
        ends_packed, mask_set = sem("ends_packed"), sem("mask_set")
        c_turned, c_staged, half_used = sem("c_turned"), sem("c_staged"), sem("half_used")
        y_turned, y_copied_a, y_copied_v = sem("y_turned"), sem("y_copied_a"), sem("y_copied_v")

        W_GATE, W_O, W_OUT, W_UP = 16 * 3, (16 * 9, 16 * 7), (16 * 10, 16 * 8), (16 * 10, 16 * 8)
        PLACE = [8, 9, 10, 11, 20, 21, 22, 23, 0, 1, 2, 3, 4, 5, 6, 7]
        GATE_AT = {2: 0, 7: 1, 10: 2, 12: 3, 14: 4, 16: 5}
        T_GATE, T_OA, T_OB, T_OUT, T_UP, T_DOWN = 24, 40, 48, 56, 64, 108

        w_in_v = a["w_in"][0].rearrange("(k p) n -> p k n", p=P)
        w_gate_v = a["w_gate"][0].rearrange("(k p) n -> p k n", p=P)
        w_oa_v = a["w_out_a"][0].rearrange("(k p) n -> p k n", p=P)
        w_ob_v = a["w_out_b"][0].rearrange("(k p) n -> p k n", p=P)
        w_out_v = a["w_out"][0].rearrange("(k p) n -> p k n", p=P)
        w_up_v = a["w_up"][0].rearrange("(k p) (h n) -> p k h n", p=P, h=2)
        w_down_v = a["w_down"][0].rearrange("(k p) n -> p k n", p=P)

        def slot8(s):
            return wbuf[:, s, :].rearrange("p (k n) -> p k n", k=8)

        def slot4(s):
            return wbuf[:, s, :].rearrange("p (k n) -> p k n", k=4)

        def slot_gate(s):
            return wbuf[:, s, 0:2048].rearrange("p (k n) -> p k n", k=8)

        def slot_up(s, h):
            return wbuf[:, s, 2048 * h:2048 * h + 2048].rearrange("p (k n) -> p k n", k=8)

        def slot11(s):
            return wbuf[:, s, 0:11 * 256].rearrange("p (k n) -> p k n", k=11)

        block = ctx.enter_context(nc.Block())

        @block.sync
        def _(sp):
            for n, (t0, cnt) in enumerate(TOKENS):
                src = a["x_prompt"][0][t0:t0 + cnt] if n < 2 else a["x_sample"].rearrange("b t n -> (b t) n")
                sp.dma_start(xnat[0:cnt, n, :], src).then_inc(x_in, 16)
            sp.dma_start(con[:, :], a["constants"]).then_inc(con_in, 16)
            sp.dma_start(vecs[0:1, :], a["norm_attn"]).then_inc(small_in, 16)
            sp.dma_start(vecs[1:2, :], a["norm_ffn"]).then_inc(small_in, 16)
            sp.dma_start(vecs[2:3, :], a["norm_final"].rearrange("(o n) -> o n", o=1)).then_inc(small_in, 16)
            for t in range(T):
                sp.dma_start(relb[32 * t:32 * t + 32, :], a["rel_bias"]).then_inc(small_in, 16)
            sp.dma_start(relm[0:BUCKETS, :], a["rel_bias"]).then_inc(small_in, 16)
            sp.dma_start(small[:, 4:5], a["diff_norm"].rearrange("o n -> n o")).then_inc(small_in, 16)
            for n, name in enumerate(("lambda_q1", "lambda_k1", "lambda_q2", "lambda_k2")):
                sp.dma_start(lamv[:, n, :], a[name].broadcast_to([P, HD])).then_inc(small_in, 16)
            sp.dma_start(pages[:, :], a["page_table"].rearrange("(o b) g -> o (b g)", o=1)).then_inc(pt_in, 16)
            sp.wait_ge(set_up, 2)
            sp.dma_start(gdram[:, :, :], Gsb.unsqueeze(1).broadcast_to([HEADS, P, GW])).then_inc(g_out, 16)
            sp.wait_ge(g_out, 16)
            g = gdram[:, :, :]
            sp.dma_start(pbias[:, :, 0:256], bass.AP(g.tensor, P - 1, [[GW - 1, P], [P * GW, HEADS], [1, 256]])
                         ).then_inc(bias_in, 16)
            sp.dma_start(pbias[:, :, 256:384], bass.AP(g.tensor, 2 * P - 1, [[GW - 1, P], [P * GW, HEADS], [1, P]])
                         ).then_inc(bias_in, 16)
            sp.wait_ge(pt_in, 16)

            def page_id(entry):
                return sp.value_load(pages[0:1, bass.ds(entry, 1)], min_val=0, max_val=NPHYS - 1)

            def page(name, pg):
                return a[name][0].rearrange("g p h n -> g p (h n)")[bass.ds(pg, 1)].rearrange("o p n -> (o p) n")

            def load_k(b):
                for g in range(NPG):
                    pg = page_id(b * NPG + g)
                    if g == 0 and not first(b):
                        sp.wait_ge(scored, b)
                    for kind, name in enumerate(("cache_moba_k", "cache_diff_k")):
                        sp.dma_start(keys[:, g, kind * WID:kind * WID + WID], page(name, pg)).then_inc(k_in[g], 16)

            def load_v(b, kind):
                for g in range(NPG):
                    pg = page_id(b * NPG + g)
                    if g == 0 and not first(b):
                        sp.wait_ge((v_half_used, v_used)[kind], b)
                    sp.dma_start(vals[:, kind, g, :], page(("cache_moba_v", "cache_diff_v")[kind], pg)
                                 ).then_inc(v_in[kind], 16)

            load_k(0)
            load_k(1)
            sp.wait_ge(p_taken, 8)
            load_v(0, 0)
            load_v(0, 1)
            with sp.Fori(1, LAST) as b:
                load_k(b + 1)
                load_v(b, 0)
                load_v(b, 1)
            load_v(LAST, 0)
            load_v(LAST, 1)

            def conv_rows(c, par):
                for r0, src in ((0, a["state_conv"][0].rearrange("b r n -> (b r) n")),
                                (16, a["conv_w"][0]), (19, a["conv_b"])):
                    rows = src.shape[0]
                    for h in range(2):
                        sp.dma_start(frow[r0:r0 + rows, par, h * 256:h * 256 + 256],
                                     src[:, bass.ds(c * 256 + h * FF, 256)]).then_inc(f_in[par], 16)

            sp.wait_ge(scored, DB)
            conv_rows(0, 0)
            conv_rows(1, 1)
            sp.wait_ge(f_turned, 1)
            conv_rows(2, 0)
            with sp.Fori(1, 5) as i:
                for c, par in ((2 * i + 1, 1), (2 * i + 2, 0)):
                    sp.wait_ge(f_turned, c - 1)
                    conv_rows(c, par)

        @block.gpsimd
        def _(pool):
            nc.gpsimd.memset(ones[:, :], 1.0).then_inc(consts_set, 1)
            nc.gpsimd.memset(Qbd[:, :, :, :], 0.0).then_inc(consts_set, 1)
            nc.gpsimd.memset(ownS[:, :, :, :], MASKED).then_inc(consts_set, 1)
            nc.gpsimd.memset(ownmax[:, :, :], LOWEST).then_inc(consts_set, 1)
            for g in range(12):
                kind, tt = divmod(g, 3)
                pool.wait_ge(nat_taken, g + 1)
                src = (knat if kind < 2 else vnat)[0:TOKENS[tt][1], tt, kind % 2, :]
                name = ("moba_k", "diff_k", "moba_v", "diff_v")[kind]
                if tt < 2:
                    dst = out[name + "_prompt"][0, 0, tt * P:tt * P + P].rearrange("t h n -> t (h n)")
                else:
                    dst = out[name + "_sample"][0].rearrange("b t h n -> (b t) (h n)")
                pool.dma_start(dst, src).then_inc(k_out if kind < 2 else stored, 16)

            pool.wait_ge(k_out, 16 * 6)
            nc.gpsimd.memset(Z[:, :, :], 0.0).then_inc(z_cleared, 1)

            def conv_store(c, par):
                pool.wait_ge(c_staged, c + 1)
                for h in range(2):
                    cols = slice(h * 256, h * 256 + 256)
                    for part, dst in ((cst[0:2, par, cols], out["conv_prompt"][0, 0]),
                                      (cst[2:18, par, cols], out["conv_sample"][0].rearrange("b r n -> (b r) n"))):
                        pool.dma_start(dst[:, bass.ds(c * 256 + h * FF, 256)], part).then_inc(cst_out[par], 16)

            for c in range(3):
                conv_store(c, c % 2)
            with pool.Fori(1, 5) as i:
                conv_store(2 * i + 1, 1)
                conv_store(2 * i + 2, 0)
            for n, (t0, cnt) in enumerate(TOKENS):
                pool.wait_ge(y_copied_a, n + 1)
                pool.wait_ge(y_copied_v, n + 1)
                dst = out["y_prompt"][0][t0:t0 + cnt] if n < 2 else out["y_sample"].rearrange("b t n -> (b t) n")
                pool.dma_start(dst, ynat[0:cnt, n, :]).then_inc(stored, 16)
            pool.wait_ge(stored, 16 * 9)
            pool.wait_ge(cst_out[0], 64 * 6)
            pool.wait_ge(cst_out[1], 64 * 5)

        @block.tensor
        def _(pe):
            mm, turn = nc.tensor.matmul, nc.tensor.transpose

            def sum_of_squares(use):
                for j in range(DT):
                    pe.wait_ge(squared, DT * use + j + 1)
                    last = mm(ps[:, 7, 0:TOK], ones[:, :], hT[:, j, :], start=(j == 0), stop=(j == DT - 1))
                last.then_inc(summed, 1)

            def tile(bank, weights, moving, opens=True, stop=True, after=None):
                for k, (w, x) in enumerate(zip(weights, moving)):
                    if after is not None:
                        pe.wait_ge(normed, after + k + 1)
                    last = mm(ps[:, bank, 0:TOK], w, x, start=(opens and k == 0),
                              stop=(stop and k == len(moving) - 1))
                return last

            pe.wait_ge(x_in, 48)
            pe.wait_ge(con_in, 16)
            for j in range(DT):
                if j >= 4:
                    pe.wait_ge(x_copied, j - 3)
                for n, (t0, cnt) in enumerate(TOKENS):
                    last = turn(ps[:, j % 4, t0:t0 + cnt], xnat[0:cnt, n, j * P:j * P + P], ident[0:cnt, 0:cnt])
                last.then_inc(x_turned, 1)
            pe.wait_ge(consts_set, 4)
            sum_of_squares(0)
            pe.wait_ge(small_in, 16 * 13)
            pe.wait_ge(mask_set, 1)
            for j in range(DT):
                last = turn(ps[:, 4, 4 * j:4 * j + 3], vecs[0:3, j * P:j * P + P], ident[0:3, 0:3])
            last.then_inc(set_pe, 1)
            mm(ps[0:HEADS, 5, 0:GW], relm[:, :], con[0:BUCKETS + 1, C_G:C_G + GW], start=True, stop=True
               ).then_inc(set_pe, 1)
            pe.wait_ge(set_up, 4)
            for kind in range(2):
                last = mm(ps[:, 6, 256 * kind:256 * kind + 161], Wrel[:, kind, :], hot, start=True, stop=True)
            last.then_inc(set_pe, 1)

            h = [hT[:, k, :] for k in range(DT)]
            with pe.Fori(0, 3) as i:
                for s in range(2):
                    pe.wait_ge(w_in[s], (i + 1) * 16)
                    for q in range(4):
                        pe.wait_ge(in_taken, i * 8 + (4 * s + q + 1))
                        tile(q, [slot8(s)[:, k, q * P:q * P + P] for k in range(DT)], h,
                             after=0 if s == q == 0 else None).then_inc(tile_ready, 1)

            pe.wait_ge(set_up, SET_UP)
            for g in range(12):
                kind, tt = divmod(g, 3)
                m0 = (4, 16, 8, 20)[kind]
                t0, cnt = TOKENS[tt]
                pe.wait_ge(in_taken, 4 + m0 + 4)
                if g >= 2:
                    pe.wait_ge(nat_taken, g - 1)
                for q in range(4):
                    last = turn(ps[0:cnt, 4 + g % 2, q * P:q * P + P], qkvT[:, m0 + q, t0:t0 + cnt], ident)
                last.then_inc(nat_ready, 1)

            pe.wait_ge(q_laid, 4)
            pe.wait_ge(sel_set, 1)
            for kind in range(2):
                for n in range(4):
                    last = mm(ps[:, 6 + kind, n * P:n * P + P], sel[:, n, :],
                              qkvT[:, 12 * kind:12 * kind + 4, SEQ:TOK], start=True, stop=True)
            last.then_inc(q_spread, 1)
            pe.wait_ge(nat_taken, 12)
            own = ps[0:NEW, 4, :].rearrange("r (b k c) -> r b k c", b=DB, c=8)
            for k in range(8):
                last = mm(own[:, :, k, :], qkvT[:, 12 * (k // 4) + 4 + k % 4, SEQ:TOK], Qbd[:, k, :, :],
                          start=True, stop=True)
            last.then_inc(own_scored, 1)

            def p_score(u):
                kind, p, hh = u // 8, u % 8 // 2, u % 2
                q0, k0, rows = 12 * kind + p, 12 * kind + 4 + p, slice(64 * hh, 64 * hh + 64)
                if u >= 2:
                    pe.wait_ge(p_biased, 2 * (u - 1))
                mm(ps[:, 1 + u % 2, 0:256], qkvT[rows, q0, P:2 * P], qkvT[rows, k0, 0:256], start=True, stop=True)
                mm(ps[:, 1 + u % 2, 256:384], qkvT[rows, q0, 0:P], qkvT[rows, k0, 0:P], start=True, stop=True
                   ).then_inc(p_scores, 1)

            def p_turn(v):
                u = RESULT[v]
                pe.wait_ge(p_probs, 2 * (v + 1))
                if v >= 2:
                    pe.wait_ge(p_pt, v - 1)
                b = 3 + v % 2
                turn(ps[:, b, 0:P], pS[:, u % 4, 256:384], ident)
                turn(ps[:, b, P:2 * P], pS[:, u % 4, 0:P], ident)
                turn(ps[:, b, 2 * P:3 * P], pS[:, u % 4, P:2 * P], ident).then_inc(p_turned, 1)

            def p_mix(v):
                kind, o = v // 8, (v // 2 if v < 8 else v - 4)
                if kind == 0:
                    rows, cols = slice(64 * (v % 2), 64 * (v % 2) + 64), slice(HD * v, HD * v + HD)
                else:
                    rows, cols = slice(0, P), slice(P * (v - 8), P * (v - 8) + P)
                if o >= 2 and (kind == 1 or v % 2 == 0):
                    pe.wait_ge(p_taken, o - 1)
                pe.wait_ge(p_pt, v + 1)
                b = 5 + o % 2
                mm(ps[rows, b, 0:256], vnat[:, 0, kind, cols], pPT[:, v % 2, 0:256], start=True, stop=False)
                mm(ps[rows, b, P:256], vnat[:, 1, kind, cols], pPT[:, v % 2, 256:384], start=False, stop=True
                   ).then_inc(p_mixed, 1)

            pe.wait_ge(in_taken, 4 + 24)
            pe.wait_ge(own_done, 1)
            pe.wait_ge(q_copied, 2)
            def s_keys(b, kinds=(0, 1)):
                pe.wait_ge(k_turned, b * NPG + NPG)
                pe.wait_ge(z_ready, b * 8 + 8)
                for kind in kinds:
                    for n in range(16):
                        c0 = 128 * n
                        last = mm(ps[:, 0, HALF * kind:HALF * kind + HALF], Z[:, kind, c0:c0 + P],
                                  kblocks[:, :, kind, n, :], start=(n == 0), stop=(n == 15))
                if 1 in kinds:
                    last.then_inc(scored, 1)

            def s_stats(b):
                pe.wait_ge(stats_ready, b + 1)
                mm(ps[:, 1, 0:NBLK], con[:, C_SUM:C_SUM + P], blocksum, start=True, stop=True)
                turn(ps[0:10, 1, P:2 * P], smax.rearrange("p k n -> p (k n)"), ident).then_inc(stats_turned, 1)

            def s_maxima(b):
                pe.wait_ge(max_ready, b + 1)
                mm(ps[:, 1, 256:266], mxb.rearrange("p j r -> p (j r)"), ident[0:10, 0:10], start=True, stop=True
                   ).then_inc(max_turned, 1)

            def s_sums(b, e):
                if not first(b):
                    pe.wait_ge(o_taken, b * 4)
                pe.wait_ge(s_exped, b * 2 + 2)
                for kind in range(2):
                    last = mm(ps[ROWS * kind:ROWS * kind + ROWS, 3, 400:402], con[:, C_SUM:C_SUM + ROWS], rowsum[:, e],
                              start=True, stop=True)
                last.then_inc(s_summed, 1)
                pe.wait_ge(pt_ready, b + 1)

            def s_values(b, e, kinds=(0, 1)):
                for kind in kinds:
                    o = ps[ROWS * kind:ROWS * kind + ROWS, 2, :]
                    pe.wait_ge(v_in[kind], b * P + P)
                    for g in range(NPG):
                        mm(o, PT[:, e, kind, g, :], vals[:, kind, g, :], start=(g == 0), stop=False)
                    mm(o, PT[0:NEW, e, kind, NPG, :], vnat[0:NEW, 2, kind, :], start=False, stop=True
                       ).then_inc((v_half_used, v_used)[kind], 1)

            def s_turn_out(b):
                pe.wait_ge(on_ready, b + 1)
                for p in range(4):
                    last = mm(ps[:, 3, 64 * p:64 * p + 64], On[:, p * P:p * P + P], ident[0:64, 0:64],
                              start=True, stop=True)
                last.then_inc(o_turned, 1)

            def s_step(b, e):
                s_keys(b + 1, (0,))
                if not first(b):
                    s_turn_out(b - 1)
                s_keys(b + 1, (1,))
                s_sums(b, e)
                s_values(b, e, (0,))
                s_stats(b + 1)
                pe.wait_ge(in_taken, b + (4 + T_GATE + 6))
                q = 1 - e
                if not first(b):
                    pe.wait_ge(w_in[0], (b + e) * 8 + (W_GATE + 32))
                tile(5 - e, [slot_gate(1 if first(b) else 0)[:, k, q * P:q * P + P] for k in range(DT)], h
                     ).then_inc(tile_ready, 1)
                s_maxima(b + 1)
                s_values(b, e, (1,))

            for u in range(16 + 3):
                if u < 16:
                    p_score(u)
                if u - 2 in RESULT:
                    p_turn(RESULT.index(u - 2))
                if u - 3 in RESULT:
                    p_mix(RESULT.index(u - 3))
                if u in GATE_AT:
                    m = GATE_AT[u]
                    pe.wait_ge(w_in[m // 2 % 2], W_GATE + 16 * (m // 4 + 1))
                    pe.wait_ge(in_taken, 4 + T_GATE + m)
                    tile(7, [slot_gate(m // 2 % 2)[:, k, m % 2 * P:m % 2 * P + P] for k in range(DT)], h
                         ).then_inc(tile_ready, 1)
                if u in (5, 8):
                    s_keys(0, (u // 8,))

            pe.wait_ge(p_taken, 8)
            s_stats(0)
            pe.wait_ge(w_in[1], W_GATE + 32)
            tile(4, [slot_gate(1)[:, k, 0:P] for k in range(DT)], h).then_inc(tile_ready, 1)
            s_maxima(0)
            s_step(0, 0)
            with pe.Fori(0, 3) as i:
                s_step(2 * i + 1, 1)
                s_step(2 * i + 2, 0)
            s_turn_out(LAST - 1)
            pe.wait_ge(w_in[1], W_GATE + 48)
            for q in range(2):
                pe.wait_ge(in_taken, 4 + T_GATE + 13 + q)
                tile(4 + q, [slot_gate(1)[:, k, q * P:q * P + P] for k in range(DT)], h).then_inc(tile_ready, 1)
            s_sums(LAST, 1)
            s_values(LAST, 1)
            s_turn_out(LAST)
            pe.wait_ge(o_taken, 4 * DB)
            for kind in range(2):
                if kind == 1:
                    pe.wait_ge(d_done, 1)
                pe.wait_ge(w_in[kind], W_O[kind])
                for m in range(DT):
                    if kind == 0 and m == 2:
                        pe.wait_ge(in_taken, 4 + T_OA)
                        pe.wait_ge(d_squared, 1)
                        for n in range(4):
                            last = mm(ps[:, 4 + n, 0:TOK], ones[:, :], dsq[:, n, :], start=True, stop=True)
                        last.then_inc(d_summed, 1)
                    if 8 * kind + m >= 4:
                        pe.wait_ge(mix_taken, 8 * kind + m - 3)
                    tile(m % 4, [slot4(kind)[:, k, m * P:m * P + P] for k in range(4)],
                         [oT[:, 4 * kind + k, :] for k in range(4)]).then_inc(tile_ready, 1)
            pe.wait_ge(mix_taken, 16)
            for m in range(DT):
                s = m // 4
                if m % 4 == 0:
                    pe.wait_ge(w_in[s], W_OUT[s])
                pe.wait_ge(mix_taken, 16 + max(m - 3, 0))
                tile(m % 4, [slot8(s)[:, k, (m % 4) * P:(m % 4) * P + P] for k in range(DT)],
                     [mT[:, k, :] for k in range(DT)]).then_inc(tile_ready, 1)
            sum_of_squares(1)

            def state_turn(c, par):
                pe.wait_ge(ends_packed, c + 1)
                if not first(c):
                    pe.wait_ge(c_staged, c)
                for q in range(4):
                    last = turn(ps[0:18, 5, q * P:q * P + P], ends[:, par, q, :], ident)
                last.then_inc(c_turned, 1)

            def up(c, par):
                pe.wait_ge(f_in[par], so_far(c, par, 96))
                if not first(c):
                    pe.wait_ge(f_copied, c)
                for q in range(4):
                    last = mm(ps[:, 4, 20 * q:20 * q + 20], frow[0:20, par, q * P:q * P + P], ident[0:20, 0:20],
                              start=True, stop=True)
                last.then_inc(f_turned, 1)
                pe.wait_ge(w_in[par], W_UP[par] + so_far(c, par, 32))
                for q in range(4):
                    if not first(c):
                        pe.wait_ge(ext_ready, c * 8 + 2 * (q - 3))
                    tile(q, [slot_up(par, q // 2)[:, k, (q % 2) * P:(q % 2) * P + P] for k in range(DT)], h,
                         after=DT if first(c) and q == 0 else None).then_inc(tile_ready, 1)

            pe.wait_ge(mix_taken, 24)
            up(0, 0)
            up(1, 1)
            state_turn(0, 0)
            up(2, 0)
            state_turn(1, 1)
            with pe.Fori(1, 5) as i:
                up(2 * i + 1, 1)
                state_turn(2 * i, 0)
                up(2 * i + 2, 0)
                state_turn(2 * i + 1, 1)
            state_turn(10, 0)

            pe.wait_ge(ff_done, 22)
            with pe.Fori(0, 2) as i:
                for e in range(2):
                    for half in range(2):
                        s = 1 - half
                        pe.wait_ge(w_in[s], i * 32 + (W_UP[s] + 32 * (5 + half) + 16 * (e + 1)))
                        for q in range(2):
                            if half == 0:
                                pe.wait_ge(down_taken, i * 4 + (2 * e + q + 1))
                            last = tile(2 * e + q, [slot11(s)[:, k, q * P:q * P + P] for k in range(11)],
                                        [ffT[:, 11 * half + k, :] for k in range(11)], half == 0, half == 1)
                            if half == 1:
                                last.then_inc(tile_ready, 1)
                        if half == 0:
                            last.then_inc(half_used, 1)
            sum_of_squares(2)

            for g in range(6):
                n, half = divmod(g, 2)
                t0, cnt = TOKENS[n]
                if g >= 4:
                    pe.wait_ge((y_copied_a, y_copied_v)[half], n - 1)
                for q in range(4):
                    if n == 0:
                        pe.wait_ge(normed, 2 * DT + 4 * half + q + 1)
                    last = turn(ps[0:cnt, g % 4, q * P:q * P + P], hT[:, 4 * half + q, t0:t0 + cnt], ident)
                last.then_inc(y_turned, 1)

        @block.scalar
        def _(act):
            fn, copy = nc.scalar.activation, nc.scalar.copy

            def load(s, dst, src):
                act.dma_start(dst, src).then_inc(w_in[s], 16)

            def load_up(c, par):
                for hlf in range(2):
                    src = w_up_v[:, :, hlf, :][:, :, bass.ds(c * 256, 256)]
                    act.dma_start(slot_up(par, hlf), src).then_inc(w_in[par], 16)

            def root(use):
                act.wait_ge(meaned, use + 1)
                fn(rr[:, :], rr[:, :], ACT.Sqrt).then_inc(rooted, 1)

            act.wait_ge(x_in, 48)
            act.wait_ge(small_in, 16 * 13)
            load(0, slot8(0), w_in_v[:, :, 0:512])
            load(1, slot8(1), w_in_v[:, :, 512:1024])
            for j in range(DT):
                act.wait_ge(x_turned, j + 1)
                fn(hT[:, j, :], ps[:, j % 4, 0:TOK], ACT.Square).then_inc(squared, 1)
                copy(xT[:, j, :], ps[:, j % 4, 0:TOK]).then_inc(x_copied, 1)
            act.wait_ge(lam_summed, 2)
            fn(small[:, 10:12], small[:, 8:10], ACT.Exp).then_inc(lam_exped, 1)
            root(0)
            act.sem_inc(in_taken, 4)

            def take_in(n, dst0):
                for q in range(4):
                    act.wait_ge(tile_ready, n * 4 + q + 1)
                    copy(qkvT[:, bass.ds(n * 4 + q, 1), :].rearrange("p o t -> p (o t)"), ps[:, q, 0:TOK]
                         ).then_inc(in_taken, 1)

            with act.Fori(0, 2) as i:
                for s in range(2):
                    take_in(2 * i + s, 0)
                    load(s, slot8(s), w_in_v[:, :, bass.ds((2 * i + s + 2) * 512, 512)])
            for n in (4, 5):
                take_in(n, 0)
                load(n % 2, slot_gate(n % 2), w_gate_v[:, :, (n - 4) * 256:(n - 3) * 256])

            def p_exp(u):
                act.wait_ge(p_biased, 2 * u + 2)
                act.wait_ge(vec_p, u + 1)
                fn(pS[:, u % 4, 0:256], pS[:, u % 4, 0:256], ACT.Exp, bias=pstat[:, u, 2:3],
                   accum_out=pstat[:, u, 4:5]).then_inc(p_exped, 1)
                fn(pS[:, u % 4, 256:384], pS[:, u % 4, 256:384], ACT.Exp, bias=pstat[:, u, 3:4],
                   accum_out=pstat[:, u, 5:6]).then_inc(p_exped, 1)

            def p_copy(v):
                act.wait_ge(p_turned, v + 1)
                if v >= 2:
                    act.wait_ge(p_mixed, v - 1)
                copy(pPT[:, v % 2, :], ps[:, 3 + v % 2, 0:GW]).then_inc(p_pt, 1)

            def take_gate(m, bank):
                copy(gT[:, m, :] if isinstance(m, int) else gT[:, bass.ds(m, 1), :].rearrange("p o t -> p (o t)"),
                     ps[:, bank, 0:TOK]).then_inc(in_taken, 1)

            def load_gates(n, s):
                load(s, slot_gate(s), w_gate_v[:, :, bass.ds(n * 256, 256)])

            for u in range(16 + 3):
                if u < 16:
                    p_exp(u)
                if u - 2 in RESULT:
                    p_copy(RESULT.index(u - 2))
                if u in GATE_AT:
                    m = GATE_AT[u]
                    act.wait_ge(tile_ready, T_GATE + m + 1)
                    take_gate(PLACE[m], 7)
                    if m % 2 == 1:
                        load_gates(m // 2 + 2, m // 2 % 2)

            def s_exp(b, e):
                act.wait_ge(m_ready, b * 2 + 2)
                for kind in range(2):
                    fn(S[:, kind, :], S[:, kind, :], ACT.Exp, bias=negmax[:, kind:kind + 1],
                       accum_out=rowsum[:, e, kind:kind + 1]).then_inc(s_exped, 1)

            def gate(b, e):
                act.wait_ge(tile_ready, b + (T_GATE + 8))
                take_gate(b - 1, 5 - e)

            s_exp(0, 0)
            for m in (6, 7):
                act.wait_ge(tile_ready, T_GATE + m + 1)
                take_gate(PLACE[m], m - 2)
            load_gates(7, 1)
            s_exp(1, 1)
            with act.Fori(0, 2) as i:
                gate(2 * i + 1, 1)
                s_exp(2 * i + 2, 0)
                gate(2 * i + 2, 0)
                load_gates(i + 5, 0)
                s_exp(2 * i + 3, 1)
            gate(5, 1)
            s_exp(6, 0)
            gate(6, 0)
            load(0, slot4(0), w_oa_v)
            s_exp(7, 1)
            for m in (14, 15):
                act.wait_ge(tile_ready, T_GATE + m + 1)
                take_gate(PLACE[m], m - 10)
            load(1, slot4(1), w_ob_v)
            act.wait_ge(o_taken, 4 * DB)
            fn(dsq[:, :, :], oT[:, 4:8, :], ACT.Square).then_inc(d_squared, 1)
            act.wait_ge(in_taken, 4 + T_OA)
            for m0, m1 in ((8, 12), (20, 24), (0, 8)):
                fn(gT[:, m0:m1, :], gT[:, m0:m1, :], ACT.Sigmoid).then_inc(gated, 1)

            act.wait_ge(d_meaned, 1)
            fn(drr[:, :, :], drr[:, :, :], ACT.Sqrt).then_inc(d_rooted, 1)
            act.wait_ge(tile_ready, T_OB)
            load(0, slot8(0), w_out_v[:, :, 0:512])
            act.wait_ge(tile_ready, T_OUT)
            load(1, slot8(1), w_out_v[:, :, 512:1024])
            act.wait_ge(tile_ready, T_OUT + 4)
            load_up(0, 0)
            for j in range(DT):
                act.wait_ge(mix_taken, 16 + j + 1)
                fn(hT[:, j, :], xT[:, j, :], ACT.Square).then_inc(squared, 1)
            load_up(1, 1)
            root(1)

            def take_up(c, par):
                for q in range(4):
                    act.wait_ge(tile_ready, c * 4 + T_UP + q + 1)
                    if q == 0 and not early(c):
                        act.wait_ge(conv_done, (c - 1) * 4)
                    e = ext[:, 4 * par + q, :]
                    copy(e[:, 2:258], ps[:, q, 0:SEQ]).then_inc(ext_ready, 1)
                    copy(e[:, 258:306].rearrange("p (b r) -> p b r", r=6)[:, :, 2:6],
                         ps[:, q, SEQ:TOK].rearrange("p (b t) -> p b t", t=T)).then_inc(ext_ready, 1)

            def silu(c):
                act.wait_ge(conv_done, c * 4 + 4)
                fn(cv[:, 0:2, 0:CONV], cv[:, 0:2, 0:CONV], ACT.Silu).then_inc(silu_done, 1)

            act.wait_ge(edges_set, 1)
            for c in range(3):
                take_up(c, c % 2)
                load_up(c + 2, c % 2)
                silu(c)
            with act.Fori(1, 4) as i:
                for c, par in ((2 * i + 1, 1), (2 * i + 2, 0)):
                    take_up(c, par)
                    load_up(c + 2, par)
                    silu(c)
            for c, par in ((9, 1), (10, 0)):
                take_up(c, par)
                load(par, slot11(par), w_down_v[:, 11 * (c - 9):11 * (c - 9) + 11, 0:256])
                silu(c)
            with act.Fori(0, 3) as d:
                for half, s in ((0, 1), (1, 0)):
                    if half == 0:
                        act.wait_ge(half_used, d + 1)
                    else:
                        act.wait_ge(tile_ready, d * 2 + T_DOWN + 2)
                    load(s, slot11(s), w_down_v[:, 11 * half:11 * half + 11, bass.ds((d + 1) * 256, 256)])
            for j in range(DT):
                act.wait_ge(down_taken, 4 + j + 1)
                fn(hT[:, j, :], xT[:, j, :], ACT.Square).then_inc(squared, 1)
            root(2)
            for n, (t0, cnt) in enumerate(TOKENS):
                act.wait_ge(y_turned, 2 * n + 1)
                copy(ynat[0:cnt, n, 0:512], ps[0:cnt, 2 * n % 4, :]).then_inc(y_copied_a, 1)

        @block.vector
        def _(dve):
            v = nc.vector

            def own(ins):
                vec_own.add(ins)
                vec_own.wait(dve)

            v.memset(relm[BUCKETS:BUCKETS + 1, :], MASKED).then_inc(mask_set, 1)
            dve.wait_ge(set_pe, 1)
            v.tensor_copy(gcol[:, :, :], ps[:, 4, 0:32].rearrange("p (j c) -> p j c", c=4)[:, :, 0:3]).then_inc(set_up, 1)
            dve.wait_ge(set_pe, 2)
            v.tensor_copy(Gsb, ps[0:HEADS, 5, 0:GW]).then_inc(set_up, 1)
            W6 = Wrel.rearrange("p k (j h t) -> p k j h t", j=QUADS, t=T)
            M6 = con[:, C_TM:C_TM + P].rearrange("p (j q c t) -> p j q c t", j=QUADS, q=4, t=T)
            v.tensor_tensor(W6[:, 0], relb[:, 0:8].unsqueeze(1).unsqueeze(3).broadcast_to([P, QUADS, 8, T]),
                            M6.rearrange("p j q c t -> p j (q c) t"), ALU.mult).then_inc(set_up, 1)
            v.tensor_tensor(Wrel[:, 1, :].rearrange("p (j q n) -> p j q n", j=QUADS, q=4),
                            relb[:, 8:12].unsqueeze(1).unsqueeze(3).broadcast_to([P, QUADS, 4, 8]),
                            M6.rearrange("p j q c t -> p j q (c t)"), ALU.mult).then_inc(set_up, 1)
            for n in range(2):
                v.tensor_tensor_reduce(lamv[:, 2 * n, :], lamv[:, 2 * n, :], lamv[:, 2 * n + 1, :], 1.0, 0.0,
                                       ALU.mult, ALU.add, small[:, 8 + n:9 + n]).then_inc(lam_summed, 1)
            v.tensor_scalar(dgain, small[:, 4:5], 1.0 - LAM0, None, ALU.mult).then_inc(set_up, 1)
            dve.wait_ge(set_pe, 3)
            b6 = ps[:, 6, :].rearrange("p (k n) -> p k n", k=2)
            v.tensor_copy(ownb, b6[0:ROWS, :, 129:161]).then_inc(set_up, 1)
            for j in range(QUADS):
                rows = slice(32 * j, 32 * j + 32)
                v.tensor_copy(bias_s[rows, :, NPG - 1, :], b6[rows, :, 1 + 32 * j:33 + 32 * j]).then_inc(set_up, 1)
            own(v.tensor_copy(far, b6[:, :, 0]))
            v.tensor_copy(bias_s[:, :, 0:NPG - 1, :],
                          far.unsqueeze(2).unsqueeze(3).broadcast_to([P, 2, NPG - 1, 32])).then_inc(set_up, 1)
            dve.wait_ge(lam_exped, 1)
            own(v.tensor_tensor(small[:, 12:13], small[:, 11:12], small[:, 10:11], ALU.subtract))
            own(v.tensor_scalar(neglam, small[:, 12:13], -LAM0, None, ALU.add))
            own(v.scalar_tensor_tensor(out=rweight, in0=con[:, C_VEC + 1:C_VEC + 2], scalar=neglam,
                                       in1=con[:, C_VEC:C_VEC + 1], op0=ALU.mult, op1=ALU.add))

            def normalise(use):
                dve.wait_ge(summed, use + 1)
                v.tensor_scalar(rr[:, :], ps[:, 7, 0:TOK], 1.0 / D, EPS, ALU.mult, ALU.add).then_inc(meaned, 1)
                dve.wait_ge(rooted, use + 1)
                own(v.reciprocal(rr[:, :], rr[:, :]))
                for j in range(DT):
                    v.scalar_tensor_tensor(out=hT[:, j, :], in0=xT[:, j, :], scalar=gcol[:, j, use:use + 1],
                                           in1=rr[:, :], op0=ALU.mult, op1=ALU.mult).then_inc(normed, 1)

            dve.wait_ge(x_copied, DT)
            normalise(0)

            def s_turn_keys(b):
                for g in range(NPG):
                    s_turn_page(b, g)

            def s_turn_page(b, g):
                dve.wait_ge(k_in[g], b * 32 + 32)
                v.transpose(keys[:, g, :], keys[:, g, :]).then_inc(k_turned, 1)

            s_turn_keys(0)
            for g in range(12):
                kind, tt = divmod(g, 3)
                cnt = TOKENS[tt][1]
                dve.wait_ge(nat_ready, g + 1)
                v.tensor_copy((knat if kind < 2 else vnat)[0:cnt, tt, kind % 2, :], ps[0:cnt, 4 + g % 2, :]
                              ).then_inc(nat_taken, 1)
            for m0 in (0, 12):
                v.tensor_scalar(qkvT[:, m0:m0 + 4, :], qkvT[:, m0:m0 + 4, :], SCALE, None, ALU.mult
                                ).then_inc(q_scaled, 1)
            dve.wait_ge(q_scaled, 2)
            dve.wait_ge(consts_set, 4)
            for kind in range(2):
                for hh in range(2):
                    rows = slice(64 * hh, 64 * hh + 64)
                    v.tensor_copy(Qbd[rows, 4 * kind:4 * kind + 4, :, 4 * hh:4 * hh + 4],
                                  qkvT[rows, 12 * kind:12 * kind + 4, SEQ:TOK].rearrange("p q (b t) -> p q b t", t=T)
                                  ).then_inc(q_laid, 1)
            v.tensor_copy(sel.rearrange("p v (j r) -> p v j r", j=QUADS),
                          ident.rearrange("p (v r) -> p v r", v=4).unsqueeze(2).broadcast_to([P, 4, QUADS, 32])
                          ).then_inc(sel_set, 1)
            dve.wait_ge(q_spread, 1)
            for kind in range(2):
                for n in range(4):
                    c = v.tensor_copy(
                        qrep[:, kind].rearrange("p b (q n) t -> p b q n t", n=4)[:, :, :, n, :],
                        ps[:, 6 + kind, n * P:n * P + P].rearrange("p (q b t) -> p b q t", q=4, t=T))
                c.then_inc(q_copied, 1)
            dve.wait_ge(own_scored, 1)
            own(v.transpose(ownS[0:ROWS].rearrange("p b k n -> p (b k n)"), ps[0:NEW, 4, :]))
            own(v.tensor_tensor(ownS[0:ROWS], ownS[0:ROWS], ownb.unsqueeze(1).broadcast_to([ROWS, DB, 2, NEW]), ALU.add))
            own(v.tensor_tensor(ownS[0:ROWS], ownS[0:ROWS], con[0:ROWS, C_MASK:C_MASK + DB * NEW].rearrange(
                "p (b n) -> p b n", b=DB).unsqueeze(2).broadcast_to([ROWS, DB, 2, NEW]), ALU.add))
            v.tensor_reduce(ownmax[0:ROWS].rearrange("p b k -> p (b k)"),
                            ownS[0:ROWS].rearrange("p b k n -> p (b k) n"), AX.X, ALU.max).then_inc(own_done, 1)

            def p_bias(u):
                head = u if u < 8 else 8 + (u - 8) // 2
                dve.wait_ge(p_scores, u + 1)
                if u >= 4:
                    done = sum(c <= u - 4 for c in RESULT)
                    if done:
                        dve.wait_ge(p_turned, done)
                for n, cols in enumerate((slice(0, 256), slice(256, 384))):
                    v.tensor_tensor_reduce(pS[:, u % 4, cols], ps[:, 1 + u % 2, cols], pbias[:, head, cols], 1.0, LOWEST,
                                           ALU.add, ALU.max, pstat[:, u, n:n + 1]).then_inc(p_biased, 1)
                dve.wait_ge(p_biased, 2 * u + 2)
                v.tensor_scalar(pstat[:, u, 2:4], pstat[:, u, 0:2], -1.0, None, ALU.mult).then_inc(vec_p, 1)

            def p_norm(u):
                dve.wait_ge(p_exped, 2 * u + 2)
                own(v.reciprocal(pstat[:, u, 6:8], pstat[:, u, 4:6]))
                second = u >= 8 and u % 2 == 1
                if second:
                    own(v.tensor_scalar(pstat[:, u, 6:8], pstat[:, u, 6:8], neglam, None, ALU.mult))
                for n, cols in enumerate((slice(0, 256), slice(256, 384))):
                    x, r = pS[:, u % 4, cols], pstat[:, u, 6 + n:7 + n]
                    if second:
                        v.scalar_tensor_tensor(out=x, in0=x, scalar=r, in1=pS[:, (u - 1) % 4, cols],
                                               op0=ALU.mult, op1=ALU.add).then_inc(p_probs, 1)
                    elif u >= 8:
                        own(v.tensor_scalar(x, x, r, None, ALU.mult))
                    else:
                        v.tensor_scalar(x, x, r, None, ALU.mult).then_inc(p_probs, 1)

            def p_take(o):
                dve.wait_ge(p_mixed, 2 * o + 2 if o < 4 else o + 5)
                v.tensor_copy(oT[:, o, 0:SEQ], ps[:, 5 + o % 2, 0:SEQ]).then_inc(p_taken, 1)

            def s_queries(b):
                for kind in range(2):
                    for j in range(QUADS):
                        rows = slice(32 * j, 32 * j + 32)
                        v.tensor_copy(
                            Z[rows, kind, :].rearrange("p (h n) -> p h n", h=8)[:, :, 0:256].rearrange(
                                "p h (c n) -> p h c n", c=2)[:, :, :, 32 * j:32 * j + T],
                            qrep[rows, kind, bass.ds(b, 1)].rearrange("p o (h c) t -> p (o h) c t", c=2)
                            ).then_inc(z_ready, 1)

            dve.wait_ge(bias_in, 32)
            taken = 0
            for u in range(16 + 4):
                if u == 4:
                    dve.wait_ge(z_cleared, 1)
                    s_queries(0)
                if u >= 12:
                    s_turn_page(1, u - 12)
                if u < 16:
                    p_bias(u)
                if 1 <= u < 17:
                    p_norm(u - 1)
                if u - 4 in RESULT:
                    r = RESULT.index(u - 4)
                    if r >= 8 or r % 2 == 1:
                        p_take(taken)
                        taken += 1

            def s_stats(b):
                raw = ps[:, 0, :].rearrange("p (k n) -> p k n", k=2)
                if not first(b):
                    dve.wait_ge(pt_ready, b)
                vec_own.add(v.tensor_tensor(S[:, :, 0:HALF], raw, bias_s.rearrange("p k g i -> p k (g i)"), ALU.add))
                vec_own.add(v.tensor_copy(S[:, :, HALF:LINE], ownS[:, bass.ds(b, 1)].rearrange("p o k n -> p (o k) n")))
                vec_own.add(v.tensor_reduce(blocksum, ps[:, 0, 0:HALF].rearrange("p (n i) -> p n i", n=NBLK),
                                            AX.X, ALU.add))
                vec_own.add(v.tensor_copy(smax[:, :, NBLK:NBLK + 1], ownmax[:, bass.ds(b, 1)].rearrange("p o (k n) -> p (o k) n", n=1)))
                vec_own.wait(dve)
                v.tensor_reduce(smax[:, :, 0:NBLK], S[:, :, 0:HALF].rearrange("p k (n i) -> p k n i", n=NBLK),
                                AX.X, ALU.max).then_inc(stats_ready, 1)

            def s_select(b):
                dve.wait_ge(stats_turned, b + 1)
                vec_own.add(v.tensor_copy(allsum, ps[:, 1, 0:NBLK]))
                own(v.tensor_reduce(mx, ps[0:10, 1, P:2 * P].rearrange("p (j r) -> p r j", j=QUADS), AX.X, ALU.max))
                v.tensor_copy(mxb, mx.unsqueeze(1).broadcast_to([10, QUADS, ROWS])).then_inc(max_ready, 1)
                own(v.tensor_reduce(low, allsum, AX.X, ALU.min))
                own(v.scalar_tensor_tensor(out=order, in0=allsum, scalar=low, in1=con[:, C_VEC + 3:C_VEC + 7],
                                           op0=ALU.is_equal, op1=ALU.mult))
                own(v.tensor_reduce(worst, order, AX.X, ALU.max))
                own(v.tensor_scalar(pen, order, worst, MASKED, ALU.is_equal, ALU.mult))
                s0 = S[:, 0, 0:HALF].rearrange("p (n i) -> p n i", n=NBLK)
                v.tensor_tensor(s0, s0, pen.unsqueeze(2).broadcast_to([P, NBLK, 64]), ALU.add).then_inc(m_ready, 1)

            def s_row_maxima(b):
                dve.wait_ge(max_turned, b + 1)
                vec_own.add(v.tensor_copy(fmax.rearrange("p k n -> p (k n)"), ps[:, 1, 256:266]))
                vec_own.wait(dve)
                own(v.tensor_tensor(fmax[:, 0, 0:NBLK], fmax[:, 0, 0:NBLK], pen, ALU.add))
                own(v.tensor_reduce(rowmax, fmax, AX.X, ALU.max))
                v.tensor_scalar(negmax, rowmax, -1.0, None, ALU.mult).then_inc(m_ready, 1)

            def s_probs(b, e):
                dve.wait_ge(s_exped, b * 2 + 2)
                if not early(b):
                    dve.wait_ge(v_used, b - 1)
                v.transpose(PT[:, e].rearrange("p k g r -> p (k g r)"), S.rearrange("p k n -> p (k n)")
                            ).then_inc(pt_ready, 1)

            def s_scale(b):
                dve.wait_ge(s_summed, b + 1)
                for kind in range(2):
                    rows = slice(ROWS * kind, ROWS * kind + ROWS)
                    vec_own.add(v.reciprocal(owt[rows, 0:1], ps[rows, 3, 400 + kind:401 + kind]))
                vec_own.wait(dve)
                own(v.tensor_tensor(owt[:, 1:2], owt[:, 0:1], rweight[0:2 * ROWS], ALU.mult))
                dve.wait_ge(v_used, b + 1)
                v.tensor_scalar(On, ps[0:2 * ROWS, 2, :], owt[:, 1:2], None, ALU.mult).then_inc(on_ready, 1)

            def s_take(b):
                dve.wait_ge(o_turned, b + 1)
                O = ps[:, 3, 0:288].rearrange("p (q n) -> p q n", q=4)
                dst = oT[:, :, bass.ds(b * T + SEQ, T)]
                for hh in range(2):
                    rows = slice(64 * hh, 64 * hh + 64)
                    v.tensor_copy(dst[rows, 0:4], O[rows, :, T * hh:T * hh + T]).then_inc(o_taken, 1)
                v.tensor_copy(dst[:, 4:8], O[:, :, 32:32 + T]).then_inc(o_taken, 1)
                dve.wait_ge(o_taken, b * 4 + 3)
                v.tensor_tensor(dst[:, 4:8], dst[:, 4:8], O[:, :, 32 + T:32 + 2 * T], ALU.add).then_inc(o_taken, 1)

            def s_step(b, e, more):
                if not (isinstance(b, int) and b <= 0):
                    s_take(b - 1)
                dve.wait_ge(scored, b + 2)
                s_stats(b + 1)
                if more:
                    s_queries(b + 2)
                turns = more and not (isinstance(b, int) and b < 0)
                for g in range(5 if turns else 0):
                    s_turn_page(b + 2, g)
                s_select(b + 1)
                for g in range(5, NPG if turns else 5):
                    s_turn_page(b + 2, g)
                s_row_maxima(b + 1)
                s_probs(b + 1, 1 - e)
                if not (isinstance(b, int) and b < 0):
                    s_scale(b)

            s_step(-1, 1, True)
            s_step(0, 0, True)
            with dve.Fori(0, 2) as i:
                vec_own.enter(i, 0, 2 * 16)
                s_step(2 * i + 1, 1, True)
                s_step(2 * i + 2, 0, True)
            vec_own.leave(2)
            s_step(5, 1, True)
            s_step(6, 0, False)
            s_take(6)
            s_scale(7)
            s_take(7)

            dve.wait_ge(d_summed, 1)
            v.tensor_scalar(drr[:, :, :], ps[:, 4:8, 0:TOK], 1.0 / P, EPS, ALU.mult, ALU.add).then_inc(d_meaned, 1)
            dve.wait_ge(d_rooted, 1)
            own(v.reciprocal(drr[:, :, :], drr[:, :, :]))
            v.scalar_tensor_tensor(out=oT[:, 4:8, :], in0=oT[:, 4:8, :], scalar=dgain, in1=drr[:, :, :],
                                   op0=ALU.mult, op1=ALU.mult).then_inc(d_done, 1)
            dve.wait_ge(gated, 3)
            for m in range(DT):
                dve.wait_ge(tile_ready, T_OA + m + 1)
                v.tensor_tensor(mT[:, m, :], ps[:, m % 4, 0:TOK], gT[:, PLACE[m], :], ALU.mult).then_inc(mix_taken, 1)
            for m in range(DT):
                dve.wait_ge(tile_ready, T_OB + m + 1)
                own(v.tensor_tensor(ztmp[:, m % 2, :], ps[:, m % 4, 0:TOK], gT[:, PLACE[DT + m], :], ALU.mult))
                v.tensor_tensor(mT[:, m, :], mT[:, m, :], ztmp[:, m % 2, :], ALU.add).then_inc(mix_taken, 1)
            for m in range(DT):
                dve.wait_ge(tile_ready, T_OUT + m + 1)
                v.tensor_tensor(xT[:, m, :], xT[:, m, :], ps[:, m % 4, 0:TOK], ALU.add).then_inc(mix_taken, 1)
            v.memset(ext[:, :, 0:2], 0.0).then_inc(edges_set, 1)
            dve.wait_ge(mix_taken, 24)
            normalise(1)

            def convolve(c, par):
                dve.wait_ge(f_turned, c + 1)
                v.tensor_copy(fcol[:, :, :], ps[:, 4, 0:80].rearrange("p (m n) -> p m n", n=20)).then_inc(f_copied, 1)
                dve.wait_ge(f_copied, c + 1)
                own(v.tensor_copy(
                    ext[:, 4 * par:4 * par + 4, 258:306].rearrange("p m (b r) -> p m b r", r=6)[:, :, :, 0:2],
                    fcol[:, :, 0:16].rearrange("p m (b r) -> p m b r", r=2)))
                for q in range(4):
                    dve.wait_ge(ext_ready, c * 8 + 2 * q + 2)
                    vec_own.add(v.tensor_scalar(cv[:, q, 0:CONV], ext[:, 4 * par + q, 0:CONV], fcol[:, q, 16:17],
                                                fcol[:, q, 19:20], ALU.mult, ALU.add))
                vec_own.wait(dve)
                for q in range(4):
                    vec_own.add(v.scalar_tensor_tensor(out=cv[:, q, 0:CONV], in0=ext[:, 4 * par + q, 1:1 + CONV],
                                                       scalar=fcol[:, q, 17:18], in1=cv[:, q, 0:CONV],
                                                       op0=ALU.mult, op1=ALU.add))
                if not early(c):
                    dve.wait_ge(c_turned, c - 1)
                v.tensor_copy(ends[:, par].rearrange("p q (s r) -> p q s r", r=2),
                              ext[:, 4 * par:4 * par + 4, 256:310].rearrange("p q (s r) -> p q s r", r=6)[:, :, :, 0:2]
                              ).then_inc(ends_packed, 1)
                vec_own.wait(dve)
                for q in range(4):
                    v.scalar_tensor_tensor(out=cv[:, q, 0:CONV], in0=ext[:, 4 * par + q, 2:2 + CONV],
                                           scalar=fcol[:, q, 18:19], in1=cv[:, q, 0:CONV],
                                           op0=ALU.mult, op1=ALU.add).then_inc(conv_done, 1)
                dve.wait_ge(conv_done, c * 4 + 4)
                dve.wait_ge(silu_done, c + 1)
                v.tensor_tensor(ffT[:, bass.ds(c * 2, 2), 0:SEQ], cv[:, 0:2, 0:SEQ], cv[:, 2:4, 0:SEQ], ALU.mult
                                ).then_inc(ff_done, 1)
                new = cv[:, :, 258:306].rearrange("p m (b r) -> p m b r", r=6)[:, :, :, 0:T]
                v.tensor_tensor(ffT[:, bass.ds(c * 2, 2), SEQ:TOK].rearrange("p m (b t) -> p m b t", t=T),
                                new[:, 0:2], new[:, 2:4], ALU.mult).then_inc(ff_done, 1)

            def stage_state(c, par):
                dve.wait_ge(c_turned, c + 1)
                if not early(c):
                    dve.wait_ge(cst_out[par], so_far(c, par, 64) - 64)
                v.tensor_copy(cst[0:18, par, :], ps[0:18, 5, :]).then_inc(c_staged, 1)

            convolve(0, 0)
            convolve(1, 1)
            stage_state(0, 0)
            convolve(2, 0)
            stage_state(1, 1)
            with dve.Fori(1, 5) as i:
                vec_own.enter(i, 1, 18)
                convolve(2 * i + 1, 1)
                stage_state(2 * i, 0)
                convolve(2 * i + 2, 0)
                stage_state(2 * i + 1, 1)
            vec_own.leave(4)
            stage_state(10, 0)
            dve.sem_inc(down_taken, 4)
            for m in range(DT):
                dve.wait_ge(tile_ready, T_DOWN + m + 1)
                v.tensor_tensor(xT[:, m, :], xT[:, m, :], ps[:, m % 4, 0:TOK], ALU.add).then_inc(down_taken, 1)
            dve.wait_ge(down_taken, 4 + DT)
            normalise(2)
            for n, (t0, cnt) in enumerate(TOKENS):
                dve.wait_ge(y_turned, 2 * n + 2)
                v.tensor_copy(ynat[0:cnt, n, 512:1024], ps[0:cnt, (2 * n + 1) % 4, :]).then_inc(y_copied_v, 1)


_INS = ["x_prompt", "x_sample", "cache_moba_k", "cache_moba_v", "cache_diff_k", "cache_diff_v", "state_conv",
        "page_table", "rel_bias", "norm_attn", "w_in", "w_gate", "w_out_a", "w_out_b", "w_out",
        "lambda_q1", "lambda_k1", "lambda_q2", "lambda_k2", "diff_norm", "norm_ffn", "w_up", "conv_w", "conv_b",
        "w_down", "norm_final"]
_OUTS = [("y_prompt", (1, SEQ, D)), ("y_sample", (DB, T, D)),
         ("moba_k_prompt", (1, 1, SEQ, 8, HD)), ("moba_v_prompt", (1, 1, SEQ, 8, HD)),
         ("diff_k_prompt", (1, 1, SEQ, 4, 2 * HD)), ("diff_v_prompt", (1, 1, SEQ, 4, 2 * HD)),
         ("conv_prompt", (1, 1, 2, 2 * FF)),
         ("moba_k_sample", (1, DB, T, 8, HD)), ("moba_v_sample", (1, DB, T, 8, HD)),
         ("diff_k_sample", (1, DB, T, 4, 2 * HD)), ("diff_v_sample", (1, DB, T, 4, 2 * HD)),
         ("conv_sample", (1, DB, 2, 2 * FF))]


def kernel(**inputs):
    import concourse.bacc as _bacc
    from concourse.bass_utils import run_bass_kernel_spmd as _run

    nc = _bacc.Bacc("TRN2", target_bir_lowering=False, num_devices=1)
    arrays, ins, outs = {}, {}, {}
    given = {name: np.ascontiguousarray(inputs[name]) for name in _INS}
    given["constants"] = constants()
    for name, x in given.items():
        arrays[f"in_{name}"] = x
        ins[name] = nc.dram_tensor(f"in_{name}", x.shape, mybir.dt.from_np(x.dtype), kind="ExternalInput").ap()
    for name, shape in _OUTS:
        outs[name] = nc.dram_tensor(f"out_{name}", shape, F32, kind="ExternalOutput").ap()
    build(nc, ins, outs)
    r = _run(nc, [arrays], core_ids=[0])
    return tuple(r.results[0][f"out_{name}"] for name, _ in _OUTS)
```

```python
import math
from contextlib import ExitStack

import numpy as np
import concourse.bass as bass
from concourse import mybir

F32 = mybir.dt.float32
F32R = mybir.dt.float32r
I32 = mybir.dt.int32
ALU = mybir.AluOpType
ACT = mybir.ActivationFunctionType
AX = mybir.AxisListType

P = 128
D = 1024
DT = D // P
SEQ = 256
DB, T = 8, 4
NEW = DB * T
TOK = SEQ + NEW
PAST, PAGE = 1024, 128
NPG = PAST // PAGE
NPHYS = DB * NPG + DB * NPG // 4
BLOCK = 256
NBLK = PAST // BLOCK
HD = 64
WID = 512
FF = 2816
FT = FF // P
BUCKETS, HEADS = 32, 12
EPS = 1e-6
LAM0 = 0.8 - 0.6 * math.exp(0.0)
SCALE = HD ** -0.5
MASKED = -1.0e30
LOWEST = -3.0e38

TOKENS = [(0, P), (P, P), (SEQ, NEW)]
LAST = DB - 1
QUADS = 4
ROWS = 8 * T
HALF = NPG * 32
LINE = HALF + NEW
RESULT = [0, 1, 2, 3, 4, 5, 6, 7, 9, 11, 13, 15]
SET_UP = 11
EXT = 310
CONV = 304
GW = 384

C_ID, C_TM, C_HOT, C_MASK, C_G, C_SUM, C_VEC = 0, 128, 256, 417, 673, 1057, 1185
C_ALL = 1192


def bucket(n):
    n = max(int(n), 0)
    if n < BUCKETS // 2:
        return n
    large = 16 + int(np.float32(np.log(np.float32(n) / np.float32(16))) / np.float32(math.log(8.0)) * np.float32(16))
    return min(large, BUCKETS - 1)


def constants():
    c = np.zeros((P, C_ALL), np.float32)
    c[:, C_ID:C_ID + P] = np.eye(P)
    rows = np.arange(P)
    for part in range(P):
        t, b = divmod(part, BUCKETS)
        c[part, C_TM:C_TM + P] = rows % T == t
        hot = [bucket(PAST)] + [bucket(PAST + t - k) for k in range(PAST - PAGE, PAST)]
        hot += [bucket(t - k % T) for k in range(NEW)]
        c[part, C_HOT:C_HOT + 161] = np.array(hot) == b
    for r in range(ROWS):
        for b in range(DB):
            for k in range(NEW):
                c[r, C_MASK + NEW * b + k] = 0.0 if k // T == b and k % T <= r % T else MASKED
    for m in range(GW):
        n = 2 * P - 1 - m
        c[bucket(n) if n >= 0 else BUCKETS, C_G + m] = 1.0
    c[:, C_SUM:C_SUM + P] = rows[:, None] % ROWS == rows[None, :] % ROWS
    second = (rows // ROWS == 1) & (rows // T % 2 == 1)
    c[:, C_VEC] = ~second
    c[:, C_VEC + 1] = second
    c[:, C_VEC + 3:C_VEC + 7] = np.arange(1, NBLK + 1)
    return c


def so_far(c, par, per):
    return (c + par) * (per // 2) + (0 if par else per)


def first(i):
    return isinstance(i, int) and i == 0


def early(c):
    return isinstance(c, int) and c < 2


class Tally:

    def __init__(self, sem):
        self.sem, self.n, self.base = sem, 0, 0

    def add(self, ins):
        ins.then_inc(self.sem, 1)
        self.n += 1

    def wait(self, eng):
        eng.wait_ge(self.sem, self.base + self.n)

    def enter(self, i, first, per):
        self.start, self.per = self.n, per
        self.base, self.n = (i - first) * per + self.n, 0

    def leave(self, times):
        assert self.n == self.per, (self.n, self.per)
        self.base, self.n = 0, self.start + times * self.per


def build(nc, a, out):
    with ExitStack() as ctx:
        def sb(name, shape, dt=F32):
            return ctx.enter_context(nc.sbuf_tensor(name, shape, dt))

        def sem(name):
            return ctx.enter_context(nc.semaphore(name))

        ps = ctx.enter_context(nc.psum_tensor("ps", [P, 8, 512], F32))
        con = sb("con", [P, C_ALL])
        ones = sb("ones", [P, P])
        xT = sb("xT", [P, DT, TOK])
        hT = sb("hT", [P, DT, TOK])
        oT = sb("oT", [P, 8, TOK])
        wbuf = sb("wbuf", [P, 2, 4096])
        arena_q = sb("arena_q", [P, 24 * TOK])
        vnat = sb("vnat", [P, 3, 2, WID])
        at_v = nc.sbuf_base
        arena_v = sb("arena_v", [P, 8192])
        at_k = nc.sbuf_base
        arena_k = sb("arena_k", [P, 8192])
        at_s = nc.sbuf_base
        arena_s = sb("arena_s", [P, 6400])
        phi = nc.alloc_sbuf_tensor_at("phi", [P, 4, DT, P], F32R, offset=at_k)
        plo = nc.alloc_sbuf_tensor_at("plo", [P, 4, DT, P], F32R, offset=at_k + 16384)
        whi = nc.alloc_sbuf_tensor_at("whi", [P, 4, DT, P], F32R, offset=at_v)
        wlo = nc.alloc_sbuf_tensor_at("wlo", [P, 4, DT, P], F32R, offset=at_v + 16384)
        xhi = nc.alloc_sbuf_tensor_at("xhi", [P, DT, TOK], F32R, offset=at_s)
        xlo = nc.alloc_sbuf_tensor_at("xlo", [P, DT, TOK], F32R, offset=at_s + 4 * DT * TOK)
        bias_s = sb("bias_s", [P, 2, NPG, 32])
        ownS = sb("ownS", [P, DB, 2, NEW])
        qrep = sb("qrep", [P, 2, DB, 16, T])
        stats = sb("stats", [P, 256])
        gcol = sb("gcol", [P, DT, 3])
        vecs = sb("vecs", [4, D])
        relb = sb("relb", [P, HEADS])
        relm = sb("relm", [BUCKETS + 1, HEADS])
        pages = sb("pages", [1, DB * NPG], I32)
        small = sb("small", [P, 64])
        rr = sb("rr", [P, TOK])
        endbuf = sb("endbuf", [P, 2 * 4 * 18])

        ident = con[:, C_ID:C_ID + P]
        hot = con[:, C_HOT:C_HOT + 161]
        qkvT = arena_q[:, :].rearrange("p (m t) -> p m t", t=TOK)
        ffT = arena_q[:, 0:FT * TOK].rearrange("p (m t) -> p m t", t=TOK)
        gT = qkvT
        vals = arena_v[:, :].rearrange("p (k g n) -> p k g n", k=2, n=WID)
        pbias = arena_v[:, 0:HEADS * GW].rearrange("p (h n) -> p h n", n=GW)
        pS = arena_v[:, 4608:4608 + 4 * GW].rearrange("p (u n) -> p u n", n=GW)
        pPT = arena_v[:, 6144:6144 + 2 * GW].rearrange("p (u n) -> p u n", n=GW)
        pstat = arena_v[:, 6912:6912 + 16 * 8].rearrange("p (u n) -> p u n", n=8)
        sel = arena_v[:, 7040:7552].rearrange("p (v n) -> p v n", v=4)
        Qbd = arena_v[:, 7552:8064].rearrange("p (k b c) -> p k b c", k=8, c=8)
        keys = arena_k[:, :].rearrange("p (g n) -> p g n", g=NPG)
        kblocks = arena_k[:, :].rearrange("p (g k c i) -> p g k c i", g=NPG, k=2, i=32)
        mT = arena_k[:, 0:DT * TOK].rearrange("p (m t) -> p m t", t=TOK)
        ext = arena_k[:, 2304:2304 + 8 * EXT].rearrange("p (m t) -> p m t", t=EXT)
        cv = arena_k[:, 4784:4784 + 4 * 306].rearrange("p (m t) -> p m t", t=306)
        frow = arena_k[:, 6016:6016 + 2 * 512].rearrange("p (s n) -> p s n", s=2)
        fcol = arena_k[:, 7040:7040 + 80].rearrange("p (m n) -> p m n", n=20)
        ends = endbuf[:, :].rearrange("p (s q r) -> p s q r", s=2, q=4)
        cst = arena_k[:, 7120:7120 + 1024].rearrange("p (s n) -> p s n", s=2)
        Z = arena_s[:, 0:4160].rearrange("p (k n) -> p k n", k=2)
        S = arena_s[:, 4160:4736].rearrange("p (k n) -> p k n", k=2)
        PT = arena_s[:, 4736:5888].rearrange("p (e k g r) -> p e k g r", e=2, k=2, r=ROWS)
        On = arena_s[0:2 * ROWS, 5888:6400]
        smax = stats[:, 0:10].rearrange("p (k n) -> p k n", k=2)
        blocksum = stats[:, 10:14]
        allsum, pen = stats[:, 14:18], stats[:, 18:22]
        low, order, worst = stats[:, 22:23], stats[:, 23:27], stats[:, 27:28]
        fmax = stats[:, 28:38].rearrange("p (k n) -> p k n", k=2)
        rowmax, negmax = stats[:, 38:40], stats[:, 40:42]
        rowsum = stats[:, 224:228].rearrange("p (e k) -> p e k", e=2)
        owt = stats[0:2 * ROWS, 44:46]
        ownmax = stats[:, 46:62].rearrange("p (b k) -> p b k", k=2)
        mx = stats[0:10, 64:96]
        mxb = stats[0:10, 96:224].rearrange("p (j r) -> p j r", j=QUADS)
        xnat = arena_s[:, 0:3072].rearrange("p (t n) -> p t n", n=D)
        knat = arena_s[:, 2048:5120].rearrange("p (t k n) -> p t k n", t=3, n=WID)
        Wrel = arena_s[:, 5120:5376].rearrange("p (k n) -> p k n", k=2)
        Gsb = arena_s[0:HEADS, 5376:5376 + GW]
        lamv = arena_s[:, 5760:6016].rearrange("p (v n) -> p v n", v=4)
        ownb = arena_s[0:ROWS, 6016:6080].rearrange("p (k n) -> p k n", k=2)
        ynat = arena_s[:, 0:3072].rearrange("p (t n) -> p t n", n=D)
        dsq = arena_s[:, 0:4 * TOK].rearrange("p (m t) -> p m t", t=TOK)
        drr = arena_s[:, 1152:1152 + 4 * TOK].rearrange("p (m t) -> p m t", t=TOK)
        ztmp = arena_s[:, 2304:2304 + 2 * TOK].rearrange("p (s t) -> p s t", s=2)
        neglam, dgain = small[:, 0:1], small[:, 1:2]
        far = small[:, 14:16]
        rweight = small[:, 3:4]

        gdram = nc.dram_tensor("bias_lines", [HEADS, P, GW], F32, kind="Internal")

        x_in, con_in, small_in, pt_in, bias_in = (sem(n) for n in ("x_in", "con_in", "small_in", "pt_in", "bias_in"))
        w_in = [sem(f"w_in{s}") for s in range(2)]
        k_in = [[sem(f"k_in{kind}_{g}") for g in range(NPG)] for kind in range(2)]
        v_in = [sem(f"v_in{s}") for s in range(2)]
        f_in = [sem(f"f_in{s}") for s in range(2)]
        g_out, k_out, stored = sem("g_out"), sem("k_out"), sem("stored")
        cst_out = [sem(f"cst_out{s}") for s in range(2)]
        consts_set, set_up, set_pe, lam_summed, lam_exped = (
            sem(n) for n in ("consts_set", "set_up", "set_pe", "lam_summed", "lam_exped"))
        vec_own = Tally(sem("vec_own"))
        gated = sem("gated")
        x_turned, x_copied = sem("x_turned"), sem("x_copied")
        squared, summed, meaned, rooted, normed = (sem(n) for n in ("squared", "summed", "meaned", "rooted", "normed"))
        tile_ready = sem("tile_ready")
        in_taken, mix_taken, down_taken = sem("in_taken"), sem("mix_taken"), sem("down_taken")
        nat_ready, nat_taken = sem("nat_ready"), sem("nat_taken")
        q_scaled = sem("q_scaled")
        p_scores, p_biased, p_exped, p_probs = (sem(n) for n in ("p_scores", "p_biased", "p_exped", "p_probs"))
        p_turned, p_pt, p_mixed, p_taken = (sem(n) for n in ("p_turned", "p_pt", "p_mixed", "p_taken"))
        vec_p, edges_set = sem("p_maxima"), sem("edges_set")
        sel_set, q_laid, q_spread, z_cleared = sem("sel_set"), sem("q_laid"), sem("q_spread"), sem("z_cleared")
        q_copied, own_scored, own_done = sem("q_copied"), sem("own_scored"), sem("own_done")
        k_turned = [sem("k_turned_moba"), sem("k_turned_diff")]
        z_ready = sem("z_ready")
        half_scored = sem("half_scored")
        scored = sem("scored")
        stats_ready, stats_turned = sem("stats_ready"), sem("stats_turned")
        max_ready, max_turned, m_ready = sem("max_ready"), sem("max_turned"), sem("m_ready")
        s_exped, pt_ready, s_summed = sem("s_exped"), sem("pt_ready"), sem("s_summed")
        v_half_used = sem("v_half_used")
        v_used = sem("v_used")
        on_ready, o_turned, o_taken = sem("on_ready"), sem("o_turned"), sem("o_taken")
        d_squared, d_summed, d_meaned, d_rooted, d_done = (
            sem(n) for n in ("d_squared", "d_summed", "d_meaned", "d_rooted", "d_done"))
        f_turned, f_copied, ext_ready = sem("f_turned"), sem("f_copied"), sem("ext_ready")
        w_high, w_split = sem("w_high"), sem("w_split")
        p_high, p_split = sem("p_high"), sem("p_split")
        x_high, x_split = sem("x_high"), sem("x_split")
        conv_done, silu_done, ff_done = sem("conv_done"), sem("silu_done"), sem("ff_done")
        ends_packed, mask_set = sem("ends_packed"), sem("mask_set")
        c_turned, c_staged, half_used = sem("c_turned"), sem("c_staged"), sem("half_used")
        y_turned, y_copied_a, y_copied_v = sem("y_turned"), sem("y_copied_a"), sem("y_copied_v")

        W_GATE, W_O, W_OUT, W_UP = 16 * 3, (16 * 9, 16 * 7), (16 * 10, 16 * 8), (16 * 10, 16 * 8)
        PLACE = [8, 9, 10, 11, 20, 21, 22, 23, 0, 1, 2, 3, 4, 5, 6, 7]
        GATE_AT = {2: 0, 10: 1, 12: 2, 14: 3, 16: 4, 18: 5}
        T_GATE, T_OA, T_OB, T_OUT, T_UP, T_DOWN = 24, 40, 48, 56, 64, 108

        w_in_v = a["w_in"][0].rearrange("(k p) n -> p k n", p=P)
        w_gate_v = a["w_gate"][0].rearrange("(k p) n -> p k n", p=P)
        w_oa_v = a["w_out_a"][0].rearrange("(k p) n -> p k n", p=P)
        w_ob_v = a["w_out_b"][0].rearrange("(k p) n -> p k n", p=P)
        w_out_v = a["w_out"][0].rearrange("(k p) n -> p k n", p=P)
        w_up_v = a["w_up"][0].rearrange("(k p) (h n) -> p k h n", p=P, h=2)
        w_down_v = a["w_down"][0].rearrange("(k p) n -> p k n", p=P)

        def kpage(g, kind):
            return keys[:, g, kind * WID:kind * WID + WID]

        def slot8(s):
            return wbuf[:, s, :].rearrange("p (k n) -> p k n", k=8)

        def slot4(s):
            return wbuf[:, s, :].rearrange("p (k n) -> p k n", k=4)

        def slot_gate(s):
            return wbuf[:, s, 0:2048].rearrange("p (k n) -> p k n", k=8)

        def slot_up(s, h):
            return wbuf[:, s, 2048 * h:2048 * h + 2048].rearrange("p (k n) -> p k n", k=8)

        def up_weights(s, q):
            return slot_up(s, q // 2)[:, :, (q % 2) * P:(q % 2) * P + P]

        def slot11(s):
            return wbuf[:, s, 0:11 * 256].rearrange("p (k n) -> p k n", k=11)

        block = ctx.enter_context(nc.Block())

        @block.sync
        def _(sp):
            for n, (t0, cnt) in enumerate(TOKENS):
                src = a["x_prompt"][0][t0:t0 + cnt] if n < 2 else a["x_sample"].rearrange("b t n -> (b t) n")
                sp.dma_start(xnat[0:cnt, n, :], src).then_inc(x_in, 16)
            sp.dma_start(con[:, :], a["constants"]).then_inc(con_in, 16)
            sp.dma_start(vecs[0:1, :], a["norm_attn"]).then_inc(small_in, 16)
            sp.dma_start(vecs[1:2, :], a["norm_ffn"]).then_inc(small_in, 16)
            sp.dma_start(vecs[2:3, :], a["norm_final"].rearrange("(o n) -> o n", o=1)).then_inc(small_in, 16)
            for t in range(T):
                sp.dma_start(relb[32 * t:32 * t + 32, :], a["rel_bias"]).then_inc(small_in, 16)
            sp.dma_start(relm[0:BUCKETS, :], a["rel_bias"]).then_inc(small_in, 16)
            sp.dma_start(small[:, 4:5], a["diff_norm"].rearrange("o n -> n o")).then_inc(small_in, 16)
            for n, name in enumerate(("lambda_q1", "lambda_k1", "lambda_q2", "lambda_k2")):
                sp.dma_start(lamv[:, n, :], a[name].broadcast_to([P, HD])).then_inc(small_in, 16)
            sp.dma_start(pages[:, :], a["page_table"].rearrange("(o b) g -> o (b g)", o=1)).then_inc(pt_in, 16)
            sp.wait_ge(set_up, 2)
            sp.dma_start(gdram[:, :, :], Gsb.unsqueeze(1).broadcast_to([HEADS, P, GW])).then_inc(g_out, 16)
            sp.wait_ge(g_out, 16)
            g = gdram[:, :, :]
            sp.dma_start(pbias[:, :, 0:256], bass.AP(g.tensor, P - 1, [[GW - 1, P], [P * GW, HEADS], [1, 256]])
                         ).then_inc(bias_in, 16)
            sp.dma_start(pbias[:, :, 256:384], bass.AP(g.tensor, 2 * P - 1, [[GW - 1, P], [P * GW, HEADS], [1, P]])
                         ).then_inc(bias_in, 16)
            sp.wait_ge(pt_in, 16)

            def page_id(entry):
                return sp.value_load(pages[0:1, bass.ds(entry, 1)], min_val=0, max_val=NPHYS - 1)

            def page(name, pg):
                return a[name][0].rearrange("g p h n -> g p (h n)")[bass.ds(pg, 1)].rearrange("o p n -> (o p) n")

            def load_k(b):
                ids = [page_id(b * NPG + g) for g in range(NPG)]
                for kind, name in enumerate(("cache_moba_k", "cache_diff_k")):
                    for g in range(NPG):
                        if g == 0 and not first(b):
                            sp.wait_ge((half_scored, scored)[kind], b)
                        sp.dma_start(kpage(g, kind), page(name, ids[g])).then_inc(k_in[kind][g], 16)

            def load_v(b):
                for g in range(NPG):
                    pg = page_id(b * NPG + g)
                    if g == 0 and not first(b):
                        sp.wait_ge(v_used, b)
                    for kind, name in enumerate(("cache_moba_v", "cache_diff_v")):
                        sp.dma_start(vals[:, kind, g, :], page(name, pg)).then_inc(v_in[kind], 16)

            sp.wait_ge(tile_ready, T_GATE)
            load_k(0)
            load_k(1)
            sp.wait_ge(p_taken, 8)
            load_v(0)
            with sp.Fori(1, LAST) as b:
                load_k(b + 1)
                load_v(b)
            ids = [page_id(LAST * NPG + g) for g in range(NPG)]
            for kind, name in enumerate(("cache_moba_v", "cache_diff_v")):
                sp.wait_ge((v_half_used, v_used)[kind], LAST)
                for g in range(NPG):
                    sp.dma_start(vals[:, kind, g, :], page(name, ids[g])).then_inc(v_in[kind], 16)

            def conv_rows(c, par):
                for r0, src in ((0, a["state_conv"][0].rearrange("b r n -> (b r) n")),
                                (16, a["conv_w"][0]), (19, a["conv_b"])):
                    rows = src.shape[0]
                    for h in range(2):
                        sp.dma_start(frow[r0:r0 + rows, par, h * 256:h * 256 + 256],
                                     src[:, bass.ds(c * 256 + h * FF, 256)]).then_inc(f_in[par], 16)

            sp.wait_ge(scored, DB)
            conv_rows(0, 0)
            conv_rows(1, 1)
            sp.wait_ge(f_turned, 1)
            conv_rows(2, 0)
            with sp.Fori(1, 5) as i:
                for c, par in ((2 * i + 1, 1), (2 * i + 2, 0)):
                    sp.wait_ge(f_turned, c - 1)
                    conv_rows(c, par)

        @block.gpsimd
        def _(pool):
            nc.gpsimd.memset(ones[:, :], 1.0).then_inc(consts_set, 1)
            nc.gpsimd.memset(Qbd[:, :, :, :], 0.0).then_inc(consts_set, 1)
            nc.gpsimd.memset(ownS[:, :, :, :], MASKED).then_inc(consts_set, 1)
            nc.gpsimd.memset(ownmax[:, :, :], LOWEST).then_inc(consts_set, 1)

            def lower_stream(use):
                for j in range(DT):
                    pool.wait_ge(x_high, DT * use + j + 1)
                    nc.gpsimd.tensor_tensor(xlo[:, j, :], hT[:, j, :], xhi[:, j, :].bitcast(F32), ALU.subtract
                                            ).then_inc(x_split, 1)

            lower_stream(0)
            for g in range(12):
                kind, tt = divmod(g, 3)
                pool.wait_ge(nat_taken, g + 1)
                src = (knat if kind < 2 else vnat)[0:TOKENS[tt][1], tt, kind % 2, :]
                name = ("moba_k", "diff_k", "moba_v", "diff_v")[kind]
                if tt < 2:
                    dst = out[name + "_prompt"][0, 0, tt * P:tt * P + P].rearrange("t h n -> t (h n)")
                else:
                    dst = out[name + "_sample"][0].rearrange("b t h n -> (b t) (h n)")
                pool.dma_start(dst, src).then_inc(k_out if kind < 2 else stored, 16)

            pool.wait_ge(k_out, 16 * 6)
            nc.gpsimd.memset(Z[:, :, :], 0.0).then_inc(z_cleared, 1)

            def conv_store(c, par):
                pool.wait_ge(c_staged, c + 1)
                for h in range(2):
                    cols = slice(h * 256, h * 256 + 256)
                    for part, dst in ((cst[0:2, par, cols], out["conv_prompt"][0, 0]),
                                      (cst[2:18, par, cols], out["conv_sample"][0].rearrange("b r n -> (b r) n"))):
                        pool.dma_start(dst[:, bass.ds(c * 256 + h * FF, 256)], part).then_inc(cst_out[par], 16)

            lower_stream(1)
            for c in range(3):
                conv_store(c, c % 2)
            with pool.Fori(1, 5) as i:
                conv_store(2 * i + 1, 1)
                conv_store(2 * i + 2, 0)
            for n, (t0, cnt) in enumerate(TOKENS):
                pool.wait_ge(y_copied_a, n + 1)
                pool.wait_ge(y_copied_v, n + 1)
                dst = out["y_prompt"][0][t0:t0 + cnt] if n < 2 else out["y_sample"].rearrange("b t n -> (b t) n")
                pool.dma_start(dst, ynat[0:cnt, n, :]).then_inc(stored, 16)
            pool.wait_ge(stored, 16 * 9)
            pool.wait_ge(cst_out[0], 64 * 6)
            pool.wait_ge(cst_out[1], 64 * 5)

        @block.tensor
        def _(pe):
            mm, turn = nc.tensor.matmul, nc.tensor.transpose

            def sum_of_squares(use):
                for j in range(DT):
                    pe.wait_ge(squared, DT * use + j + 1)
                    last = mm(ps[:, 7, 0:TOK], ones[:, :], hT[:, j, :], start=(j == 0), stop=(j == DT - 1))
                last.then_inc(summed, 1)

            def tile(bank, weights, moving, opens=True, stop=True, after=None, signal=normed):
                for k, (w, x) in enumerate(zip(weights, moving)):
                    if after is not None:
                        pe.wait_ge(signal, after + k + 1)
                    last = mm(ps[:, bank, 0:TOK], w, x, start=(opens and k == 0),
                              stop=(stop and k == len(moving) - 1))
                return last

            pe.wait_ge(x_in, 48)
            pe.wait_ge(con_in, 16)
            for j in range(DT):
                if j >= 4:
                    pe.wait_ge(x_copied, j - 3)
                for n, (t0, cnt) in enumerate(TOKENS):
                    last = turn(ps[:, j % 4, t0:t0 + cnt], xnat[0:cnt, n, j * P:j * P + P], ident[0:cnt, 0:cnt])
                last.then_inc(x_turned, 1)
            pe.wait_ge(consts_set, 4)
            sum_of_squares(0)
            def split_tile(q, high, low, after):
                for k in range(DT):
                    if after is not None:
                        pe.wait_ge(x_split, after + k + 1)
                    mm(ps[:, q, 0:TOK], high[:, q, k, :], xhi[:, k, :], start=(k == 0), stop=False)
                    mm(ps[:, q, 0:TOK], high[:, q, k, :], xlo[:, k, :], start=False, stop=False)
                    last = mm(ps[:, q, 0:TOK], low[:, q, k, :], xhi[:, k, :], start=False, stop=(k == DT - 1))
                return last

            pe.wait_ge(small_in, 16 * 13)
            pe.wait_ge(mask_set, 1)
            for j in range(DT):
                last = turn(ps[:, 4, 4 * j:4 * j + 3], vecs[0:3, j * P:j * P + P], ident[0:3, 0:3])
            last.then_inc(set_pe, 1)
            mm(ps[0:HEADS, 5, 0:GW], relm[:, :], con[0:BUCKETS + 1, C_G:C_G + GW], start=True, stop=True
               ).then_inc(set_pe, 1)
            pe.wait_ge(set_up, 4)
            for kind in range(2):
                last = mm(ps[:, 6, 256 * kind:256 * kind + 161], Wrel[:, kind, :], hot, start=True, stop=True)
            last.then_inc(set_pe, 1)

            h = [hT[:, k, :] for k in range(DT)]
            with pe.Fori(0, 3) as i:
                for s in range(2):
                    for q in range(4):
                        pe.wait_ge(in_taken, i * 8 + (4 * s + q + 1))
                        pe.wait_ge(p_split, i * 8 + (4 * s + q + 1))
                        split_tile(q, phi, plo, 0 if s == q == 0 else None).then_inc(tile_ready, 1)

            pe.wait_ge(set_up, SET_UP)
            for g in range(12):
                kind, tt = divmod(g, 3)
                m0 = (4, 16, 8, 20)[kind]
                t0, cnt = TOKENS[tt]
                pe.wait_ge(in_taken, 4 + m0 + 4)
                if g >= 2:
                    pe.wait_ge(nat_taken, g - 1)
                for q in range(4):
                    last = turn(ps[0:cnt, 4 + g % 2, q * P:q * P + P], qkvT[:, m0 + q, t0:t0 + cnt], ident)
                last.then_inc(nat_ready, 1)

            pe.wait_ge(q_laid, 4)
            pe.wait_ge(sel_set, 1)
            for kind in range(2):
                for n in range(4):
                    last = mm(ps[:, 6 + kind, n * P:n * P + P], sel[:, n, :],
                              qkvT[:, 12 * kind:12 * kind + 4, SEQ:TOK], start=True, stop=True)
            last.then_inc(q_spread, 1)
            pe.wait_ge(nat_taken, 12)
            own = ps[0:NEW, 4, :].rearrange("r (b k c) -> r b k c", b=DB, c=8)
            for k in range(8):
                last = mm(own[:, :, k, :], qkvT[:, 12 * (k // 4) + 4 + k % 4, SEQ:TOK], Qbd[:, k, :, :],
                          start=True, stop=True)
            last.then_inc(own_scored, 1)

            def p_score(u):
                kind, p, hh = u // 8, u % 8 // 2, u % 2
                q0, k0, rows = 12 * kind + p, 12 * kind + 4 + p, slice(64 * hh, 64 * hh + 64)
                if u >= 2:
                    pe.wait_ge(p_biased, 2 * (u - 1))
                mm(ps[:, 1 + u % 2, 0:256], qkvT[rows, q0, P:2 * P], qkvT[rows, k0, 0:256], start=True, stop=True)
                mm(ps[:, 1 + u % 2, 256:384], qkvT[rows, q0, 0:P], qkvT[rows, k0, 0:P], start=True, stop=True
                   ).then_inc(p_scores, 1)

            def p_turn(v):
                u = RESULT[v]
                pe.wait_ge(p_probs, 2 * (v + 1))
                if v >= 2:
                    pe.wait_ge(p_pt, v - 1)
                b = 3 + v % 2
                turn(ps[:, b, 0:P], pS[:, u % 4, 256:384], ident)
                turn(ps[:, b, P:2 * P], pS[:, u % 4, 0:P], ident)
                turn(ps[:, b, 2 * P:3 * P], pS[:, u % 4, P:2 * P], ident).then_inc(p_turned, 1)

            def p_mix(v):
                kind, o = v // 8, (v // 2 if v < 8 else v - 4)
                if kind == 0:
                    rows, cols = slice(64 * (v % 2), 64 * (v % 2) + 64), slice(HD * v, HD * v + HD)
                else:
                    rows, cols = slice(0, P), slice(P * (v - 8), P * (v - 8) + P)
                if o >= 2 and (kind == 1 or v % 2 == 0):
                    pe.wait_ge(p_taken, o - 1)
                pe.wait_ge(p_pt, v + 1)
                b = 5 + o % 2
                mm(ps[rows, b, 0:256], vnat[:, 0, kind, cols], pPT[:, v % 2, 0:256], start=True, stop=False)
                mm(ps[rows, b, P:256], vnat[:, 1, kind, cols], pPT[:, v % 2, 256:384], start=False, stop=True
                   ).then_inc(p_mixed, 1)

            pe.wait_ge(in_taken, 4 + 24)
            def s_keys(b, kinds=(0, 1)):
                pe.wait_ge(z_ready, b * 8 + 8)
                for kind in kinds:
                    pe.wait_ge(k_turned[kind], b * NPG + NPG)
                    for n in range(16):
                        c0 = 128 * n
                        last = mm(ps[:, 0, HALF * kind:HALF * kind + HALF], Z[:, kind, c0:c0 + P],
                                  kblocks[:, :, kind, n, :], start=(n == 0), stop=(n == 15))
                    last.then_inc((half_scored, scored)[kind], 1)

            def s_stats(b):
                pe.wait_ge(stats_ready, b + 1)
                mm(ps[:, 1, 0:NBLK], con[:, C_SUM:C_SUM + P], blocksum, start=True, stop=True)
                turn(ps[0:10, 1, P:2 * P], smax.rearrange("p k n -> p (k n)"), ident).then_inc(stats_turned, 1)

            def s_maxima(b):
                pe.wait_ge(max_ready, b + 1)
                mm(ps[:, 1, 256:266], mxb.rearrange("p j r -> p (j r)"), ident[0:10, 0:10], start=True, stop=True
                   ).then_inc(max_turned, 1)

            def s_sums(b, e):
                if not first(b):
                    pe.wait_ge(o_taken, b * 4)
                pe.wait_ge(s_exped, b * 2 + 2)
                for kind in range(2):
                    last = mm(ps[ROWS * kind:ROWS * kind + ROWS, 3, 400:402], con[:, C_SUM:C_SUM + ROWS], rowsum[:, e],
                              start=True, stop=True)
                last.then_inc(s_summed, 1)
                pe.wait_ge(pt_ready, b + 1)

            def s_values(b, e, kinds=(0, 1)):
                for kind in kinds:
                    o = ps[ROWS * kind:ROWS * kind + ROWS, 2, :]
                    pe.wait_ge(v_in[kind], b * P + P)
                    for g in range(NPG):
                        mm(o, PT[:, e, kind, g, :], vals[:, kind, g, :], start=(g == 0), stop=False)
                    last = mm(o, PT[0:NEW, e, kind, NPG, :], vnat[0:NEW, 2, kind, :], start=False, stop=True)
                    last.then_inc((v_half_used, v_used)[kind], 1)

            def s_turn_out(b):
                pe.wait_ge(on_ready, b + 1)
                for p in range(4):
                    last = mm(ps[:, 3, 64 * p:64 * p + 64], On[:, p * P:p * P + P], ident[0:64, 0:64],
                              start=True, stop=True)
                last.then_inc(o_turned, 1)

            def s_step(b, e):
                s_keys(b + 1, (0,))
                if not first(b):
                    s_turn_out(b - 1)
                s_keys(b + 1, (1,))
                s_sums(b, e)
                s_values(b, e, (0,))
                s_stats(b + 1)
                pe.wait_ge(in_taken, b + (4 + T_GATE + 6))
                q = 1 - e
                if not first(b):
                    pe.wait_ge(w_in[0], (b + e) * 8 + (W_GATE + 32))
                tile(5 - e, [slot_gate(1 if first(b) else 0)[:, k, q * P:q * P + P] for k in range(DT)], h
                     ).then_inc(tile_ready, 1)
                s_maxima(b + 1)
                s_values(b, e, (1,))

            for u in range(16 + 3):
                if u < 16:
                    p_score(u)
                if u == 2:
                    pe.wait_ge(q_copied, 2)
                if u == 3:
                    pe.wait_ge(own_done, 1)
                if u - 2 in RESULT:
                    p_turn(RESULT.index(u - 2))
                if u - 3 in RESULT:
                    p_mix(RESULT.index(u - 3))
                if u in GATE_AT:
                    m = GATE_AT[u]
                    pe.wait_ge(w_in[m // 2 % 2], W_GATE + 16 * (m // 4 + 1))
                    pe.wait_ge(in_taken, 4 + T_GATE + m)
                    tile(7, [slot_gate(m // 2 % 2)[:, k, m % 2 * P:m % 2 * P + P] for k in range(DT)], h
                         ).then_inc(tile_ready, 1)
                if u in (5, 8):
                    s_keys(0, (u // 8,))

            pe.wait_ge(p_taken, 8)
            s_stats(0)
            pe.wait_ge(w_in[1], W_GATE + 32)
            tile(4, [slot_gate(1)[:, k, 0:P] for k in range(DT)], h).then_inc(tile_ready, 1)
            s_maxima(0)
            s_step(0, 0)
            with pe.Fori(0, 3) as i:
                s_step(2 * i + 1, 1)
                s_step(2 * i + 2, 0)
            pe.wait_ge(w_in[1], W_GATE + 48)
            for q in range(2):
                pe.wait_ge(in_taken, 4 + T_GATE + 13 + q)
                tile(4 + q, [slot_gate(1)[:, k, q * P:q * P + P] for k in range(DT)], h).then_inc(tile_ready, 1)
            s_turn_out(LAST - 1)
            s_sums(LAST, 1)
            s_values(LAST, 1)
            s_turn_out(LAST)
            pe.wait_ge(o_taken, 4 * DB)
            for kind in range(2):
                pe.wait_ge(w_in[kind], W_O[kind])
                for m in range(DT):
                    if kind == 0 and m == 2:
                        pe.wait_ge(in_taken, 4 + T_OA)
                        pe.wait_ge(d_squared, 1)
                        for n in range(4):
                            last = mm(ps[:, 4 + n, 0:TOK], ones[:, :], dsq[:, n, :], start=True, stop=True)
                        last.then_inc(d_summed, 1)
                    if 8 * kind + m >= 4:
                        pe.wait_ge(mix_taken, 8 * kind + m - 3)
                    tile(m % 4, [slot4(kind)[:, k, m * P:m * P + P] for k in range(4)],
                         [oT[:, 4 * kind + k, :] for k in range(4)],
                         after=0 if kind == 1 and m == 0 else None, signal=d_done).then_inc(tile_ready, 1)
            pe.wait_ge(mix_taken, 16)
            for m in range(DT):
                s = m // 4
                if m % 4 == 0:
                    pe.wait_ge(w_in[s], W_OUT[s])
                pe.wait_ge(mix_taken, 16 + max(m - 3, 0))
                tile(m % 4, [slot8(s)[:, k, (m % 4) * P:(m % 4) * P + P] for k in range(DT)],
                     [mT[:, k, :] for k in range(DT)]).then_inc(tile_ready, 1)
            sum_of_squares(1)

            def state_turn(c, par):
                pe.wait_ge(ends_packed, c + 1)
                if not early(c):
                    pe.wait_ge(c_staged, c - 1)
                for q in range(4):
                    last = turn(ps[0:18, 5 + par, q * P:q * P + P], ends[:, par, q, :], ident)
                last.then_inc(c_turned, 1)

            def up(c, par):
                pe.wait_ge(f_in[par], so_far(c, par, 96))
                if not first(c):
                    pe.wait_ge(f_copied, c)
                for q in range(4):
                    last = mm(ps[:, 4, 20 * q:20 * q + 20], frow[0:20, par, q * P:q * P + P], ident[0:20, 0:20],
                              start=True, stop=True)
                last.then_inc(f_turned, 1)
                for q in range(4):
                    if not first(c):
                        pe.wait_ge(ext_ready, c * 8 + 2 * (q - 3))
                    pe.wait_ge(w_split, c * 4 + q + 1)
                    split_tile(q, whi, wlo, DT if first(c) and q == 0 else None).then_inc(tile_ready, 1)

            pe.wait_ge(mix_taken, 24)
            up(0, 0)
            up(1, 1)
            state_turn(0, 0)
            up(2, 0)
            state_turn(1, 1)
            with pe.Fori(1, 5) as i:
                up(2 * i + 1, 1)
                state_turn(2 * i, 0)
                up(2 * i + 2, 0)
                state_turn(2 * i + 1, 1)
            state_turn(10, 0)

            with pe.Fori(0, 2) as i:
                for e in range(2):
                    for half in range(2):
                        pe.wait_ge(ff_done, 22 if half else 12)
                        s = 1 - half
                        pe.wait_ge(w_in[s], i * 32 + (W_UP[s] + 32 * (5 + half) + 16 * (e + 1)))
                        for q in range(2):
                            if half == 0:
                                pe.wait_ge(down_taken, i * 4 + (2 * e + q + 1))
                            last = tile(2 * e + q, [slot11(s)[:, k, q * P:q * P + P] for k in range(11)],
                                        [ffT[:, 11 * half + k, :] for k in range(11)], half == 0, half == 1)
                            if half == 1:
                                last.then_inc(tile_ready, 1)
                        if half == 0:
                            last.then_inc(half_used, 1)
            sum_of_squares(2)

            for g in range(6):
                n, half = divmod(g, 2)
                t0, cnt = TOKENS[n]
                if g >= 4:
                    pe.wait_ge((y_copied_a, y_copied_v)[half], n - 1)
                for q in range(4):
                    if n == 0:
                        pe.wait_ge(normed, 2 * DT + 4 * half + q + 1)
                    last = turn(ps[0:cnt, g % 4, q * P:q * P + P], hT[:, 4 * half + q, t0:t0 + cnt], ident)
                last.then_inc(y_turned, 1)

        @block.scalar
        def _(act):
            fn, copy = nc.scalar.activation, nc.scalar.copy

            def load(s, dst, src):
                act.dma_start(dst, src).then_inc(w_in[s], 16)

            def load_up(c, par):
                for hlf in range(2):
                    src = w_up_v[:, :, hlf, :][:, :, bass.ds(c * 256, 256)]
                    act.dma_start(slot_up(par, hlf), src).then_inc(w_in[par], 16)

            def upper_part(c, par, q):
                if q == 0:
                    act.wait_ge(w_in[par], W_UP[par] + so_far(c, par, 32))
                if not first(c):
                    act.wait_ge(tile_ready, c * 4 + (T_UP - 4 + q + 1))
                copy(whi[:, q], up_weights(par, q)).then_inc(w_high, 1)

            def root(use):
                act.wait_ge(meaned, use + 1)
                fn(rr[:, :], rr[:, :], ACT.Sqrt).then_inc(rooted, 1)

            act.wait_ge(x_in, 48)
            act.wait_ge(small_in, 16 * 13)
            load(0, slot8(0), w_in_v[:, :, 0:512])
            load(1, slot8(1), w_in_v[:, :, 512:1024])
            for j in range(DT):
                act.wait_ge(x_turned, j + 1)
                fn(hT[:, j, :], ps[:, j % 4, 0:TOK], ACT.Square).then_inc(squared, 1)
                copy(xT[:, j, :], ps[:, j % 4, 0:TOK]).then_inc(x_copied, 1)
            act.wait_ge(lam_summed, 2)
            fn(small[:, 10:12], small[:, 8:10], ACT.Exp).then_inc(lam_exped, 1)
            root(0)
            act.sem_inc(in_taken, 4)

            def upper_in(n, q):
                if q == 0:
                    act.wait_ge(w_in[n % 2], 16 * (n // 2 + 1))
                if n >= 1:
                    act.wait_ge(tile_ready, 4 * (n - 1) + q + 1)
                copy(phi[:, q], slot8(n % 2)[:, :, q * P:q * P + P]).then_inc(p_high, 1)

            upper_in(0, 0)
            for j in range(DT):
                act.wait_ge(normed, j + 1)
                copy(xhi[:, j, :], hT[:, j, :]).then_inc(x_high, 1)
            for q in range(1, 4):
                upper_in(0, q)
            act.wait_ge(p_split, 4)
            load(0, slot8(0), w_in_v[:, :, 2 * 512:3 * 512])
            for n in range(6):
                for q in range(4):
                    act.wait_ge(tile_ready, n * 4 + q + 1)
                    copy(qkvT[:, 4 * n + q, :], ps[:, q, 0:TOK]).then_inc(in_taken, 1)
                    if n < 5:
                        upper_in(n + 1, q)
                s = (n + 1) % 2
                if n < 5:
                    act.wait_ge(p_split, 4 * (n + 2))
                if n < 3:
                    load(s, slot8(s), w_in_v[:, :, (n + 3) * 512:(n + 4) * 512])
                elif n < 5:
                    load(s, slot_gate(s), w_gate_v[:, :, (n - 3) * 256:(n - 2) * 256])

            def p_exp(u):
                act.wait_ge(p_biased, 2 * u + 2)
                act.wait_ge(vec_p, u + 1)
                fn(pS[:, u % 4, 0:256], pS[:, u % 4, 0:256], ACT.Exp, bias=pstat[:, u, 2:3],
                   accum_out=pstat[:, u, 4:5]).then_inc(p_exped, 1)
                fn(pS[:, u % 4, 256:384], pS[:, u % 4, 256:384], ACT.Exp, bias=pstat[:, u, 3:4],
                   accum_out=pstat[:, u, 5:6]).then_inc(p_exped, 1)

            def p_copy(v):
                act.wait_ge(p_turned, v + 1)
                if v >= 2:
                    act.wait_ge(p_mixed, v - 1)
                copy(pPT[:, v % 2, :], ps[:, 3 + v % 2, 0:GW]).then_inc(p_pt, 1)

            def take_gate(m, bank):
                copy(gT[:, m, :] if isinstance(m, int) else gT[:, bass.ds(m, 1), :].rearrange("p o t -> p (o t)"),
                     ps[:, bank, 0:TOK]).then_inc(in_taken, 1)

            def load_gates(n, s):
                load(s, slot_gate(s), w_gate_v[:, :, bass.ds(n * 256, 256)])

            for u in range(16 + 3):
                if u < 16:
                    p_exp(u)
                if u - 2 in RESULT:
                    p_copy(RESULT.index(u - 2))
                if u in GATE_AT:
                    m = GATE_AT[u]
                    act.wait_ge(tile_ready, T_GATE + m + 1)
                    take_gate(PLACE[m], 7)
                    if m % 2 == 1:
                        load_gates(m // 2 + 2, m // 2 % 2)

            def s_exp(b, e):
                act.wait_ge(m_ready, b * 2 + 2)
                for kind in range(2):
                    fn(S[:, kind, :], S[:, kind, :], ACT.Exp, bias=negmax[:, kind:kind + 1],
                       accum_out=rowsum[:, e, kind:kind + 1]).then_inc(s_exped, 1)

            def gate(b, e):
                act.wait_ge(tile_ready, b + (T_GATE + 8))
                take_gate(b - 1, 5 - e)

            s_exp(0, 0)
            for m in (6, 7):
                act.wait_ge(tile_ready, T_GATE + m + 1)
                take_gate(PLACE[m], m - 2)
            load_gates(7, 1)
            s_exp(1, 1)
            with act.Fori(0, 2) as i:
                gate(2 * i + 1, 1)
                s_exp(2 * i + 2, 0)
                gate(2 * i + 2, 0)
                load_gates(i + 5, 0)
                s_exp(2 * i + 3, 1)
            gate(5, 1)
            s_exp(6, 0)
            gate(6, 0)
            s_exp(7, 1)
            for m in (14, 15):
                act.wait_ge(tile_ready, T_GATE + m + 1)
                take_gate(PLACE[m], m - 10)
            act.wait_ge(v_in[1], P * DB)
            load(0, slot4(0), w_oa_v)
            load(1, slot4(1), w_ob_v)
            act.wait_ge(in_taken, 4 + T_OA)
            for m0, m1 in ((8, 12), (20, 24), (0, 8)):
                fn(gT[:, m0:m1, :], gT[:, m0:m1, :], ACT.Sigmoid).then_inc(gated, 1)

            act.wait_ge(o_taken, 4 * DB)
            fn(dsq[:, :, :], oT[:, 4:8, :], ACT.Square).then_inc(d_squared, 1)
            act.wait_ge(d_meaned, 1)
            fn(drr[:, :, :], drr[:, :, :], ACT.Sqrt).then_inc(d_rooted, 1)
            act.wait_ge(tile_ready, T_OB)
            load(0, slot8(0), w_out_v[:, :, 0:512])
            act.wait_ge(tile_ready, T_OUT)
            load(1, slot8(1), w_out_v[:, :, 512:1024])
            act.wait_ge(tile_ready, T_OUT + 4)
            load_up(0, 0)
            for j in range(DT):
                if j >= 4:
                    upper_part(0, 0, j - 4)
                act.wait_ge(mix_taken, 16 + j + 1)
                fn(hT[:, j, :], xT[:, j, :], ACT.Square).then_inc(squared, 1)
            load_up(1, 1)
            root(1)
            act.wait_ge(w_split, 4)
            load_up(2, 0)
            for j in range(DT):
                act.wait_ge(normed, DT + j + 1)
                copy(xhi[:, j, :], hT[:, j, :]).then_inc(x_high, 1)

            def take_up(c, par, more=True):
                for q in range(4):
                    act.wait_ge(tile_ready, c * 4 + T_UP + q + 1)
                    if q == 0 and not early(c):
                        act.wait_ge(conv_done, (c - 1) * 4)
                    e = ext[:, 4 * par + q, :]
                    copy(e[:, 2:258], ps[:, q, 0:SEQ]).then_inc(ext_ready, 1)
                    copy(e[:, 258:306].rearrange("p (b r) -> p b r", r=6)[:, :, 2:6],
                         ps[:, q, SEQ:TOK].rearrange("p (b t) -> p b t", t=T)).then_inc(ext_ready, 1)
                    if more:
                        upper_part(c + 1, 1 - par, q)
                if more:
                    act.wait_ge(w_split, c * 4 + 8)

            def silu(c):
                act.wait_ge(conv_done, c * 4 + 4)
                fn(cv[:, 0:2, 0:CONV], cv[:, 0:2, 0:CONV], ACT.Silu).then_inc(silu_done, 1)

            act.wait_ge(edges_set, 1)
            for c in range(3):
                take_up(c, c % 2)
                load_up(c + 3, 1 - c % 2)
                silu(c)
            with act.Fori(1, 3) as i:
                for c, par in ((2 * i + 1, 1), (2 * i + 2, 0)):
                    take_up(c, par)
                    load_up(c + 3, 1 - par)
                    silu(c)
            take_up(7, 1)
            load_up(10, 0)
            silu(7)
            for c in (8, 9):
                take_up(c, c % 2)
                load(1 - c % 2, slot11(1 - c % 2), w_down_v[:, 11 * (c - 8):11 * (c - 8) + 11, 0:256])
                silu(c)
            take_up(10, 0, False)
            silu(10)
            with act.Fori(0, 3) as d:
                for half, s in ((0, 1), (1, 0)):
                    if half == 0:
                        act.wait_ge(half_used, d + 1)
                    else:
                        act.wait_ge(tile_ready, d * 2 + T_DOWN + 2)
                    load(s, slot11(s), w_down_v[:, 11 * half:11 * half + 11, bass.ds((d + 1) * 256, 256)])
            for j in range(DT):
                act.wait_ge(down_taken, 4 + j + 1)
                fn(hT[:, j, :], xT[:, j, :], ACT.Square).then_inc(squared, 1)
            root(2)
            for n, (t0, cnt) in enumerate(TOKENS):
                act.wait_ge(y_turned, 2 * n + 1)
                copy(ynat[0:cnt, n, 0:512], ps[0:cnt, 2 * n % 4, :]).then_inc(y_copied_a, 1)

        @block.vector
        def _(dve):
            v = nc.vector

            def own(ins):
                vec_own.add(ins)
                vec_own.wait(dve)

            v.memset(relm[BUCKETS:BUCKETS + 1, :], MASKED).then_inc(mask_set, 1)
            dve.wait_ge(set_pe, 1)
            v.tensor_copy(gcol[:, :, :], ps[:, 4, 0:32].rearrange("p (j c) -> p j c", c=4)[:, :, 0:3]).then_inc(set_up, 1)
            dve.wait_ge(set_pe, 2)
            v.tensor_copy(Gsb, ps[0:HEADS, 5, 0:GW]).then_inc(set_up, 1)
            W6 = Wrel.rearrange("p k (j h t) -> p k j h t", j=QUADS, t=T)
            M6 = con[:, C_TM:C_TM + P].rearrange("p (j q c t) -> p j q c t", j=QUADS, q=4, t=T)
            v.tensor_tensor(W6[:, 0], relb[:, 0:8].unsqueeze(1).unsqueeze(3).broadcast_to([P, QUADS, 8, T]),
                            M6.rearrange("p j q c t -> p j (q c) t"), ALU.mult).then_inc(set_up, 1)
            v.tensor_tensor(Wrel[:, 1, :].rearrange("p (j q n) -> p j q n", j=QUADS, q=4),
                            relb[:, 8:12].unsqueeze(1).unsqueeze(3).broadcast_to([P, QUADS, 4, 8]),
                            M6.rearrange("p j q c t -> p j q (c t)"), ALU.mult).then_inc(set_up, 1)
            for n in range(2):
                v.tensor_tensor_reduce(lamv[:, 2 * n, :], lamv[:, 2 * n, :], lamv[:, 2 * n + 1, :], 1.0, 0.0,
                                       ALU.mult, ALU.add, small[:, 8 + n:9 + n]).then_inc(lam_summed, 1)
            v.tensor_scalar(dgain, small[:, 4:5], 1.0 - LAM0, None, ALU.mult).then_inc(set_up, 1)
            dve.wait_ge(set_pe, 3)
            b6 = ps[:, 6, :].rearrange("p (k n) -> p k n", k=2)
            v.tensor_copy(ownb, b6[0:ROWS, :, 129:161]).then_inc(set_up, 1)
            for j in range(QUADS):
                rows = slice(32 * j, 32 * j + 32)
                v.tensor_copy(bias_s[rows, :, NPG - 1, :], b6[rows, :, 1 + 32 * j:33 + 32 * j]).then_inc(set_up, 1)
            own(v.tensor_copy(far, b6[:, :, 0]))
            v.tensor_copy(bias_s[:, :, 0:NPG - 1, :],
                          far.unsqueeze(2).unsqueeze(3).broadcast_to([P, 2, NPG - 1, 32])).then_inc(set_up, 1)
            dve.wait_ge(lam_exped, 1)
            own(v.tensor_tensor(small[:, 12:13], small[:, 11:12], small[:, 10:11], ALU.subtract))
            own(v.tensor_scalar(neglam, small[:, 12:13], -LAM0, None, ALU.add))
            own(v.scalar_tensor_tensor(out=rweight, in0=con[:, C_VEC + 1:C_VEC + 2], scalar=neglam,
                                       in1=con[:, C_VEC:C_VEC + 1], op0=ALU.mult, op1=ALU.add))

            def normalise(use):
                dve.wait_ge(summed, use + 1)
                v.tensor_scalar(rr[:, :], ps[:, 7, 0:TOK], 1.0 / D, EPS, ALU.mult, ALU.add).then_inc(meaned, 1)
                dve.wait_ge(rooted, use + 1)
                own(v.reciprocal(rr[:, :], rr[:, :]))
                for j in range(DT):
                    v.scalar_tensor_tensor(out=hT[:, j, :], in0=xT[:, j, :], scalar=gcol[:, j, use:use + 1],
                                           in1=rr[:, :], op0=ALU.mult, op1=ALU.mult).then_inc(normed, 1)

            dve.wait_ge(x_copied, DT)
            normalise(0)

            def s_turn_keys(b, kind, pages=range(NPG)):
                for g in pages:
                    dve.wait_ge(k_in[kind][g], b * 16 + 16)
                    v.transpose(kpage(g, kind), kpage(g, kind)).then_inc(k_turned[kind], 1)

            def lower_in(n, q):
                dve.wait_ge(p_high, 4 * n + q + 1)
                v.tensor_tensor(plo[:, q], slot8(n % 2)[:, :, q * P:q * P + P], phi[:, q].bitcast(F32), ALU.subtract
                                ).then_inc(p_split, 1)

            lower_in(0, 0)
            for n in range(1, 24):
                lower_in(n // 4, n % 4)
            v.tensor_copy(sel.rearrange("p v (j r) -> p v j r", j=QUADS),
                          ident.rearrange("p (v r) -> p v r", v=4).unsqueeze(2).broadcast_to([P, 4, QUADS, 32])
                          ).then_inc(sel_set, 1)
            dve.wait_ge(consts_set, 4)
            for kind in range(2):
                m0 = 12 * kind
                dve.wait_ge(in_taken, 4 + m0 + 4)
                v.tensor_scalar(qkvT[:, m0:m0 + 4, :], qkvT[:, m0:m0 + 4, :], SCALE, None, ALU.mult
                                ).then_inc(q_scaled, 1)
                dve.wait_ge(q_scaled, kind + 1)
                for hh in range(2):
                    rows = slice(64 * hh, 64 * hh + 64)
                    v.tensor_copy(Qbd[rows, 4 * kind:4 * kind + 4, :, 4 * hh:4 * hh + 4],
                                  qkvT[rows, 12 * kind:12 * kind + 4, SEQ:TOK].rearrange("p q (b t) -> p q b t", t=T)
                                  ).then_inc(q_laid, 1)
            for g in range(12):
                kind, tt = divmod(g, 3)
                cnt = TOKENS[tt][1]
                dve.wait_ge(nat_ready, g + 1)
                v.tensor_copy((knat if kind < 2 else vnat)[0:cnt, tt, kind % 2, :], ps[0:cnt, 4 + g % 2, :]
                              ).then_inc(nat_taken, 1)
            def p_bias(u):
                head = u if u < 8 else 8 + (u - 8) // 2
                dve.wait_ge(p_scores, u + 1)
                if u >= 4:
                    done = sum(c <= u - 4 for c in RESULT)
                    if done:
                        dve.wait_ge(p_turned, done)
                for n, cols in enumerate((slice(0, 256), slice(256, 384))):
                    v.tensor_tensor_reduce(pS[:, u % 4, cols], ps[:, 1 + u % 2, cols], pbias[:, head, cols], 1.0, LOWEST,
                                           ALU.add, ALU.max, pstat[:, u, n:n + 1]).then_inc(p_biased, 1)
                dve.wait_ge(p_biased, 2 * u + 2)
                v.tensor_scalar(pstat[:, u, 2:4], pstat[:, u, 0:2], -1.0, None, ALU.mult).then_inc(vec_p, 1)

            def p_norm(u):
                dve.wait_ge(p_exped, 2 * u + 2)
                own(v.reciprocal(pstat[:, u, 6:8], pstat[:, u, 4:6]))
                second = u >= 8 and u % 2 == 1
                if second:
                    own(v.tensor_scalar(pstat[:, u, 6:8], pstat[:, u, 6:8], neglam, None, ALU.mult))
                for n, cols in enumerate((slice(0, 256), slice(256, 384))):
                    x, r = pS[:, u % 4, cols], pstat[:, u, 6 + n:7 + n]
                    if second:
                        v.scalar_tensor_tensor(out=x, in0=x, scalar=r, in1=pS[:, (u - 1) % 4, cols],
                                               op0=ALU.mult, op1=ALU.add).then_inc(p_probs, 1)
                    elif u >= 8:
                        own(v.tensor_scalar(x, x, r, None, ALU.mult))
                    else:
                        v.tensor_scalar(x, x, r, None, ALU.mult).then_inc(p_probs, 1)

            def p_take(o):
                dve.wait_ge(p_mixed, 2 * o + 2 if o < 4 else o + 5)
                v.tensor_copy(oT[:, o, 0:SEQ], ps[:, 5 + o % 2, 0:SEQ]).then_inc(p_taken, 1)

            def s_queries(b):
                for kind in range(2):
                    for j in range(QUADS):
                        rows = slice(32 * j, 32 * j + 32)
                        v.tensor_copy(
                            Z[rows, kind, :].rearrange("p (h n) -> p h n", h=8)[:, :, 0:256].rearrange(
                                "p h (c n) -> p h c n", c=2)[:, :, :, 32 * j:32 * j + T],
                            qrep[rows, kind, bass.ds(b, 1)].rearrange("p o (h c) t -> p (o h) c t", c=2)
                            ).then_inc(z_ready, 1)

            def spread_queries():
                dve.wait_ge(q_spread, 1)
                for kind in range(2):
                    for n in range(4):
                        c = v.tensor_copy(
                            qrep[:, kind].rearrange("p b (q n) t -> p b q n t", n=4)[:, :, :, n, :],
                            ps[:, 6 + kind, n * P:n * P + P].rearrange("p (q b t) -> p b q t", q=4, t=T))
                    c.then_inc(q_copied, 1)

            def own_scores():
                dve.wait_ge(own_scored, 1)
                own(v.transpose(ownS[0:ROWS].rearrange("p b k n -> p (b k n)"), ps[0:NEW, 4, :]))
                own(v.tensor_tensor(ownS[0:ROWS], ownS[0:ROWS], ownb.unsqueeze(1).broadcast_to([ROWS, DB, 2, NEW]), ALU.add))
                own(v.tensor_tensor(ownS[0:ROWS], ownS[0:ROWS], con[0:ROWS, C_MASK:C_MASK + DB * NEW].rearrange(
                    "p (b n) -> p b n", b=DB).unsqueeze(2).broadcast_to([ROWS, DB, 2, NEW]), ALU.add))
                v.tensor_reduce(ownmax[0:ROWS].rearrange("p b k -> p (b k)"),
                                ownS[0:ROWS].rearrange("p b k n -> p (b k) n"), AX.X, ALU.max).then_inc(own_done, 1)

            dve.wait_ge(bias_in, 32)
            taken = 0
            for u in range(16 + 4):
                if u == 1:
                    spread_queries()
                if u == 2:
                    own_scores()
                if 1 <= u < 5:
                    s_turn_keys(0, 0, [2 * u - 2, 2 * u - 1])
                if 4 <= u < 8:
                    s_turn_keys(0, 1, [2 * u - 8, 2 * u - 7])
                if u == 4:
                    dve.wait_ge(z_cleared, 1)
                    s_queries(0)
                if u >= 12:
                    s_turn_keys(1, 0, [u - 12])
                if u >= 16:
                    s_turn_keys(1, 1, [2 * u - 32, 2 * u - 31])
                if u < 16:
                    p_bias(u)
                if 1 <= u < 17:
                    p_norm(u - 1)
                if u - 4 in RESULT:
                    r = RESULT.index(u - 4)
                    if r >= 8 or r % 2 == 1:
                        p_take(taken)
                        taken += 1

            def s_stats(b):
                raw = ps[:, 0, :].rearrange("p (k n) -> p k n", k=2)
                if not first(b):
                    dve.wait_ge(pt_ready, b)
                vec_own.add(v.tensor_tensor(S[:, :, 0:HALF], raw, bias_s.rearrange("p k g i -> p k (g i)"), ALU.add))
                vec_own.add(v.tensor_copy(S[:, :, HALF:LINE], ownS[:, bass.ds(b, 1)].rearrange("p o k n -> p (o k) n")))
                vec_own.add(v.tensor_reduce(blocksum, ps[:, 0, 0:HALF].rearrange("p (n i) -> p n i", n=NBLK),
                                            AX.X, ALU.add))
                vec_own.add(v.tensor_copy(smax[:, :, NBLK:NBLK + 1], ownmax[:, bass.ds(b, 1)].rearrange("p o (k n) -> p (o k) n", n=1)))
                vec_own.wait(dve)
                v.tensor_reduce(smax[:, :, 0:NBLK], S[:, :, 0:HALF].rearrange("p k (n i) -> p k n i", n=NBLK),
                                AX.X, ALU.max).then_inc(stats_ready, 1)

            def s_select(b):
                dve.wait_ge(stats_turned, b + 1)
                vec_own.add(v.tensor_copy(allsum, ps[:, 1, 0:NBLK]))
                own(v.tensor_reduce(mx, ps[0:10, 1, P:2 * P].rearrange("p (j r) -> p r j", j=QUADS), AX.X, ALU.max))
                v.tensor_copy(mxb, mx.unsqueeze(1).broadcast_to([10, QUADS, ROWS])).then_inc(max_ready, 1)
                own(v.tensor_reduce(low, allsum, AX.X, ALU.min))
                own(v.scalar_tensor_tensor(out=order, in0=allsum, scalar=low, in1=con[:, C_VEC + 3:C_VEC + 7],
                                           op0=ALU.is_equal, op1=ALU.mult))
                own(v.tensor_reduce(worst, order, AX.X, ALU.max))
                own(v.tensor_scalar(pen, order, worst, MASKED, ALU.is_equal, ALU.mult))
                s0 = S[:, 0, 0:HALF].rearrange("p (n i) -> p n i", n=NBLK)
                v.tensor_tensor(s0, s0, pen.unsqueeze(2).broadcast_to([P, NBLK, 64]), ALU.add).then_inc(m_ready, 1)

            def s_row_maxima(b):
                dve.wait_ge(max_turned, b + 1)
                vec_own.add(v.tensor_copy(fmax.rearrange("p k n -> p (k n)"), ps[:, 1, 256:266]))
                vec_own.wait(dve)
                own(v.tensor_tensor(fmax[:, 0, 0:NBLK], fmax[:, 0, 0:NBLK], pen, ALU.add))
                own(v.tensor_reduce(rowmax, fmax, AX.X, ALU.max))
                v.tensor_scalar(negmax, rowmax, -1.0, None, ALU.mult).then_inc(m_ready, 1)

            def s_probs(b, e):
                dve.wait_ge(s_exped, b * 2 + 2)
                if not early(b):
                    dve.wait_ge(v_used, b - 1)
                v.transpose(PT[:, e].rearrange("p k g r -> p (k g r)"), S.rearrange("p k n -> p (k n)")
                            ).then_inc(pt_ready, 1)

            def s_scale(b):
                dve.wait_ge(s_summed, b + 1)
                for kind in range(2):
                    rows = slice(ROWS * kind, ROWS * kind + ROWS)
                    vec_own.add(v.reciprocal(owt[rows, 0:1], ps[rows, 3, 400 + kind:401 + kind]))
                vec_own.wait(dve)
                own(v.tensor_tensor(owt[:, 1:2], owt[:, 0:1], rweight[0:2 * ROWS], ALU.mult))
                dve.wait_ge(v_used, b + 1)
                v.tensor_scalar(On, ps[0:2 * ROWS, 2, :], owt[:, 1:2], None, ALU.mult).then_inc(on_ready, 1)

            def s_take(b):
                dve.wait_ge(o_turned, b + 1)
                O = ps[:, 3, 0:288].rearrange("p (q n) -> p q n", q=4)
                dst = oT[:, :, bass.ds(b * T + SEQ, T)]
                for hh in range(2):
                    rows = slice(64 * hh, 64 * hh + 64)
                    v.tensor_copy(dst[rows, 0:4], O[rows, :, T * hh:T * hh + T]).then_inc(o_taken, 1)
                v.tensor_copy(dst[:, 4:8], O[:, :, 32:32 + T]).then_inc(o_taken, 1)
                dve.wait_ge(o_taken, b * 4 + 3)
                v.tensor_tensor(dst[:, 4:8], dst[:, 4:8], O[:, :, 32 + T:32 + 2 * T], ALU.add).then_inc(o_taken, 1)

            def s_step(b, e, more):
                if not (isinstance(b, int) and b <= 0):
                    s_take(b - 1)
                dve.wait_ge(scored, b + 2)
                s_stats(b + 1)
                if more:
                    s_queries(b + 2)
                turns = more and not (isinstance(b, int) and b < 0)
                if turns:
                    s_turn_keys(b + 2, 0)
                s_select(b + 1)
                if turns:
                    s_turn_keys(b + 2, 1)
                s_row_maxima(b + 1)
                s_probs(b + 1, 1 - e)
                if not (isinstance(b, int) and b < 0):
                    s_scale(b)

            s_step(-1, 1, True)
            s_step(0, 0, True)
            with dve.Fori(0, 2) as i:
                vec_own.enter(i, 0, 2 * 16)
                s_step(2 * i + 1, 1, True)
                s_step(2 * i + 2, 0, True)
            vec_own.leave(2)
            s_step(5, 1, True)
            s_step(6, 0, False)
            s_take(6)
            s_scale(7)
            s_take(7)

            def head_norm(n):
                own(v.reciprocal(drr[:, n, :], drr[:, n, :]))
                v.scalar_tensor_tensor(out=oT[:, 4 + n, :], in0=oT[:, 4 + n, :], scalar=dgain, in1=drr[:, n, :],
                                       op0=ALU.mult, op1=ALU.mult).then_inc(d_done, 1)

            dve.wait_ge(gated, 3)
            for m in range(DT):
                dve.wait_ge(tile_ready, T_OA + m + 1)
                v.tensor_tensor(mT[:, m, :], ps[:, m % 4, 0:TOK], gT[:, PLACE[m], :], ALU.mult).then_inc(mix_taken, 1)
                if m == 1:
                    dve.wait_ge(d_summed, 1)
                    v.tensor_scalar(drr[:, :, :], ps[:, 4:8, 0:TOK], 1.0 / P, EPS, ALU.mult, ALU.add).then_inc(d_meaned, 1)
                if 3 <= m < 7:
                    if m == 3:
                        dve.wait_ge(d_rooted, 1)
                    head_norm(m - 3)
            for m in range(DT):
                dve.wait_ge(tile_ready, T_OB + m + 1)
                own(v.tensor_tensor(ztmp[:, m % 2, :], ps[:, m % 4, 0:TOK], gT[:, PLACE[DT + m], :], ALU.mult))
                v.tensor_tensor(mT[:, m, :], mT[:, m, :], ztmp[:, m % 2, :], ALU.add).then_inc(mix_taken, 1)
            def lower_part(c, par, q):
                dve.wait_ge(w_high, c * 4 + q + 1)
                v.tensor_tensor(wlo[:, q], up_weights(par, q), whi[:, q].bitcast(F32), ALU.subtract).then_inc(w_split, 1)

            for m in range(DT):
                if m >= 4:
                    lower_part(0, 0, m - 4)
                dve.wait_ge(tile_ready, T_OUT + m + 1)
                v.tensor_tensor(xT[:, m, :], xT[:, m, :], ps[:, m % 4, 0:TOK], ALU.add).then_inc(mix_taken, 1)
            v.memset(ext[:, :, 0:2], 0.0).then_inc(edges_set, 1)
            dve.wait_ge(mix_taken, 24)
            normalise(1)
            def convolve(c, par):
                dve.wait_ge(f_turned, c + 1)
                v.tensor_copy(fcol[:, :, :], ps[:, 4, 0:80].rearrange("p (m n) -> p m n", n=20)).then_inc(f_copied, 1)
                dve.wait_ge(f_copied, c + 1)
                own(v.tensor_copy(
                    ext[:, 4 * par:4 * par + 4, 258:306].rearrange("p m (b r) -> p m b r", r=6)[:, :, :, 0:2],
                    fcol[:, :, 0:16].rearrange("p m (b r) -> p m b r", r=2)))
                for q in range(4):
                    dve.wait_ge(ext_ready, c * 8 + 2 * q + 2)
                    vec_own.add(v.tensor_scalar(cv[:, q, 0:CONV], ext[:, 4 * par + q, 0:CONV], fcol[:, q, 16:17],
                                                fcol[:, q, 19:20], ALU.mult, ALU.add))
                    if not (isinstance(c, int) and c == 10):
                        lower_part(c + 1, 1 - par, q)
                if not early(c):
                    dve.wait_ge(c_turned, c - 1)
                v.tensor_copy(ends[:, par].rearrange("p q (s r) -> p q s r", r=2),
                              ext[:, 4 * par:4 * par + 4, 256:310].rearrange("p q (s r) -> p q s r", r=6)[:, :, :, 0:2]
                              ).then_inc(ends_packed, 1)
                vec_own.wait(dve)
                for q in range(4):
                    vec_own.add(v.scalar_tensor_tensor(out=cv[:, q, 0:CONV], in0=ext[:, 4 * par + q, 1:1 + CONV],
                                                       scalar=fcol[:, q, 17:18], in1=cv[:, q, 0:CONV],
                                                       op0=ALU.mult, op1=ALU.add))
                vec_own.wait(dve)
                for q in range(4):
                    v.scalar_tensor_tensor(out=cv[:, q, 0:CONV], in0=ext[:, 4 * par + q, 2:2 + CONV],
                                           scalar=fcol[:, q, 18:19], in1=cv[:, q, 0:CONV],
                                           op0=ALU.mult, op1=ALU.add).then_inc(conv_done, 1)
                dve.wait_ge(conv_done, c * 4 + 4)
                dve.wait_ge(silu_done, c + 1)
                v.tensor_tensor(ffT[:, bass.ds(c * 2, 2), 0:SEQ], cv[:, 0:2, 0:SEQ], cv[:, 2:4, 0:SEQ], ALU.mult
                                ).then_inc(ff_done, 1)
                new = cv[:, :, 258:306].rearrange("p m (b r) -> p m b r", r=6)[:, :, :, 0:T]
                v.tensor_tensor(ffT[:, bass.ds(c * 2, 2), SEQ:TOK].rearrange("p m (b t) -> p m b t", t=T),
                                new[:, 0:2], new[:, 2:4], ALU.mult).then_inc(ff_done, 1)

            def stage_state(c, par):
                dve.wait_ge(c_turned, c + 1)
                if not early(c):
                    dve.wait_ge(cst_out[par], so_far(c, par, 64) - 64)
                v.tensor_copy(cst[0:18, par, :], ps[0:18, 5 + par, :]).then_inc(c_staged, 1)

            convolve(0, 0)
            convolve(1, 1)
            stage_state(0, 0)
            convolve(2, 0)
            stage_state(1, 1)
            with dve.Fori(1, 4) as i:
                vec_own.enter(i, 1, 18)
                convolve(2 * i + 1, 1)
                stage_state(2 * i, 0)
                convolve(2 * i + 2, 0)
                stage_state(2 * i + 1, 1)
            vec_own.leave(3)
            convolve(9, 1)
            stage_state(8, 0)
            convolve(10, 0)
            stage_state(9, 1)
            stage_state(10, 0)
            dve.sem_inc(down_taken, 4)
            for m in range(DT):
                dve.wait_ge(tile_ready, T_DOWN + m + 1)
                v.tensor_tensor(xT[:, m, :], xT[:, m, :], ps[:, m % 4, 0:TOK], ALU.add).then_inc(down_taken, 1)
            dve.wait_ge(down_taken, 4 + DT)
            normalise(2)
            for n, (t0, cnt) in enumerate(TOKENS):
                dve.wait_ge(y_turned, 2 * n + 2)
                v.tensor_copy(ynat[0:cnt, n, 512:1024], ps[0:cnt, (2 * n + 1) % 4, :]).then_inc(y_copied_v, 1)


_INS = ["x_prompt", "x_sample", "cache_moba_k", "cache_moba_v", "cache_diff_k", "cache_diff_v", "state_conv",
        "page_table", "rel_bias", "norm_attn", "w_in", "w_gate", "w_out_a", "w_out_b", "w_out",
        "lambda_q1", "lambda_k1", "lambda_q2", "lambda_k2", "diff_norm", "norm_ffn", "w_up", "conv_w", "conv_b",
        "w_down", "norm_final"]
_OUTS = [("y_prompt", (1, SEQ, D)), ("y_sample", (DB, T, D)),
         ("moba_k_prompt", (1, 1, SEQ, 8, HD)), ("moba_v_prompt", (1, 1, SEQ, 8, HD)),
         ("diff_k_prompt", (1, 1, SEQ, 4, 2 * HD)), ("diff_v_prompt", (1, 1, SEQ, 4, 2 * HD)),
         ("conv_prompt", (1, 1, 2, 2 * FF)),
         ("moba_k_sample", (1, DB, T, 8, HD)), ("moba_v_sample", (1, DB, T, 8, HD)),
         ("diff_k_sample", (1, DB, T, 4, 2 * HD)), ("diff_v_sample", (1, DB, T, 4, 2 * HD)),
         ("conv_sample", (1, DB, 2, 2 * FF))]


def kernel(**inputs):
    import concourse.bacc as _bacc
    from concourse.bass_utils import run_bass_kernel_spmd as _run

    nc = _bacc.Bacc("TRN2", target_bir_lowering=False, num_devices=1)
    arrays, ins, outs = {}, {}, {}
    given = {name: np.ascontiguousarray(inputs[name]) for name in _INS}
    given["constants"] = constants()
    for name, x in given.items():
        arrays[f"in_{name}"] = x
        ins[name] = nc.dram_tensor(f"in_{name}", x.shape, mybir.dt.from_np(x.dtype), kind="ExternalInput").ap()
    for name, shape in _OUTS:
        outs[name] = nc.dram_tensor(f"out_{name}", shape, F32, kind="ExternalOutput").ap()
    build(nc, ins, outs)
    r = _run(nc, [arrays], core_ids=[0])
    return tuple(r.results[0][f"out_{name}"] for name, _ in _OUTS)
```
